# Optimizing a Trainium2 kernel written in Bass

```python
import math
import jax, jax.numpy as jnp
from jax import lax
import numpy as np

D_MODEL = 1024
BATCH = 1
SEQ = 512
DEPTH = 1

N_MIXERS = 3
HEAD_DIM = 64
MIX_WIDTH = 768
N_MEM_HEADS = 4
MEM_WIDTH = N_MEM_HEADS * HEAD_DIM
N_MEM = 256
BRANCH = MIX_WIDTH + MEM_WIDTH
IN_WIDTH = 3 * MIX_WIDTH + MEM_WIDTH + BRANCH
RMS_EPS = 1e-6
SUBLN_EPS = 1e-5
NEG_INF = -1e30

DSW_GROUPS = ((128, 1), (512, 4), (2048, 16))
DSW_HEADS_PER_GROUP = 4
DSW_HEADS = DSW_HEADS_PER_GROUP * len(DSW_GROUPS)
DSW_GROUP_WIDTH = DSW_HEADS_PER_GROUP * HEAD_DIM
BAND_BLOCK = 128

MOBA_HEADS = MIX_WIDTH // HEAD_DIM
MOBA_BLOCK = 256
MOBA_TOPK = 3
MOBA_Q_CHUNK = 64

DIFF_HEADS = 6
DIFF_D = 64
DIFF_Q_BLOCK = 128
N_DIFF_LAYERS = len(range(2, DEPTH, N_MIXERS))


def alibi_slopes(n):
    return jnp.asarray(2.0 ** (-8.0 * np.arange(1, n + 1) / n), dtype=jnp.float32)

def rmsnorm(x, g, eps=RMS_EPS):
    xf = x.astype(jnp.float32)
    y = xf * lax.rsqrt(jnp.mean(xf * xf, axis=-1, keepdims=True) + eps)
    return (y * g.astype(jnp.float32)).astype(x.dtype)

def split_heads(t, n):
    b, s, _ = t.shape
    return t.reshape(b, s, n, -1).transpose(0, 2, 1, 3)

def merge_heads(t):
    b, h, s, d = t.shape
    return t.transpose(0, 2, 1, 3).reshape(b, s, h * d)

def banded_causal_attention(q, k, v, span, slopes):
    b, h, L, hd = q.shape
    nb = -(-L // BAND_BLOCK)
    Lp = nb * BAND_BLOCK
    pad = ((0, 0), (0, 0), (0, Lp - L), (0, 0))
    qb = jnp.pad(q, pad).reshape(b, h, nb, BAND_BLOCK, hd)
    kb = jnp.pad(k, pad).reshape(b, h, nb, BAND_BLOCK, hd)
    vb = jnp.pad(v, pad).reshape(b, h, nb, BAND_BLOCK, hd)
    shift = ((0, 0), (0, 0), (1, 0), (0, 0), (0, 0))
    kk = jnp.concatenate([jnp.pad(kb, shift)[:, :, :-1], kb], axis=3)
    vv = jnp.concatenate([jnp.pad(vb, shift)[:, :, :-1], vb], axis=3)
    dist = (jnp.arange(BAND_BLOCK)[:, None] + BAND_BLOCK) - jnp.arange(2 * BAND_BLOCK)[None, :]
    kpos = jnp.arange(nb)[:, None] * BAND_BLOCK - BAND_BLOCK + jnp.arange(2 * BAND_BLOCK)[None, :]
    valid = ((dist >= 0) & (dist <= span))[None, :, :] & (kpos >= 0)[:, None, :]
    s = jnp.einsum('bhnqd,bhnkd->bhnqk', qb, kk).astype(jnp.float32) * (hd ** -0.5)
    s = s - slopes[None, :, None, None, None] * dist.astype(jnp.float32)
    s = jnp.where(valid, s, NEG_INF)
    lse = jax.nn.logsumexp(s, axis=-1)
    p = jnp.exp(s - lse[..., None])
    out = jnp.einsum('bhnqk,bhnkd->bhnqd', p, vv.astype(jnp.float32))
    return out.reshape(b, h, Lp, hd)[:, :, :L], lse.reshape(b, h, Lp)[:, :, :L]

def dilated_window_mixer(q, k, v):
    b, S, _ = q.shape
    hg = DSW_HEADS_PER_GROUP
    slopes_all = alibi_slopes(DSW_HEADS)
    outs, lses = [], []
    for g, (window, dil) in enumerate(DSW_GROUPS):
        cols = slice(g * DSW_GROUP_WIDTH, (g + 1) * DSW_GROUP_WIDTH)
        U = S // dil

        def to_residue(t):
            t = t.reshape(b, U, dil, hg, HEAD_DIM).transpose(0, 3, 2, 1, 4)
            return t.reshape(b, hg * dil, U, HEAD_DIM)

        slopes = jnp.repeat(slopes_all[g * hg:(g + 1) * hg] * dil, dil)
        o, lse = banded_causal_attention(to_residue(q[..., cols]), to_residue(k[..., cols]),
                                         to_residue(v[..., cols]), window // dil, slopes)
        o = o.reshape(b, hg, dil, U, HEAD_DIM).transpose(0, 3, 2, 1, 4).reshape(b, S, hg, HEAD_DIM)
        lse = lse.reshape(b, hg, dil, U).transpose(0, 3, 2, 1).reshape(b, S, hg)
        outs.append(o)
        lses.append(lse)
    alpha = jax.nn.softmax(jnp.stack(lses, axis=0), axis=0)
    mixed = [(outs[g] * alpha[g][..., None]).reshape(b, S, DSW_GROUP_WIDTH) for g in range(len(DSW_GROUPS))]
    return jnp.concatenate(mixed, axis=-1).astype(q.dtype)

def moba_mixer(q, k, v):
    b, S, _ = q.shape
    H = MOBA_HEADS
    slopes = alibi_slopes(H)
    nblk = -(-S // MOBA_BLOCK)
    Sp = nblk * MOBA_BLOCK
    n_gate = max(nblk, MOBA_TOPK)
    pad = ((0, 0), (0, 0), (0, Sp - S), (0, 0))
    qh = jnp.pad(split_heads(q, H), pad)
    kb = jnp.pad(split_heads(k, H), pad).reshape(b, H, nblk, MOBA_BLOCK, HEAD_DIM)
    vb = jnp.pad(split_heads(v, H), pad).reshape(b, H, nblk, MOBA_BLOCK, HEAD_DIM)
    kmean = jnp.mean(kb.astype(jnp.float32), axis=3)
    nchunk = Sp // MOBA_Q_CHUNK
    qc = qh.reshape(b, H, nchunk, MOBA_Q_CHUNK, HEAD_DIM).transpose(2, 0, 1, 3, 4)
    bi = jnp.arange(b)[:, None, None, None]
    hi = jnp.arange(H)[None, :, None, None]
    scale = HEAD_DIM ** -0.5

    def one_chunk(args):
        c, qx = args
        t = c * MOBA_Q_CHUNK + jnp.arange(MOBA_Q_CHUNK)
        n = (c * MOBA_Q_CHUNK) // MOBA_BLOCK
        gate = jnp.einsum('bhqd,bhnd->bhqn', qx.astype(jnp.float32), kmean)
        gate = jnp.pad(gate, ((0, 0), (0, 0), (0, 0), (0, n_gate - nblk)), constant_values=NEG_INF)
        gate = jnp.where(jnp.arange(n_gate) < n, gate, NEG_INF)
        _, idx = lax.top_k(gate, MOBA_TOPK)
        idx = jnp.minimum(idx, nblk - 1)
        sel_ok = jnp.arange(MOBA_TOPK) < n
        ks = kb[bi, hi, idx]
        vs = vb[bi, hi, idx]
        kpos_sel = idx[..., None] * MOBA_BLOCK + jnp.arange(MOBA_BLOCK)
        dist_sel = (t[None, None, :, None, None] - kpos_sel).astype(jnp.float32)
        s_sel = jnp.einsum('bhqd,bhqjkd->bhqjk', qx, ks).astype(jnp.float32) * scale
        s_sel = s_sel - slopes[None, :, None, None, None] * dist_sel
        s_sel = jnp.where(sel_ok[:, None], s_sel, NEG_INF)
        k_own = lax.dynamic_index_in_dim(kb, n, axis=2, keepdims=False)
        v_own = lax.dynamic_index_in_dim(vb, n, axis=2, keepdims=False)
        dist_own = t[:, None] - (n * MOBA_BLOCK + jnp.arange(MOBA_BLOCK))[None, :]
        s_own = jnp.einsum('bhqd,bhkd->bhqk', qx, k_own).astype(jnp.float32) * scale
        s_own = jnp.where(dist_own >= 0,
                          s_own - slopes[None, :, None, None] * dist_own.astype(jnp.float32), NEG_INF)
        s_all = jnp.concatenate([s_sel.reshape(b, H, MOBA_Q_CHUNK, MOBA_TOPK * MOBA_BLOCK), s_own], axis=-1)
        p = jax.nn.softmax(s_all, axis=-1)
        p_sel = p[..., :MOBA_TOPK * MOBA_BLOCK].reshape(b, H, MOBA_Q_CHUNK, MOBA_TOPK, MOBA_BLOCK)
        p_own = p[..., MOBA_TOPK * MOBA_BLOCK:]
        return (jnp.einsum('bhqjk,bhqjkd->bhqd', p_sel, vs.astype(jnp.float32))
                + jnp.einsum('bhqk,bhkd->bhqd', p_own, v_own.astype(jnp.float32)))

    o = lax.map(one_chunk, (jnp.arange(nchunk), qc))
    o = o.transpose(1, 2, 0, 3, 4).reshape(b, H, Sp, HEAD_DIM)[:, :, :S]
    return merge_heads(o).astype(q.dtype)

def diff_mixer(q, k, v, lq1, lk1, lq2, lk2, subln_g, lambda_init):
    b, S, _ = q.shape
    H = DIFF_HEADS
    slopes = alibi_slopes(H)
    qh = q.reshape(b, S, H, 2, DIFF_D).transpose(0, 2, 3, 1, 4)
    kh = k.reshape(b, S, H, 2, DIFF_D).transpose(0, 2, 3, 1, 4)
    vh = split_heads(v, H).astype(jnp.float32)
    lam = (jnp.exp(jnp.sum(lq1.astype(jnp.float32) * lk1.astype(jnp.float32)))
           - jnp.exp(jnp.sum(lq2.astype(jnp.float32) * lk2.astype(jnp.float32))) + lambda_init)
    nqb = S // DIFF_Q_BLOCK
    qblocks = qh.reshape(b, H, 2, nqb, DIFF_Q_BLOCK, DIFF_D).transpose(3, 0, 1, 2, 4, 5)
    kpos = jnp.arange(S)

    def one_block(args):
        j, qx = args
        t = j * DIFF_Q_BLOCK + jnp.arange(DIFF_Q_BLOCK)
        dist = t[:, None] - kpos[None, :]
        s = jnp.einsum('bhmqd,bhmkd->bhmqk', qx, kh).astype(jnp.float32) * (DIFF_D ** -0.5)
        s = jnp.where(dist >= 0, s - slopes[None, :, None, None, None] * dist.astype(jnp.float32), NEG_INF)
        p = jax.nn.softmax(s, axis=-1)
        w = p[:, :, 0] - lam * p[:, :, 1]
        return jnp.einsum('bhqk,bhkd->bhqd', w, vh)

    o = lax.map(one_block, (jnp.arange(nqb), qblocks))
    o = o.transpose(1, 2, 0, 3, 4).reshape(b, H, S, 2 * DIFF_D)
    o = rmsnorm(o, subln_g, SUBLN_EPS) * (1.0 - lambda_init)
    return merge_heads(o).astype(q.dtype)

def memory_attention(qm, mem_n, w_mem_kv):
    kv = mem_n @ w_mem_kv
    km = split_heads(kv[..., :MEM_WIDTH], N_MEM_HEADS)
    vm = split_heads(kv[..., MEM_WIDTH:], N_MEM_HEADS)
    qh = split_heads(qm, N_MEM_HEADS)
    s = jnp.einsum('bhqd,bhkd->bhqk', qh, km).astype(jnp.float32) * (HEAD_DIM ** -0.5)
    p = jax.nn.softmax(s, axis=-1)
    return merge_heads(jnp.einsum('bhqk,bhkd->bhqd', p, vm.astype(jnp.float32))).astype(qm.dtype)

def first_inputs(seed: int = 0) -> dict:
    key = jax.random.key(seed)
    ks = jax.random.split(key, 14)
    f32 = jnp.float32
    nd = max(N_DIFF_LAYERS, 0)
    return {
        "x": jax.random.normal(ks[0], (BATCH, SEQ, D_MODEL), f32),
        "mem": jax.random.normal(ks[1], (BATCH, N_MEM, D_MODEL), f32),
        "norm_g": 1.0 + 0.02 * jax.random.normal(ks[2], (DEPTH, D_MODEL), f32),
        "w_in": jax.random.normal(ks[3], (DEPTH, D_MODEL, IN_WIDTH), f32) * D_MODEL ** -0.5,
        "w_out": jax.random.normal(ks[4], (DEPTH, BRANCH, D_MODEL), f32) * BRANCH ** -0.5,
        "mem_norm_g": 1.0 + 0.02 * jax.random.normal(ks[5], (DEPTH, D_MODEL), f32),
        "w_mem_kv": jax.random.normal(ks[6], (DEPTH, D_MODEL, 2 * MEM_WIDTH), f32) * D_MODEL ** -0.5,
        "diff_lambda_q1": 0.1 * jax.random.normal(ks[7], (nd, DIFF_D), f32),
        "diff_lambda_k1": 0.1 * jax.random.normal(ks[8], (nd, DIFF_D), f32),
        "diff_lambda_q2": 0.1 * jax.random.normal(ks[9], (nd, DIFF_D), f32),
        "diff_lambda_k2": 0.1 * jax.random.normal(ks[10], (nd, DIFF_D), f32),
        "diff_subln_g": 1.0 + 0.02 * jax.random.normal(ks[11], (nd, 2 * DIFF_D), f32),
        "final_norm_g": 1.0 + 0.02 * jax.random.normal(ks[12], (D_MODEL,), f32),
    }

def first_block(x, mem, norm_g, w_in, w_out, mem_norm_g, w_mem_kv, diff_lambda_q1, diff_lambda_k1,
              diff_lambda_q2, diff_lambda_k2, diff_subln_g, final_norm_g):
    c1, c2, c3, c4 = MIX_WIDTH, 2 * MIX_WIDTH, 3 * MIX_WIDTH, 3 * MIX_WIDTH + MEM_WIDTH
    for i in range(DEPTH):
        h = rmsnorm(x, norm_g[i])
        proj = h @ w_in[i]
        q, k, v = proj[..., :c1], proj[..., c1:c2], proj[..., c2:c3]
        qm, gate = proj[..., c3:c4], proj[..., c4:]
        kind = i % N_MIXERS
        if kind == 0:
            mix = dilated_window_mixer(q, k, v)
        elif kind == 1:
            mix = moba_mixer(q, k, v)
        else:
            c = i // N_MIXERS
            lambda_init = 0.8 - 0.6 * math.exp(-0.3 * i)
            mix = diff_mixer(q, k, v, diff_lambda_q1[c], diff_lambda_k1[c], diff_lambda_q2[c],
                             diff_lambda_k2[c], diff_subln_g[c], lambda_init)
        mo = memory_attention(qm, rmsnorm(mem, mem_norm_g[i]), w_mem_kv[i])
        y = jnp.concatenate([mix, mo], axis=-1) * jax.nn.silu(gate)
        x = x + y @ w_out[i]
    return rmsnorm(x, final_norm_g)


DEPTH_2 = 2

N_EVEN = (DEPTH_2 + 1) // 2
N_ODD = DEPTH_2 // 2
D_PLE = 256
EPS = 1e-6

CONV_GROUPS = 8
CONV_GROUP_DIM = 64
CONV_DIM = CONV_GROUPS * CONV_GROUP_DIM
CONV_WIDTH = 3
GMLP_HEADS = 8
GMLP_HEAD_DIM = 64
GMLP_DIM = GMLP_HEADS * GMLP_HEAD_DIM
GMLP_CHUNK = 128
EVEN_IN = 3 * CONV_DIM + 2 * GMLP_DIM
EVEN_MIX = CONV_DIM + GMLP_DIM

MLA_HEADS = 8
MLA_NOPE = 64
MLA_ROPE = 32
MLA_V = 64
MLA_QK = MLA_NOPE + MLA_ROPE
Q_LORA = 384
KV_LORA = 256
ROPE_THETA = 10000.0
ATTN_BLOCK = 128
MLSTM_HEADS = 4
MLSTM_QK = 64
MLSTM_V = 128
MLSTM_CHUNK = 64
ODD_IN = Q_LORA + KV_LORA + MLA_ROPE + 2 * MLSTM_HEADS * MLSTM_QK + 2 * MLSTM_HEADS * MLSTM_V + 2 * MLSTM_HEADS
ODD_MIX = MLA_HEADS * MLA_V + MLSTM_HEADS * MLSTM_V

D_FF = -(-8 * D_MODEL // (3 * 256)) * 256


def rmsnorm_2(x, g):
    xf = x.astype(jnp.float32)
    y = xf * lax.rsqrt(jnp.mean(xf * xf, axis=-1, keepdims=True) + EPS)
    return (y * g.astype(jnp.float32)).astype(x.dtype)

def swiglu(h, w_gate, w_up, w_down):
    return (jax.nn.silu(h @ w_gate) * (h @ w_up)) @ w_down

def short_gated_conv(b_gate, c_gate, x_in, w_conv):
    z = c_gate * x_in
    conv = lax.conv_general_dilated(
        z, w_conv[:, None, :].astype(z.dtype), window_strides=(1,),
        padding=[(CONV_WIDTH - 1, 0)], dimension_numbers=('NWC', 'WIO', 'NWC'),
        feature_group_count=CONV_DIM)
    return b_gate * conv

def chunked_spatial_gating(u, v, g_v, w_s, b_s):
    bsz, seq, _ = u.shape
    n_chunks = seq // GMLP_CHUNK
    shape5 = (bsz, n_chunks, GMLP_CHUNK, GMLP_HEADS, GMLP_HEAD_DIM)
    u = jax.nn.gelu(u).reshape(shape5)
    v = rmsnorm_2(jax.nn.gelu(v).reshape(shape5), g_v)
    causal = jnp.tril(jnp.ones((GMLP_CHUNK, GMLP_CHUNK), dtype=w_s.dtype))
    mixed = jnp.einsum('hts,bnshd->bnthd', w_s * causal, v) + b_s.T[:, :, None]
    return (u * mixed).reshape(bsz, seq, GMLP_DIM)

def rope_tables(positions, dim, dtype):
    inv_freq = ROPE_THETA ** (-jnp.arange(0, dim, 2, dtype=jnp.float32) / dim)
    ang = positions.astype(jnp.float32)[..., None] * inv_freq
    return jnp.cos(ang)[:, :, None, :].astype(dtype), jnp.sin(ang)[:, :, None, :].astype(dtype)

def apply_rope(x, cos, sin):
    half = x.shape[-1] // 2
    x1, x2 = x[..., :half], x[..., half:]
    return jnp.concatenate([x1 * cos - x2 * sin, x2 * cos + x1 * sin], axis=-1)

def causal_block_attention(q, k, v):
    bsz, seq, heads, dk = q.shape
    n_blocks = seq // ATTN_BLOCK
    q_blocks = q.reshape(bsz, n_blocks, ATTN_BLOCK, heads, dk).transpose(1, 0, 2, 3, 4)
    k_idx = jnp.arange(seq)
    scale = dk ** -0.5

    def one_block(args):
        qi, bi = args
        s = jnp.einsum('bqhd,bkhd->bhqk', qi, k).astype(jnp.float32) * scale
        q_idx = bi * ATTN_BLOCK + jnp.arange(ATTN_BLOCK)
        s = jnp.where(k_idx[None, :] <= q_idx[:, None], s, -jnp.inf)
        pr = jax.nn.softmax(s, axis=-1).astype(v.dtype)
        return jnp.einsum('bhqk,bkhv->bqhv', pr, v)

    out = lax.map(one_block, (q_blocks, jnp.arange(n_blocks)))
    return out.transpose(1, 0, 2, 3, 4).reshape(bsz, seq, heads, v.shape[-1])

def latent_attention(q_lat, kv_lat, k_pe, positions, g_qa, g_kva, w_q_up, w_kv_up, g_q, g_k):
    bsz, seq, _ = q_lat.shape
    q = (rmsnorm_2(q_lat, g_qa) @ w_q_up).reshape(bsz, seq, MLA_HEADS, MLA_QK)
    kv = (rmsnorm_2(kv_lat, g_kva) @ w_kv_up).reshape(bsz, seq, MLA_HEADS, MLA_NOPE + MLA_V)
    k_nope, v = kv[..., :MLA_NOPE], kv[..., MLA_NOPE:]
    cos, sin = rope_tables(positions, MLA_ROPE, q.dtype)
    q_nope = rmsnorm_2(q[..., :MLA_NOPE], g_q[:MLA_NOPE])
    q_pe = apply_rope(rmsnorm_2(q[..., MLA_NOPE:], g_q[MLA_NOPE:]), cos, sin)
    k_nope = rmsnorm_2(k_nope, g_k[:MLA_NOPE])
    k_pe = apply_rope(rmsnorm_2(k_pe[:, :, None, :], g_k[MLA_NOPE:]), cos, sin)
    q = jnp.concatenate([q_nope, q_pe], axis=-1)
    k = jnp.concatenate([k_nope, jnp.broadcast_to(k_pe, (bsz, seq, MLA_HEADS, MLA_ROPE))], axis=-1)
    return causal_block_attention(q, k, v).reshape(bsz, seq, MLA_HEADS * MLA_V)

def mlstm_chunkwise(q, k, v, i_pre, f_pre):
    out_dtype = v.dtype
    bsz, seq, heads, dk = q.shape
    dv = v.shape[-1]
    L = MLSTM_CHUNK
    nc = seq // L
    f32 = jnp.float32

    def to_chunks(a):
        return a.astype(f32).reshape(bsz, nc, L, heads, -1).transpose(1, 0, 3, 2, 4)

    def gate_chunks(a):
        return a.astype(f32).reshape(bsz, nc, L, heads).transpose(1, 0, 3, 2)

    qc = to_chunks(q) * (dk ** -0.5)
    kc, vc = to_chunks(k), to_chunks(v)
    ic = gate_chunks(i_pre)
    ac = jnp.cumsum(jax.nn.log_sigmoid(gate_chunks(f_pre)), axis=-1)
    causal = jnp.tril(jnp.ones((L, L), dtype=bool))

    def step(carry, xs):
        c_mat, n_vec, m = carry
        qb, kb, vb, ib, ab = xs
        d = jnp.where(causal, ab[..., :, None] - ab[..., None, :] + ib[..., None, :], -jnp.inf)
        inter = ab + m[..., None]
        m_t = jnp.maximum(inter, jnp.max(d, axis=-1))
        w_intra = jnp.exp(d - m_t[..., None])
        w_inter = jnp.exp(inter - m_t)
        s = jnp.einsum('bhtd,bhsd->bhts', qb, kb) * w_intra
        num = jnp.einsum('bhts,bhsv->bhtv', s, vb) + w_inter[..., None] * jnp.einsum('bhtd,bhvd->bhtv', qb, c_mat)
        den = jnp.sum(s, axis=-1) + w_inter * jnp.einsum('bhtd,bhd->bht', qb, n_vec)
        h = num / jnp.maximum(jnp.abs(den), jnp.exp(-m_t))[..., None]
        a_last = ab[..., -1]
        m_new = m_t[..., -1]
        w_s = jnp.exp(a_last[..., None] - ab + ib - m_new[..., None])
        decay = jnp.exp(a_last + m - m_new)
        c_new = decay[..., None, None] * c_mat + jnp.einsum('bhs,bhsv,bhsd->bhvd', w_s, vb, kb)
        n_new = decay[..., None] * n_vec + jnp.einsum('bhs,bhsd->bhd', w_s, kb)
        return (c_new, n_new, m_new), h

    init = (jnp.zeros((bsz, heads, dv, dk), f32), jnp.zeros((bsz, heads, dk), f32), jnp.zeros((bsz, heads), f32))
    _, hs = lax.scan(step, init, (qc, kc, vc, ic, ac))
    return hs.transpose(1, 0, 3, 2, 4).reshape(bsz, seq, heads, dv).astype(out_dtype)

def even_mixer(hn, w_in, w_conv, g_v, w_s, b_s, w_out):
    z = hn @ w_in
    b_gate, c_gate, x_in, u, v = jnp.split(z, [CONV_DIM, 2 * CONV_DIM, 3 * CONV_DIM, 3 * CONV_DIM + GMLP_DIM], axis=-1)
    y_a = short_gated_conv(b_gate, c_gate, x_in, w_conv)
    y_b = chunked_spatial_gating(u, v, g_v, w_s, b_s)
    return jnp.concatenate([y_a, y_b], axis=-1) @ w_out

def odd_mixer(hn, positions, w_in, b_gate, g_qa, g_kva, w_q_up, w_kv_up, g_q, g_k, g_mh, w_out):
    bsz, seq, _ = hn.shape
    z = hn @ w_in
    sizes = [Q_LORA, KV_LORA, MLA_ROPE, MLSTM_HEADS * MLSTM_QK, MLSTM_HEADS * MLSTM_QK,
             MLSTM_HEADS * MLSTM_V, MLSTM_HEADS * MLSTM_V, MLSTM_HEADS, MLSTM_HEADS]
    q_lat, kv_lat, k_pe, mq, mk, mv, mo, mi, mf = jnp.split(z, np.cumsum(sizes)[:-1].tolist(), axis=-1)
    y_c = latent_attention(q_lat, kv_lat, k_pe, positions, g_qa, g_kva, w_q_up, w_kv_up, g_q, g_k)
    h_m = mlstm_chunkwise(mq.reshape(bsz, seq, MLSTM_HEADS, MLSTM_QK),
                          mk.reshape(bsz, seq, MLSTM_HEADS, MLSTM_QK),
                          mv.reshape(bsz, seq, MLSTM_HEADS, MLSTM_V),
                          mi + b_gate[:MLSTM_HEADS], mf + b_gate[MLSTM_HEADS:])
    y_d = jax.nn.sigmoid(mo) * rmsnorm_2(h_m, g_mh).reshape(bsz, seq, MLSTM_HEADS * MLSTM_V)
    return jnp.concatenate([y_c, y_d], axis=-1) @ w_out

def second_inputs(seed: int = 0) -> dict:
    key = jax.random.key(seed)
    ks = list(jax.random.split(key, 40))
    f32 = jnp.float32

    def normal(shape):
        return jax.random.normal(ks.pop(), shape, f32)

    def dense(shape, fan_in):
        return normal(shape) * fan_in ** -0.5

    def gain(shape):
        return 1.0 + 0.05 * normal(shape)

    x = normal((BATCH, SEQ, D_MODEL))
    p = normal((DEPTH_2, BATCH, SEQ, D_PLE))
    positions = jnp.arange(SEQ, dtype=jnp.int32)[None, :] + jax.random.randint(ks.pop(), (BATCH, 1), 0, SEQ, dtype=jnp.int32)
    od_b_gate = jnp.concatenate([0.1 * normal((N_ODD, MLSTM_HEADS)), 3.0 + 0.1 * normal((N_ODD, MLSTM_HEADS))], axis=-1)
    return {
        'x': x,
        'p': p,
        'positions': positions,
        'g_mix': gain((DEPTH_2, D_MODEL)),
        'g_ffn': gain((DEPTH_2, D_MODEL)),
        'g_ple': gain((DEPTH_2, D_MODEL)),
        'ev_w_in': dense((N_EVEN, D_MODEL, EVEN_IN), D_MODEL),
        'ev_w_conv': dense((N_EVEN, CONV_WIDTH, CONV_DIM), CONV_WIDTH),
        'ev_g_v': gain((N_EVEN, GMLP_HEADS, GMLP_HEAD_DIM)),
        'ev_w_s': dense((N_EVEN, GMLP_HEADS, GMLP_CHUNK, GMLP_CHUNK), GMLP_CHUNK),
        'ev_b_s': 1.0 + 0.1 * normal((N_EVEN, GMLP_HEADS, GMLP_CHUNK)),
        'ev_w_out': dense((N_EVEN, EVEN_MIX, D_MODEL), EVEN_MIX),
        'od_w_in': dense((N_ODD, D_MODEL, ODD_IN), D_MODEL),
        'od_b_gate': od_b_gate,
        'od_g_qa': gain((N_ODD, Q_LORA)),
        'od_g_kva': gain((N_ODD, KV_LORA)),
        'od_w_q_up': dense((N_ODD, Q_LORA, MLA_HEADS * MLA_QK), Q_LORA),
        'od_w_kv_up': dense((N_ODD, KV_LORA, MLA_HEADS * (MLA_NOPE + MLA_V)), KV_LORA),
        'od_g_q': gain((N_ODD, MLA_QK)),
        'od_g_k': gain((N_ODD, MLA_QK)),
        'od_g_mh': gain((N_ODD, MLSTM_HEADS, MLSTM_V)),
        'od_w_out': dense((N_ODD, ODD_MIX, D_MODEL), ODD_MIX),
        'w_gate': dense((DEPTH_2, D_MODEL, D_FF), D_MODEL),
        'w_up': dense((DEPTH_2, D_MODEL, D_FF), D_MODEL),
        'w_down': dense((DEPTH_2, D_FF, D_MODEL), D_FF),
        'w_ple_proj': dense((DEPTH_2, D_PLE, D_MODEL), D_PLE),
        'w_ple_gate': dense((DEPTH_2, D_MODEL, D_MODEL), D_MODEL),
    }

def second_block(x, p, positions, g_mix, g_ffn, g_ple, ev_w_in, ev_w_conv, ev_g_v, ev_w_s, ev_b_s, ev_w_out,
              od_w_in, od_b_gate, od_g_qa, od_g_kva, od_w_q_up, od_w_kv_up, od_g_q, od_g_k, od_g_mh, od_w_out,
              w_gate, w_up, w_down, w_ple_proj, w_ple_gate):
    h = x
    for layer in range(DEPTH_2):
        j = layer // 2
        hn = rmsnorm_2(h, g_mix[layer])
        if layer % 2 == 0:
            mix = even_mixer(hn, ev_w_in[j], ev_w_conv[j], ev_g_v[j], ev_w_s[j], ev_b_s[j], ev_w_out[j])
        else:
            mix = odd_mixer(hn, positions, od_w_in[j], od_b_gate[j], od_g_qa[j], od_g_kva[j], od_w_q_up[j],
                            od_w_kv_up[j], od_g_q[j], od_g_k[j], od_g_mh[j], od_w_out[j])
        h = h + mix
        h = h + swiglu(rmsnorm_2(h, g_ffn[layer]), w_gate[layer], w_up[layer], w_down[layer])
        gate = jax.nn.sigmoid(rmsnorm_2(h, g_ple[layer]) @ w_ple_gate[layer])
        h = h + gate * (p[layer] @ w_ple_proj[layer])
    return h


def setup_inputs(seed=0):
    out = dict(first_inputs(seed))
    for name, value in second_inputs(seed + 1).items():
        if name != "x":
            out[name + "_2"] = value
    return out


def reference(
    x, mem, norm_g, w_in, w_out, mem_norm_g, w_mem_kv, diff_lambda_q1, diff_lambda_k1,
    diff_lambda_q2, diff_lambda_k2, diff_subln_g, final_norm_g, p_2, positions_2, g_mix_2,
    g_ffn_2, g_ple_2, ev_w_in_2, ev_w_conv_2, ev_g_v_2, ev_w_s_2, ev_b_s_2, ev_w_out_2,
    od_w_in_2, od_b_gate_2, od_g_qa_2, od_g_kva_2, od_w_q_up_2, od_w_kv_up_2, od_g_q_2,
    od_g_k_2, od_g_mh_2, od_w_out_2, w_gate_2, w_up_2, w_down_2, w_ple_proj_2, w_ple_gate_2,
):
    x = first_block(
        x, mem, norm_g, w_in, w_out, mem_norm_g, w_mem_kv, diff_lambda_q1, diff_lambda_k1,
        diff_lambda_q2, diff_lambda_k2, diff_subln_g, final_norm_g,
    )
    return second_block(
        x, p_2, positions_2, g_mix_2, g_ffn_2, g_ple_2, ev_w_in_2, ev_w_conv_2, ev_g_v_2,
        ev_w_s_2, ev_b_s_2, ev_w_out_2, od_w_in_2, od_b_gate_2, od_g_qa_2, od_g_kva_2,
        od_w_q_up_2, od_w_kv_up_2, od_g_q_2, od_g_k_2, od_g_mh_2, od_w_out_2, w_gate_2, w_up_2,
        w_down_2, w_ple_proj_2, w_ple_gate_2,
    )


_drawn_inputs = setup_inputs


def setup_inputs(seed=0):
    import zlib

    import numpy as np

    out = dict(_drawn_inputs(seed))
    spreads = {}
    factors = {'norm_g': 8.0,
     'mem_norm_g': 8.0,
     'g_ple_2': 5.873,
     'ev_g_v_2': 4.17,
     'od_g_qa_2': 8.0,
     'od_g_kva_2': 8.0,
     'od_g_q_2': 8.0,
     'od_g_k_2': 8.0,
     'od_g_mh_2': 18.494}
    for name, (base, spread) in spreads.items():
        noise = np.random.default_rng([zlib.crc32(name.encode()), seed]).standard_normal(out[name].shape)
        drawn = base * np.exp(spread * noise) if base else spread * noise
        out[name] = __import__('jax').numpy.asarray(drawn.astype(out[name].dtype))
    for name, factor in factors.items():
        out[name] = (out[name] * factor).astype(out[name].dtype)
    return out
```

```python
import numpy as np
import concourse.bass as bass
from concourse import mybir
from contextlib import ExitStack

F32 = mybir.dt.float32
F32R = mybir.dt.float32r
I32 = mybir.dt.int32
ACT = mybir.ActivationFunctionType
ALU = mybir.AluOpType
AX = mybir.AxisListType

D, T, NMEM, DPLE, FF = 1024, 512, 256, 256, 2816
DC = D // 128
MIX, HD = 768, 64
QT = T // 128
FCH = FF // 128
PASS = [(0, 8), (8, 8), (16, 6)]
RAW, HL = 5, 4
ACC = 4
BLK = 1024
NEG = -1e30
EPS = 1e-6
DSCALE = 96.0 ** -0.5
ROUND = 12582912.0
TWO_PI = (6.28125, float(np.float32(2 * np.pi - 6.28125)), 2 * np.pi - 6.28125 - float(np.float32(2 * np.pi - 6.28125)))
PI_BELOW = 3.1415925
ORDER = (1, 4, 4)


class Plan:

    def __init__(self):
        self.blocks, self.units, self.acc = [], {}, 0

    def feature(self, name, weight, kc, cols, width=128):
        self.blocks.append((weight, [(k, cols) for k in range(kc)], width))
        self.units[name] = dict(blocks=[(len(self.blocks) - 1, 0, kc)], acc=self.acc, width=width)
        self.acc += 1

    def token(self, name, weight, kc, cols, tiles):
        first = []
        for k0 in range(0, kc, 4):
            n = min(4, kc - k0)
            self.blocks.append((weight, [(k, cols) for k in range(k0, k0 + n)], 256))
            first.append((len(self.blocks) - 1, k0, n))
        self.units[name] = dict(blocks=first, acc=self.acc, width=256, tiles=tiles)
        self.acc += tiles


def layout():
    p = Plan()
    for c in range(2):
        p.feature(("km", c), "mem_kv", DC, ("range", 128 * c))
    p.token(("vm", 0), "mem_kv", DC, ("range", 256), 2)
    for c in range(6):
        p.feature(("q", c), "in", DC, ("range", 128 * c))
    for c in range(6):
        p.feature(("k", c), "in", DC, ("range", MIX + 128 * c))
    for g in range(3):
        p.token(("v", g), "in", DC, ("range", 2 * MIX + 256 * g), QT)
    for c in range(2):
        p.feature(("qm", c), "in", DC, ("range", 3 * MIX + 128 * c))
    for c in range(DC):
        p.feature(("gate", c), "in", DC, ("range", 3 * MIX + 256 + 128 * c))
    for c in range(DC):
        p.feature(("out", c), "out", DC, ("range", 128 * c))
    for layer in range(2):
        if layer == 0:
            for c in range(4):
                p.feature(("cc", c), "ev_in", DC, ("range", 512 + 128 * c))
                p.feature(("cx", c), "ev_in", DC, ("range", 1024 + 128 * c))
                p.feature(("cb", c), "ev_in", DC, ("range", 128 * c))
            for g in range(2):
                p.token(("gv", g), "ev_in", DC, ("range", 2048 + 256 * g), QT)
            for c in range(4):
                p.feature(("gu", c), "ev_in", DC, ("range", 1536 + 128 * c))
            for c in range(DC):
                p.feature(("mixout", 0, c), "ev_out", DC, ("range", 128 * c))
        else:
            for c in range(3):
                p.feature(("ql", c), "od_in", DC, ("range", 128 * c))
            for c in range(2):
                p.feature(("kvl", c), "od_in", DC, ("range", 384 + 128 * c))
            p.feature(("small", 0), "od_in", DC, ("small", 0))
            for c in range(2):
                p.feature(("mq", c), "od_in", DC, ("range", 672 + 128 * c))
            for c in range(2):
                p.feature(("mk", c), "od_in", DC, ("range", 928 + 128 * c))
            for g in range(2):
                p.token(("mv", g), "od_in", DC, ("range", 1184 + 256 * g), QT)
            for c in range(4):
                p.feature(("qn", c), "q_up", 3, ("nope", 96, c))
            for c in range(2):
                p.feature(("qr", c), "q_up", 3, ("rope", 96, c))
            for c in range(4):
                p.feature(("kn", c), "kv_up", 2, ("nope", 128, c))
            for g in range(2):
                p.token(("va", g), "kv_up", 2, ("values", g), QT)
            for c in range(4):
                p.feature(("mo", c), "od_in", DC, ("range", 1696 + 128 * c))
            for c in range(DC):
                p.feature(("mixout", 1, c), "od_out", DC, ("range", 128 * c))
        for n, (f0, fn) in enumerate(PASS):
            for f in range(f0, f0 + fn):
                p.feature(("fg", layer, f), f"gate{layer}", DC, ("range", 128 * f))
                p.feature(("fu", layer, f), f"up{layer}", DC, ("range", 128 * f))
            for c in range(DC):
                p.feature(("fd", layer, n, c), f"down{layer}", fn, ("rows", f0, 128 * c))
        for c in range(DC):
            p.feature(("pg", layer, c), f"ple_gate{layer}", DC, ("range", 128 * c))
            p.feature(("pp", layer, c), f"ple_proj{layer}", DPLE // 128, ("range", 128 * c))
    return p


def block_columns(w, k, spec, width):
    kind = spec[0]
    if kind == "range":
        return w[128 * k:128 * k + 128, spec[1]:spec[1] + width]
    if kind == "rows":
        r = 128 * (spec[1] + k)
        return w[r:r + 128, spec[2]:spec[2] + width]
    rows = w[128 * k:128 * k + 128]
    if kind == "small":
        out = np.zeros((128, 128), w.dtype)
        out[:, 0:32] = rows[:, 640:672]
        out[:, 32:36] = rows[:, 2208:2212]
        out[:, 64:68] = rows[:, 2212:2216]
        return out
    if kind == "nope":
        heads = rows.reshape(128, -1, spec[1])
        return heads[:, 2 * spec[2]:2 * spec[2] + 2, 0:64].reshape(128, 128)
    if kind == "rope":
        heads = rows.reshape(128, -1, spec[1])
        return heads[:, 4 * spec[2]:4 * spec[2] + 4, 64:96].reshape(128, 128)
    if kind == "values":
        heads = rows.reshape(128, -1, 128)
        return heads[:, 4 * spec[1]:4 * spec[1] + 4, 64:128].reshape(128, 256)
    raise ValueError(kind)


VEC = {}


def vector_columns():
    at = 0
    for name, n in (("norm_g", 8), ("mem_norm_g", 8), ("final_g", 8), ("g_mix", 16), ("g_ffn", 16),
                    ("g_ple", 16), ("conv", 12), ("g_qa", 3), ("g_kva", 2), ("g_qn", 1), ("g_qr", 1),
                    ("g_kn", 1), ("g_kr", 1), ("g_mh", 4), ("b_i", 1), ("b_f", 1), ("b_s", 8),
                    ("eps", 1), ("inv_freq", 1), ("halfpi", 1)):
        VEC[name] = at
        at += n
    return at


NVEC = vector_columns()

CONST = {}


def const_columns():
    at = 0
    for name, n in (("ident", 128), ("ones", 128), ("blk64", 128), ("blk32", 128), ("rot", 128),
                    ("upto", 896), ("pair", 256), ("head", 512), ("causal", 128)):
        CONST[name] = at
        at += n
    return at


NCONST = const_columns()


def constants():
    c = np.zeros((128, NCONST), np.float32)
    p = np.arange(128)

    def put(name, a):
        c[:a.shape[0], CONST[name]:CONST[name] + a.shape[1]] = a

    put("ident", np.eye(128))
    put("ones", np.ones((128, 128)))
    put("blk64", p[:, None] // 64 == p[None] // 64)
    put("blk32", p[:, None] // 32 == p[None] // 32)
    rot = np.zeros((128, 128))
    for m in range(128):
        rot[m + 16 if m % 32 < 16 else m - 16, m] = -1 if m % 32 < 16 else 1
    put("rot", rot)
    put("upto", np.arange(896)[None] - 384 >= p[:, None])
    pair = np.zeros((4, 2, 128))
    for j in range(4):
        pair[j, j % 2, 64 * (j // 2):64 * (j // 2) + 64] = 1
    put("pair", pair.reshape(4, 256))
    head = np.zeros((4, 4, 128))
    for j in range(4):
        head[j, j] = 1
    put("head", head.reshape(4, 512))
    slopes = (2.0 ** (-8.0 * np.arange(1, 13) / 12)).astype(np.float32)
    bias = np.zeros((128, 4, 512), np.float32)
    b0 = bias[:, 0:2].reshape(128, 2, 2, 256)
    dist = (p[:, None] + 128) - np.arange(256)[None]
    for par in range(2):
        for hh in range(2):
            s = slopes[2 * hh + par]
            b0[:, par, hh] = np.where((dist >= 0) & (dist <= 128), -s * dist.astype(np.float32), NEG)
    d = p[:, None] - p[None]
    for par in range(2):
        for hh in range(2):
            at = (2 * par + hh) * 128
            s = slopes[4 + 2 * hh + par] * np.float32(4)
            bias[:, 2, at:at + 128] = np.where(d >= 0, -s * d.astype(np.float32), NEG)
            s = slopes[8 + 2 * hh + par] * np.float32(16)
            bias[:, 3, at:at + 128] = np.where((d >= 0) & (d % 4 == 0), -s * (d // 4).astype(np.float32), NEG)
    put("causal", np.where(d >= 0, 0.0, NEG))
    return c, bias.reshape(128, 2048)


def build(nc, x, mem, wall, ple, vec, table, bias, ws, bs, gv, pos, y):
    plan = layout()
    blocks, units = plan.blocks, plan.units
    used_width = [len(parts) * width for _, parts, width in blocks]
    nblk = len(blocks)

    ctx = ExitStack()
    with ctx:
        base = (nc.sbuf_base + 63) // 64 * 64
        top = [base]

        def place(name, shape, dt=F32, at=None):
            size = 4 * int(np.prod(shape[1:]))
            off = top[0] if at is None else at
            if at is None:
                top[0] += (size + 31) // 32 * 32
            return nc.alloc_sbuf_tensor_at(name, shape, dt, offset=off)

        KB = 1024
        X = place("x_res", [128, DC, T])
        first = top[0]
        XH = place("xg_hi", [128, DC, T], F32R)
        XL = place("xg_lo", [128, DC, T], F32R)
        second = top[0]
        YH = place("y_hi", [128, DC, T], F32R)
        YL = place("y_lo", [128, DC, T], F32R)
        scratch = top[0]
        top[0] += 56 * KB
        RAWT = place("w_raw", [128, RAW, BLK])
        WH = place("w_hi", [128, HL, BLK], F32R)
        WL = place("w_lo", [128, HL, BLK], F32R)
        VECT = place("vec_t", [128, NVEC])
        CT = place("const_t", [128, NCONST])
        RB = place("rstd_rows", [128, T])
        TMP = place("tmp", [128, 4, T])
        SQ = place("squares", [128, 2, T])
        SSQ = place("sum_sq", [128, T])
        STD = place("std", [128, T])
        RC = place("rstd_cols", [128, 14])
        GR = place("gate_rows", [4, 2, T])
        STAT = place("stats", [128, 3, 4, 4, 2])
        NEGM = place("neg_max", [128, 16])
        SUM = place("row_sum", [128, 16])
        assert top[0] <= nc.sbuf_usable_end, (top[0], nc.sbuf_usable_end)

        Q = place("q_a", [128, 6, T], at=second)
        QM = place("qm_a", [128, 2, T], at=second + 12 * KB)
        K = place("k_a", [128, 6, T], at=second + 16 * KB)
        KM = place("km_a", [128, 2, NMEM], at=second + 28 * KB)
        MIXT = place("mix_a", [128, DC, T], at=scratch)
        V = place("v_a", [128, 3, QT, 256], at=scratch + 16 * KB)
        VM = place("vm_a", [128, 2, 256], at=scratch + 28 * KB)
        SB = place("scores_a", [128, 2, 4, 256], at=scratch + 30 * KB)
        PT = place("probs_t_a", [128, 2, 8, 128], at=scratch + 38 * KB)
        ROWS = place("rows_a", [4, 6, T], at=scratch + 30 * KB)
        BIAS = place("bias_a", [128, 4, T], at=scratch + 48 * KB)
        MEMX = place("mem_a", [128, DC, NMEM], at=scratch + 16 * KB)
        MH = place("mem_hi", [128, DC, NMEM], F32R, at=scratch)
        ML = place("mem_lo", [128, DC, NMEM], F32R, at=scratch + 8 * KB)
        RBM = place("rstd_mem", [128, NMEM], at=scratch + 46 * KB)

        GV = place("gv_b", [128, QT, 512], at=scratch)
        WS = place("ws_b", [128, 8, 128], at=scratch + 8 * KB)
        BS = place("bs_b", [128, 4, 128], at=scratch + 12 * KB)
        GVB = place("gvb_b", [128, 512], at=scratch + 14 * KB)
        MB = place("spatial_b", [128, 4, T], at=scratch + 16 * KB)
        SV = place("gv_sq_b", [128, 512], at=scratch + 24 * KB)
        SS = place("gv_ss_b", [128, QT, 8], at=scratch + 26 * KB)

        PR = place("ple_raw", [128, 2, T], at=scratch)
        PH = place("ple_hi", [128, 2, T], F32R, at=scratch + 4 * KB)
        PL = place("ple_lo", [128, 2, T], F32R, at=scratch + 8 * KB)

        QF = place("q_full", [96, 8, T], at=first)
        KF = place("k_full", [96, 8, T], at=first + 16 * KB)
        LAT = place("latent", [128, 5, T], at=first)
        SMALL = place("small_d", [128, T], at=first + 10 * KB)
        LH = place("lat_hi", [128, 5, T], F32R, at=scratch)
        LL = place("lat_lo", [128, 5, T], F32R, at=scratch + 10 * KB)
        MQ = place("mq_d", [128, 2, T], at=scratch + 20 * KB)
        MK = place("mk_d", [128, 2, T], at=scratch + 24 * KB)
        MV = place("mv_d", [128, QT, 512], at=scratch + 28 * KB)
        MO = place("mo_d", [128, 4, T], at=scratch + 36 * KB)
        VA = place("va_d", [128, QT, 512], at=scratch + 44 * KB)
        COS = place("cos_d", [128, T], at=scratch + 52 * KB)
        SIN = place("sin_d", [128, T], at=scratch + 54 * KB)
        POS = place("pos_d", [128, T], I32, at=scratch + 50 * KB)
        PD = place("probs_d", [128, 4, T], at=scratch)
        PTD = place("probs_t_d", [128, 2, T], at=scratch + 8 * KB)
        WT = place("decay_d", [128, 4, T], at=first + 16 * KB)
        SW = place("weighted_d", [128, 4, T], at=first)
        HT = place("mh_d", [128, 4, T], at=first + 24 * KB)
        LFC = place("cols_d", [128, 2, 4, 4], at=scratch + 52 * KB)
        I_ROW, F_ROW = GR[:, 0, :], GR[:, 1, :]
        G_ROW, A_ROW = SSQ[0:4, :], STD[0:4, :]
        MAX_ROWS = (TMP[0:4, 2, :], TMP[0:4, 3, :])
        M_G, M_S, M_NUM, M_DEN, M_FLOOR = 4, (5, 6, 0), (2, 1), 3, 7
        HEADS = ([("small", 0, 32, "g_kr")] + [("qn", c, 64, "g_qn") for c in range(4)]
                 + [("qr", c, 32, "g_qr") for c in range(2)] + [("kn", c, 64, "g_kn") for c in range(4)])

        PS = ctx.enter_context(nc.psum_tensor("psum", [128, 8, 512], F32))

        def const(name, rows=128, at=0, n=128):
            return CT[0:rows, CONST[name] + at:CONST[name] + at + n]

        def col(name, c=0, rows=slice(0, 128)):
            return VECT[rows, VEC[name] + c:VEC[name] + c + 1]

        sems = {}

        def S(name):
            if name not in sems:
                sems[name] = ctx.enter_context(nc.semaphore(name))
            return sems[name]

        class Tally:

            def __init__(self):
                self.n = {}

            def made(self, name):
                self.n[name] = self.n.get(name, 0) + 1
                return 1

            def next(self, name, more=1):
                self.n[name] = self.n.get(name, 0) + more
                return self.n[name]

            def last(self, name):
                return self.n[name]

        raw_full = [ctx.enter_context(nc.semaphore(f"raw_full{i}")) for i in range(RAW)]
        acc_free = [ctx.enter_context(nc.semaphore(f"acc_free{i}")) for i in range(ACC)]
        S("hi_done"), S("lo_done"), S("block_used")

        def last_block(u):
            return units[u]["blocks"][-1][0]

        def bank(u, tile=0):
            return (units[u]["acc"] + tile) % ACC

        def residue(ap, g):
            return ap if g == 0 else ap.rearrange("p (u r) -> p r u", r=ORDER[g])

        def tile_tokens(ap, g, i):
            if g in (0, 3):
                return ap[:, 128 * i:128 * i + 128]
            return ap.rearrange("p (u r) -> p r u", r=4)[:, i, :]

        def freed(u, tile=0):
            return (units[u]["acc"] + tile) // ACC + 1

        TILES = [(g, i) for g in (3, 0, 1, 2) for i in range(QT)]

        SPAIR = (4, 0)

        def sbuf(n):
            return SB[:, n % 2, :, :] if n % 4 < 2 else TMP[:, 2 * (n % 2):2 * (n % 2) + 2, :].rearrange("p a (b k) -> p (a b) k", b=2)

        def keys(g, i):
            if g == 3:
                return NMEM, 0
            if g == 0:
                return (256, 128 * (i - 1)) if i else (128, 0)
            return 128, 128 * i

        TURNED = np.cumsum([keys(g, i)[0] // 128 for g, i in TILES]).tolist()

        DTILES = [(h, i) for h in range(8) for i in range(QT)]
        SBANK = (4, 5, 0, 1)

        block = ctx.enter_context(nc.Block())

        @block.sync
        def _(sp):
            def load(dst, src, name):
                sp.dma_start(dst, src).then_inc(S(name), 16)

            load(MEMX[:], mem, "mem_in")
            load(VECT[:], vec, "vec_in")
            for j in range(nblk):
                if j >= RAW:
                    sp.wait_ge(S("lo_done"), j - RAW + 1)
                n = used_width[j]
                sp.dma_start(RAWT[:, j % RAW, 0:n], wall[j, :, 0:n]).then_inc(raw_full[j % RAW], 16)
                if j == 0:
                    load(CT[:], table, "const_in")
                    load(X[:], x, "x_in")
                    load(BIAS[:], bias.rearrange("p (a b) -> p a b", a=4), "bias_in")
            for c in range(DC):
                sp.wait_ge(S("x_final"), 7 * DC + 1 + c)
                load(y[:, c, :], X[:, c, :], "y_out")
            sp.wait_ge(S("y_out"), 16 * DC)

        @block.gpsimd
        def _(pool):
            for j in range(nblk):
                n, r, s = used_width[j], j % RAW, j % HL
                pool.wait_ge(S("hi_done"), j + 1)
                pool.wait_ge(raw_full[r], 16 * (j // RAW + 1))
                nc.gpsimd.tensor_tensor(WL[:, s, 0:n], RAWT[:, r, 0:n], WH[:, s, 0:n].bitcast(F32),
                                        ALU.subtract).then_inc(S("lo_done"), 1)

        @block.scalar
        def _(act):
            t = Tally()
            at = [0]

            def split_to(j):
                while at[0] <= min(j, nblk - 1):
                    b = at[0]
                    n, r, s = used_width[b], b % RAW, b % HL
                    act.wait_ge(raw_full[r], 16 * (b // RAW + 1))
                    if b >= HL:
                        act.wait_ge(S("block_used"), b - HL + 1)
                    nc.scalar.activation(WH[:, s, 0:n], RAWT[:, r, 0:n], ACT.Copy).then_inc(S("hi_done"), 1)
                    at[0] += 1

            def unit(u):
                split_to(last_block(u) + HL - 1)
                act.wait_ge(S("block_used"), last_block(u) + 1)

            def halves(name, chunks, hi, src, scale, sq=None, behind=None):
                for c in range(chunks):
                    if behind is not None:
                        split_to(last_block(behind(c)) + HL - 1)
                    if name is not None:
                        act.wait_ge(S(name), t.next(name))
                    if sq is not None:
                        if t.n.get("sq_made", 0) >= 2:
                            act.wait_ge(S("sq_taken"), t.next("sq_taken"))
                        nc.scalar.activation(sq(c), src(c), ACT.Square).then_inc(S("sq_made"), t.made("sq_made"))
                    if hi is not None:
                        nc.scalar.activation(hi(c), src(c), ACT.Copy, scale=scale(c)).then_inc(S("xg_hi_made"), t.made("xg_hi_made"))

            def tables(name):
                nc.scalar.preload_act_table_set(name)

            LOG_EXP, SILU, SIGMOID = "natural_log_exp_and_others", "silu_and_others", "sigmoid_and_others"
            GELU = "gelu_apprx_tanh_and_others"

            def inverse_root(out, src, width, signal, between=None, rows=slice(0, 128)):
                mid = out if between is None else between
                nc.scalar.activation(mid, src, ACT.Ln, scale=1.0 / width, bias=col("eps", rows=rows)).then_inc(S("act_step"), t.made("act_step"))
                act.wait_ge(S("act_step"), t.last("act_step"))
                nc.scalar.activation(out, mid, ACT.Exp, scale=-0.5).then_inc(S(signal), t.made(signal))

            def x_norm(gain, ready="x_final", behind=None, hi=XH):
                halves(ready, DC, (lambda c: hi[:, c, :]) if gain else None, lambda c: X[:, c, :],
                       lambda c: col(gain[0], gain[1] + c), lambda c: SQ[:, c % 2, :], behind)

            def norm_part(c, gain, hi):
                act.wait_ge(S("x_final"), t.next("x_final"))
                act.wait_ge(S("sq_taken"), t.next("sq_taken"))
                nc.scalar.activation(SQ[:, c % 2, :], X[:, c, :], ACT.Square).then_inc(S("sq_made"), t.made("sq_made"))
                nc.scalar.activation(hi[:, c, :], X[:, c, :], ACT.Copy, scale=col(gain[0], gain[1] + c)).then_inc(S("xg_hi_made"), t.made("xg_hi_made"))

            def norm_root(then=None):
                tables(LOG_EXP)
                act.wait_ge(S("ssum_done"), t.next("ssum_done"))
                inverse_root(RB[:, :], PS[:, 4, :], D, "rstd_made", STD[:, :])
                if then is not None:
                    tables(then)

            tables(LOG_EXP)
            act.wait_ge(S("mem_in"), 16)
            act.wait_ge(S("vec_in"), 16)
            halves(None, DC, lambda c: MH[:, c, :], lambda c: MEMX[:, c, :],
                   lambda c: col("mem_norm_g", c), lambda c: SQ[:, c % 2, 0:NMEM])
            split_to(HL - 1)
            act.wait_ge(S("ssum_done"), t.next("ssum_done"))
            inverse_root(RBM[:, :], PS[:, 4, 0:NMEM], D, "rstd_made", STD[:, 0:NMEM])
            split_to(last_block(("vm", 0)) + HL - 2)
            act.wait_ge(S("x_in"), 16)
            x_norm(("norm_g", 0), None)
            unit(("vm", 0))
            act.wait_ge(S("cols_made"), t.next("cols_made"))
            for i in range(2):
                nc.scalar.activation(VM[:, i, :], PS[:, bank(("vm", 0), i), 0:256], ACT.Copy,
                                     scale=RC[:, 12 + i:13 + i]).then_inc(acc_free[bank(("vm", 0), i)], 1)
            split_to(last_block(("q", 0)) + HL - 1)
            norm_root()
            for u in [("q", c) for c in range(6)] + [("k", c) for c in range(6)]:
                split_to(last_block(u) + HL - 1)
            for g in range(3):
                unit(("v", g))
                if g == 0:
                    act.wait_ge(S("cols_made"), t.next("cols_made"))
                for i in range(QT):
                    b = bank(("v", g), i)
                    nc.scalar.activation(V[:, g, i, :], PS[:, b, 0:256], ACT.Copy,
                                         scale=RC[:, 4 * g + i:4 * g + i + 1]).then_inc(acc_free[b], 1)
            for c in range(2):
                unit(("qm", c))

            def exps(n):
                g, i = TILES[n]
                w, _ = keys(g, i)
                act.wait_ge(S("scores_ready"), t.next("scores_ready"))
                for j in range(4):
                    ins = nc.scalar.activation(
                        sbuf(n)[:, j, 0:w], sbuf(n)[:, j, 0:w], ACT.Exp,
                        bias=NEGM[:, 4 * (n % 4) + j:4 * (n % 4) + j + 1], scale=0.125 if g == 3 else 1.0,
                        accum_out=(SUM[:, 4 * (n % 4) + j:4 * (n % 4) + j + 1] if g == 3 else STAT[:, g, i, j, 1:2]))
                ins.then_inc(S("probs_made"), t.made("probs_made"))

            def transposed(n):
                g, i = TILES[n]
                nb = keys(g, i)[0] // 128
                for half in range(nb):
                    act.wait_ge(S("turned"), t.next("turned"))
                    nc.scalar.activation(PT[:, n % 2, 4 * half:4 * half + 4, :], PS[:, 6 + (t.n["turned"] - 1) % 2, :],
                                         ACT.Copy).then_inc(S("turned_kept"), t.made("turned_kept"))

            def mixed(n):
                g, i = TILES[n]
                act.wait_ge(S("mixed"), t.next("mixed"))
                c0 = 6 if g == 3 else 2 * g
                for hh in range(2):
                    src = PS[:, 2 + n % 2, 128 * hh:128 * hh + 128]
                    dst = tile_tokens(MIXT[:, c0 + hh, :], g, i)
                    ins = nc.scalar.activation(dst, src, ACT.Copy)
                ins.then_inc(S("mix_kept"), t.made("mix_kept"))

            for n in range(len(TILES)):
                exps(n)
                if n >= 1:
                    transposed(n - 1)
                if n >= 3:
                    mixed(n - 3)
            transposed(len(TILES) - 1)
            for n in range(len(TILES) - 3, len(TILES)):
                mixed(n)
            act.wait_ge(S("row_max_ready"), t.next("row_max_ready"))
            for g in range(3):
                ins = nc.scalar.activation(ROWS[:, g, :], ROWS[:, g, :], ACT.Exp)
            ins.then_inc(S("row_exp"), t.made("row_exp"))

            def y_hi(dst):
                act.wait_ge(S("y_made"), t.next("y_made"))
                nc.scalar.activation(dst, TMP[:, 2 + (t.n["y_made"] - 1) % 2, :], ACT.Copy).then_inc(S("y_hi_made"), t.made("y_hi_made"))

            for c in range(DC):
                split_to(last_block(("gate", c)) + HL - 1)
                act.wait_ge(S("pre"), t.next("pre"))
                nc.scalar.activation(TMP[:, c % 2, :], TMP[:, c % 2, :], ACT.Silu).then_inc(S("gate_made"), t.made("gate_made"))
                y_hi(YH[:, c, :])
            x_norm(None, behind=lambda c: ("out", c))
            norm_root()
            x_norm(("g_mix", 0))
            act.dma_start(WS[:], ws.rearrange("p (a b) -> p a b", a=8)).then_inc(S("ws_in"), 16)
            act.dma_start(BS[:], bs.rearrange("p (a b) -> p a b", a=4)).then_inc(S("bs_in"), 16)
            act.dma_start(GVB[:], gv).then_inc(S("gv_in"), 16)
            split_to(last_block(("cc", 0)) + HL - 1)
            norm_root(GELU)
            for c in range(4):
                for k in ("cc", "cx", "cb"):
                    split_to(last_block((k, c)) + HL - 1)
                y_hi(YH[:, c, :])
            for g in range(2):
                unit(("gv", g))
                if g == 0:
                    act.wait_ge(S("cols_made"), t.next("cols_made"))
                for i in range(QT):
                    b = bank(("gv", g), i)
                    nc.scalar.activation(GV[:, i, 256 * g:256 * g + 256], PS[:, b, 0:256], ACT.Gelu_apprx_tanh,
                                         scale=RC[:, i:i + 1]).then_inc(acc_free[b], 1)
            split_to(last_block(("gu", 0)) + HL - 1)
            tables(LOG_EXP)
            act.wait_ge(S("gv_summed"), t.next("gv_summed"))
            inverse_root(SS[:, :, :], SS[:, :, :], 64, "gv_rstd_made")
            tables(GELU)
            for c in range(4):
                split_to(last_block(("gu", c)) + HL - 1)
                act.wait_ge(S("pre"), t.next("pre"))
                nc.scalar.activation(TMP[:, c % 2, :], TMP[:, c % 2, :], ACT.Gelu_apprx_tanh).then_inc(S("gate_made"), t.made("gate_made"))
                y_hi(YH[:, 4 + c, :])
            x_norm(("g_ffn", 0), behind=lambda c: ("mixout", 0, c))

            def feed_forward(layer):
                act.dma_start(PR[:], ple[layer]).then_inc(S("ple_in"), 16)
                split_to(last_block(("fg", layer, 0)) + HL - 1)
                norm_root(SILU)
                for n, (f0, fn) in enumerate(PASS):
                    for f in range(f0, f0 + fn):
                        split_to(last_block(("fg", layer, f)) + HL - 1)
                        act.wait_ge(S("pre"), t.next("pre"))
                        nc.scalar.activation(TMP[:, f % 2, :], TMP[:, f % 2, :], ACT.Silu).then_inc(S("gate_made"), t.made("gate_made"))
                        split_to(last_block(("fu", layer, f)) + HL - 1)
                        if f == f0 and n:
                            act.wait_ge(S("block_used"), last_block(("fd", layer, n - 1, DC - 1)) + 1)
                        y_hi(YH[:, f - f0, :])
                    if n < len(PASS) - 1:
                        for c in range(DC):
                            split_to(last_block(("fd", layer, n, c)) + HL - 1)
                x_norm(("g_ple", DC * layer), behind=lambda c: ("fd", layer, len(PASS) - 1, c))

            def embed(layer):
                act.wait_ge(S("ple_in"), 16 * (layer + 1))
                for c in range(2):
                    nc.scalar.activation(PH[:, c, :], PR[:, c, :], ACT.Copy).then_inc(S("ple_hi_made"), t.made("ple_hi_made"))
                split_to(last_block(("pg", layer, 0)) + HL - 1)
                norm_root(SIGMOID)
                for c in range(DC):
                    split_to(last_block(("pg", layer, c)) + HL - 1)
                    act.wait_ge(S("pre"), t.next("pre"))
                    nc.scalar.activation(TMP[:, c % 2, :], TMP[:, c % 2, :], ACT.Sigmoid).then_inc(S("gate_made"), t.made("gate_made"))
                    split_to(last_block(("pp", layer, c)) + HL - 1)
                    if layer == 0:
                        norm_part(c, ("g_mix", DC), YH)

            feed_forward(0)
            embed(0)
            act.dma_start(POS[:], pos).then_inc(S("pos_in"), 16)
            split_to(last_block(("ql", 0)) + HL - 1)
            norm_root()
            act.wait_ge(S("angle_made"), t.next("angle_made"))
            nc.scalar.activation(SIN[:, :], TMP[:, 3, :], ACT.Sin).then_inc(S("act_step"), t.made("act_step"))
            nc.scalar.activation(TMP[:, 3, :], TMP[:, 3, :], ACT.Abs).then_inc(S("act_step"), t.made("act_step"))
            act.wait_ge(S("act_step"), t.last("act_step"))
            nc.scalar.activation(COS[:, :], TMP[:, 3, :], ACT.Sin, scale=-1.0, bias=col("halfpi")).then_inc(S("rotary_made"), t.made("rotary_made"))
            tables(LOG_EXP)

            def latent_squares(chunks):
                for c in chunks:
                    split_to(last_block(("ql", c) if c < 3 else ("kvl", c - 3)) + HL - 1)
                    act.wait_ge(S("lat_made"), t.next("lat_made"))
                    act.wait_ge(S("sq_taken"), t.next("sq_taken"))
                    nc.scalar.activation(SQ[:, c % 2, :], LAT[:, c, :], ACT.Square).then_inc(S("sq_made"), t.made("sq_made"))

            def latent_root(width):
                act.wait_ge(S("ssum_done"), t.next("ssum_done"))
                inverse_root(STD[:, :], PS[:, 4, :], width, "lat_rstd_made")

            latent_squares(range(3))
            split_to(last_block(("kvl", 1)) + HL - 2)
            latent_root(384)
            latent_squares(range(3, 5))
            split_to(last_block(("small", 0)) + HL - 1)
            latent_root(256)
            for c in range(5):
                act.wait_ge(S("lat_normed"), t.next("lat_normed"))
                nc.scalar.activation(LH[:, c, :], LAT[:, c, :], ACT.Copy).then_inc(S("lat_hi_made"), t.made("lat_hi_made"))
            for u in [("mq", 0), ("mq", 1), ("mk", 0), ("mk", 1)]:
                split_to(last_block(u) + HL - 1)
            for g in range(2):
                unit(("mv", g))
                if g == 0:
                    act.wait_ge(S("cols_made"), t.next("cols_made"))
                for i in range(QT):
                    b = bank(("mv", g), i)
                    nc.scalar.activation(MV[:, i, 256 * g:256 * g + 256], PS[:, b, 0:256], ACT.Copy,
                                         scale=RC[:, i:i + 1]).then_inc(acc_free[b], 1)

            def head_square(m):
                u, c, rows, _ = HEADS[m]
                if m:
                    split_to(last_block((u, c)) + HL - 1)
                act.wait_ge(S("head_raw"), t.next("head_raw"))
                if m >= 2:
                    act.wait_ge(S("head_taken"), t.next("head_taken"))
                r = 32 if m == 0 else 128
                src = SMALL[0:32, :] if m == 0 else TMP[:, m % 2, :]
                nc.scalar.activation(SQ[0:r, m % 2, :], src, ACT.Square).then_inc(S("head_sq_made"), t.made("head_sq_made"))

            def head_root(m):
                _, _, rows, _ = HEADS[m]
                r = 32 if m == 0 else 128
                act.wait_ge(S("head_summed"), t.next("head_summed"))
                inverse_root(SQ[0:r, m % 2, :], PS[0:r, 5 + m % 2, :], rows, "head_rstd_made", rows=slice(0, r))

            for m in range(len(HEADS)):
                head_square(m)
                if m >= 1:
                    head_root(m - 1)
                if m == 1:
                    act.wait_ge(S("kr_made"), t.next("kr_made"))
                    for h in range(8):
                        ins = nc.scalar.activation(KF[64:96, h, :], TMP[0:32, 2, :], ACT.Copy)
                    ins.then_inc(S("kr_kept"), t.made("kr_kept"))
            head_root(len(HEADS) - 1)
            act.wait_ge(S("gate_rows_made"), t.next("gate_rows_made"))
            nc.scalar.activation(G_ROW, F_ROW, ACT.Abs).then_inc(S("act_step"), t.made("act_step"))
            act.wait_ge(S("act_step"), t.last("act_step"))
            nc.scalar.activation(G_ROW, G_ROW, ACT.Exp, scale=-1.0).then_inc(S("act_step"), t.made("act_step"))
            act.wait_ge(S("act_step"), t.last("act_step"))
            nc.scalar.activation(G_ROW, G_ROW, ACT.Ln, bias=1.0).then_inc(S("softplus_made"), t.made("softplus_made"))
            tables(SIGMOID)
            for g in range(2):
                unit(("va", g))
                for i in range(QT):
                    b = bank(("va", g), i)
                    nc.scalar.activation(VA[:, i, 256 * g:256 * g + 256], PS[:, b, 0:256], ACT.Copy).then_inc(acc_free[b], 1)
            for c in range(4):
                split_to(last_block(("mo", c)) + HL - 1)
                act.wait_ge(S("pre"), t.next("pre"))
                nc.scalar.activation(MO[:, c, :], TMP[:, c % 2, :], ACT.Sigmoid).then_inc(S("gate_made"), t.made("gate_made"))

            tables(LOG_EXP)
            act.wait_ge(S("rows_made"), t.next("rows_made"))
            nc.scalar.activation(F_ROW, F_ROW, ACT.Exp, scale=-1.0).then_inc(S("floor_made"), t.made("floor_made"))

            def d_exp(n):
                h, i = DTILES[n]
                w = 128 * (i + 1)
                act.wait_ge(S("d_max_ready"), t.next("d_max_ready"))
                nc.scalar.activation(PD[:, n % 4, 0:w], PS[:, SBANK[n % 4], 0:w], ACT.Exp, scale=DSCALE,
                                     bias=NEGM[:, n % 4:n % 4 + 1], accum_out=SUM[:, n % 4:n % 4 + 1]).then_inc(S("d_exp_made"), t.made("d_exp_made"))

            def d_keep(n):
                h, i = DTILES[n]
                w = 128 * (i + 1)
                act.wait_ge(S("d_turned"), t.next("d_turned"))
                nc.scalar.activation(PTD[:, n % 2, 0:w], PS[:, 6 + n % 2, 0:w], ACT.Copy).then_inc(S("d_turn_kept"), t.made("d_turn_kept"))
                if n % 8 == 1 and n > 1:
                    d_hi(n // 8 - 1)

            def d_hi(c):
                act.wait_ge(S("d_mixed"), t.next("d_mixed"))
                nc.scalar.activation(YH[:, c, :], PS[:, 2 + c % 2, :], ACT.Copy).then_inc(S("y_hi_made"), t.made("y_hi_made"))

            for n in range(len(DTILES)):
                d_exp(n)
                if n >= 3:
                    d_keep(n - 3)
            for n in range(len(DTILES) - 3, len(DTILES)):
                d_keep(n)
            d_hi(3)

            def denominator(h):
                act.wait_ge(S("h_summed"), t.next("h_summed"))
                nc.scalar.activation(TMP[:, 0, :], PS[:, M_DEN, :], ACT.Abs).then_inc(S("den_abs"), t.made("den_abs"))

            for k in range(16):
                act.wait_ge(S("decay_pre"), t.next("decay_pre"))
                w = T - 128 * (k % 4)
                nc.scalar.activation(WT[:, k % 4, 0:w], WT[:, k % 4, 0:w], ACT.Exp).then_inc(S("decay_made"), t.made("decay_made"))
                if k % 4 == 2 and k > 4:
                    denominator(k // 4 - 1)
            denominator(3)

            def h_square(h):
                if h == 0:
                    act.wait_ge(S("h_made"), t.next("h_made", 4))
                nc.scalar.activation(SQ[:, h % 2, :], HT[:, h, :], ACT.Square).then_inc(S("h_sq_made"), t.made("h_sq_made"))

            h_square(0)
            for h in range(4):
                if h < 3:
                    h_square(h + 1)
                act.wait_ge(S("h_sq_summed"), t.next("h_sq_summed"))
                inverse_root(SQ[:, h % 2, :], PS[:, 5 + h % 2, :], 128, "h_rstd_made")
                y_hi(YH[:, 4 + h, :])
            x_norm(("g_ffn", DC), behind=lambda c: ("mixout", 1, c))
            feed_forward(1)
            embed(1)

        @block.vector
        def _(dve):
            t = Tally()

            def unit(u):
                dve.wait_ge(S("block_used"), last_block(u) + 1)

            def free(ins, u, tile=0):
                ins.then_inc(acc_free[bank(u, tile)], 1)

            def free_after(name, u):
                dve.wait_ge(S(name), t.last(name))
                dve.sem_inc(acc_free[bank(u)], 1)

            def sum_squares(c, n=T, first=0):
                dve.wait_ge(S("sq_made"), t.next("sq_made"))
                if c == first:
                    ins = nc.vector.tensor_copy(SSQ[:, 0:n], SQ[:, c % 2, 0:n])
                else:
                    dve.wait_ge(S("sq_taken"), t.n["sq_taken"])
                    ins = nc.vector.tensor_tensor(SSQ[:, 0:n], SSQ[:, 0:n], SQ[:, c % 2, 0:n], ALU.add)
                ins.then_inc(S("sq_taken"), t.made("sq_taken"))

            def lo_part(c, lo, src, g, hi):
                dve.wait_ge(S("xg_hi_made"), t.next("xg_hi_made"))
                nc.vector.scalar_tensor_tensor(lo, src, g, hi.bitcast(F32), ALU.mult, ALU.subtract).then_inc(S("xg_lo_made"), t.made("xg_lo_made"))

            def norm_rows():
                dve.wait_ge(S("rstd_made"), t.next("rstd_made"))

            dve.wait_ge(S("mem_in"), 16)
            dve.wait_ge(S("vec_in"), 16)
            for c in range(DC):
                sum_squares(c, NMEM)
                lo_part(c, ML[:, c, :], MEMX[:, c, :], col("mem_norm_g", c), MH[:, c, :])
            norm_rows()
            for c in range(2):
                unit(("km", c))
                free(nc.vector.tensor_tensor(KM[:, c, :], PS[:, bank(("km", c)), 0:NMEM], RBM[:, :], ALU.mult),
                     ("km", c))
            dve.wait_ge(S("cols_summed"), t.next("cols_summed"))
            nc.vector.tensor_copy(RC[:, 12:14], PS[:, 7, 12:14]).then_inc(S("cols_made"), t.made("cols_made"))
            dve.wait_ge(S("x_in"), 16)
            for c in range(DC):
                sum_squares(c)
                lo_part(c, XL[:, c, :], X[:, c, :], col("norm_g", c), XH[:, c, :])
            norm_rows()
            for c in range(6):
                unit(("q", c))
                g = c // 2
                free(nc.vector.tensor_tensor(residue(Q[:, c, :], 0) if g == 0 else Q[:, c, :].rearrange("p (r u) -> p r u", r=ORDER[g]),
                                             residue(PS[:, bank(("q", c)), :], g), residue(RB[:, :], g), ALU.mult), ("q", c))
            dve.wait_ge(S("cols_summed"), t.next("cols_summed"))
            nc.vector.tensor_copy(RC[:, 0:12], PS[:, 7, 0:12]).then_inc(S("cols_made"), t.made("cols_made"))
            for c in range(6):
                unit(("k", c))
                g = c // 2
                free(nc.vector.tensor_tensor(K[:, c, :] if g == 0 else K[:, c, :].rearrange("p (r u) -> p r u", r=ORDER[g]),
                                             residue(PS[:, bank(("k", c)), :], g), residue(RB[:, :], g), ALU.mult), ("k", c))
            for c in range(2):
                unit(("qm", c))
                nc.vector.tensor_tensor(QM[:, c, :], PS[:, bank(("qm", c)), :], RB[:, :], ALU.mult).then_inc(S("qk_ready"), t.made("qk_ready"))
                free_after("qk_ready", ("qm", c))

            def scores(n):
                g, i = TILES[n]
                w, _ = keys(g, i)
                dve.wait_ge(S("scored"), t.next("scored"))
                if n >= 4:
                    dve.wait_ge(S("turned"), TURNED[n - 4])
                s = sbuf(n)[:, :, 0:w]
                psum = PS[:, SPAIR[n % 2]:SPAIR[n % 2] + 2, 0:2 * w]
                if g == 3:
                    nc.vector.tensor_copy(sbuf(n).rearrange("p (a b) k -> p a (b k)", a=2), psum).then_inc(S("dve_step"), t.made("dve_step"))
                    dve.wait_ge(S("dve_step"), t.last("dve_step"))
                elif w == 256:
                    b = BIAS[:, 0:2, :]
                    nc.vector.scalar_tensor_tensor(sbuf(n).rearrange("p (a b) k -> p a (b k)", a=2), psum,
                                                   0.125, b, ALU.mult, ALU.add).then_inc(S("dve_step"), t.made("dve_step"))
                    dve.wait_ge(S("dve_step"), t.last("dve_step"))
                else:
                    for par in range(2):
                        if g == 0:
                            b = BIAS[:, par, :].rearrange("p (b k) -> p b k", b=2)[:, :, 128:256]
                        else:
                            b = BIAS[:, 1 + g, 256 * par:256 * par + 256].rearrange("p (b k) -> p b k", b=2)
                        ins = nc.vector.scalar_tensor_tensor(
                            sbuf(n)[:, 2 * par:2 * par + 2, 0:128],
                            PS[:, SPAIR[n % 2] + par, 0:256].rearrange("p (b k) -> p b k", b=2), 0.125, b, ALU.mult, ALU.add)
                        ins.then_inc(S("dve_step"), t.made("dve_step"))
                    dve.wait_ge(S("dve_step"), t.last("dve_step"))
                nc.vector.tensor_reduce(NEGM[:, 4 * (n % 4):4 * (n % 4) + 4], s, AX.X, ALU.max, negate=True).then_inc(S("dve_step"), t.made("dve_step"))
                dve.wait_ge(S("dve_step"), t.last("dve_step"))
                if g == 3:
                    ins = nc.vector.tensor_scalar(NEGM[:, 4 * (n % 4):4 * (n % 4) + 4], NEGM[:, 4 * (n % 4):4 * (n % 4) + 4],
                                                  0.125, None, ALU.mult)
                else:
                    ins = nc.vector.tensor_scalar(STAT[:, g, i, :, 0], NEGM[:, 4 * (n % 4):4 * (n % 4) + 4],
                                                  -1.0, None, ALU.mult)
                ins.then_inc(S("scores_ready"), t.made("scores_ready"))

            def normalise(n):
                g, i = TILES[n]
                dve.wait_ge(S("probs_made"), t.next("probs_made"))
                if g != 3:
                    return
                r = SUM[:, 4 * (n % 4):4 * (n % 4) + 4]
                nc.vector.reciprocal(r, r).then_inc(S("dve_step"), t.made("dve_step"))
                dve.wait_ge(S("dve_step"), t.last("dve_step"))
                s = sbuf(n)
                nc.vector.tensor_tensor(s, s, r.unsqueeze(2).broadcast_to([128, 4, 256]), ALU.mult).then_inc(S("probs_normal"), t.made("probs_normal"))

            dve.wait_ge(S("bias_in"), 16)
            for n in range(len(TILES)):
                scores(n)
                if n >= 1:
                    normalise(n - 1)
            normalise(len(TILES) - 1)

            dve.wait_ge(S("mix_kept"), t.next("mix_kept", len(TILES)))
            for n in range(6):
                dve.wait_ge(S("stat_turned"), t.next("stat_turned"))
                g = n % 3
                src, dst = PS[0:4, 4 + n % 2, :], ROWS[:, n, :]
                if g:
                    src = src.rearrange("p (r u) -> p r u", r=ORDER[g])
                    dst = dst.rearrange("p (u r) -> p r u", r=ORDER[g])
                nc.vector.tensor_copy(dst, src).then_inc(S("stat_kept"), t.made("stat_kept"))
            dve.wait_ge(S("stat_kept"), t.last("stat_kept"))
            top_row = SQ[0:4, 0, :]
            nc.vector.tensor_tensor(top_row, ROWS[:, 0, :], ROWS[:, 1, :], ALU.max).then_inc(S("dve_step"), t.made("dve_step"))
            dve.wait_ge(S("dve_step"), t.last("dve_step"))
            nc.vector.tensor_tensor(top_row, top_row, ROWS[:, 2, :], ALU.max).then_inc(S("dve_step"), t.made("dve_step"))
            dve.wait_ge(S("dve_step"), t.last("dve_step"))
            for g in range(3):
                ins = nc.vector.tensor_tensor(ROWS[:, g, :], ROWS[:, g, :], top_row, ALU.subtract)
            ins.then_inc(S("row_max_ready"), t.made("row_max_ready"))
            dve.wait_ge(S("row_exp"), t.next("row_exp"))
            for g in range(3):
                nc.vector.tensor_tensor(ROWS[:, 3 + g, :], ROWS[:, 3 + g, :], ROWS[:, g, :], ALU.mult).then_inc(S("dve_step"), t.made("dve_step"))
                dve.wait_ge(S("dve_step"), t.last("dve_step"))
            nc.vector.tensor_tensor(top_row, ROWS[:, 3, :], ROWS[:, 4, :], ALU.add).then_inc(S("dve_step"), t.made("dve_step"))
            dve.wait_ge(S("dve_step"), t.last("dve_step"))
            nc.vector.tensor_tensor(top_row, top_row, ROWS[:, 5, :], ALU.add).then_inc(S("dve_step"), t.made("dve_step"))
            dve.wait_ge(S("dve_step"), t.last("dve_step"))
            nc.vector.reciprocal(top_row, top_row).then_inc(S("dve_step"), t.made("dve_step"))
            dve.wait_ge(S("dve_step"), t.last("dve_step"))
            for g in range(3):
                ins = nc.vector.tensor_tensor(ROWS[:, g, :], ROWS[:, g, :], top_row, ALU.mult)
                ins.then_inc(S("row_weight"), t.made("row_weight"))

            def y_lo(dst, hi):
                dve.wait_ge(S("y_hi_made"), t.next("y_hi_made"))
                nc.vector.tensor_tensor(dst, TMP[:, 2 + (t.n["y_hi_made"] - 1) % 2, :], hi.bitcast(F32),
                                        ALU.subtract).then_inc(S("y_lo_made"), t.made("y_lo_made"))

            def ytmp():
                return TMP[:, 2 + t.n.get("y_made", 0) % 2, :]

            for c in range(DC):
                u = ("gate", c)
                unit(u)
                ins = nc.vector.tensor_tensor(TMP[:, c % 2, :], PS[:, bank(u), :], RB[:, :], ALU.mult)
                ins.then_inc(S("pre"), t.made("pre"))
                free_after("pre", u)
                if c < 6:
                    dve.wait_ge(S("weight_spread"), t.next("weight_spread"))
                    nc.vector.tensor_tensor(ytmp(), MIXT[:, c, :], PS[:, 4 + c % 2, :], ALU.mult).then_inc(S("weight_used"), t.made("weight_used"))
                    dve.wait_ge(S("weight_used"), t.last("weight_used"))
                    dve.wait_ge(S("gate_made"), t.next("gate_made"))
                    nc.vector.tensor_tensor(ytmp(), ytmp(), TMP[:, c % 2, :], ALU.mult).then_inc(S("y_made"), t.made("y_made"))
                else:
                    dve.wait_ge(S("gate_made"), t.next("gate_made"))
                    nc.vector.tensor_tensor(ytmp(), MIXT[:, c, :], TMP[:, c % 2, :], ALU.mult).then_inc(S("y_made"), t.made("y_made"))
                dve.wait_ge(S("y_made"), t.last("y_made"))
                y_lo(YL[:, c, :], YH[:, c, :])

            def residual(names, gain):
                for c in range(DC + 1):
                    if c < DC:
                        u = names(c)
                        unit(u)
                        nc.vector.tensor_tensor(X[:, c, :], X[:, c, :], PS[:, bank(u), :], ALU.add).then_inc(S("x_final"), t.made("x_final"))
                        free_after("x_final", u)
                    if c > 0:
                        norm_chunk(c - 1, gain)

            def norm_chunk(c, gain, hi=XH, lo=XL):
                sum_squares(c)
                if gain is not None:
                    lo_part(c, lo[:, c, :], X[:, c, :], col(gain[0], gain[1] + c), hi[:, c, :])

            residual(lambda c: ("out", c), None)
            norm_rows()
            for c in range(DC):
                ins = nc.vector.scalar_tensor_tensor(X[:, c, :], X[:, c, :], col("final_g", c), RB[:, :],
                                                     ALU.mult, ALU.mult)
                ins.then_inc(S("x_final"), t.made("x_final"))
            for c in range(DC):
                norm_chunk(c, ("g_mix", 0))
            norm_rows()
            for c in range(4):
                u = ("cc", c)
                unit(u)
                nc.vector.tensor_tensor(TMP[:, 0, :], PS[:, bank(u), :], RB[:, :], ALU.mult).then_inc(S("dve_step"), t.made("dve_step"))
                dve.wait_ge(S("dve_step"), t.last("dve_step"))
                free_after("dve_step", u)
                u = ("cx", c)
                unit(u)
                nc.vector.tensor_tensor(TMP[:, 1, :], PS[:, bank(u), :], RB[:, :], ALU.mult).then_inc(S("dve_step"), t.made("dve_step"))
                dve.wait_ge(S("dve_step"), t.last("dve_step"))
                free_after("dve_step", u)
                nc.vector.tensor_tensor(TMP[:, 0, :], TMP[:, 0, :], TMP[:, 1, :], ALU.mult).then_inc(S("dve_step"), t.made("dve_step"))
                dve.wait_ge(S("dve_step"), t.last("dve_step"))
                nc.vector.tensor_scalar(TMP[:, 1, :], TMP[:, 0, :], col("conv", 8 + c), None, ALU.mult).then_inc(S("dve_step"), t.made("dve_step"))
                dve.wait_ge(S("dve_step"), t.last("dve_step"))
                for tap in (1, 0):
                    d = 2 - tap
                    nc.vector.scalar_tensor_tensor(TMP[:, 1, d:T], TMP[:, 0, 0:T - d], col("conv", 4 * tap + c),
                                                   TMP[:, 1, d:T], ALU.mult, ALU.add).then_inc(S("dve_step"), t.made("dve_step"))
                    dve.wait_ge(S("dve_step"), t.last("dve_step"))
                u = ("cb", c)
                unit(u)
                nc.vector.tensor_tensor(TMP[:, 0, :], PS[:, bank(u), :], RB[:, :], ALU.mult).then_inc(S("dve_step"), t.made("dve_step"))
                dve.wait_ge(S("dve_step"), t.last("dve_step"))
                free_after("dve_step", u)
                nc.vector.tensor_tensor(ytmp(), TMP[:, 0, :], TMP[:, 1, :], ALU.mult).then_inc(S("y_made"), t.made("y_made"))
                if c == 0:
                    dve.wait_ge(S("cols_summed"), t.next("cols_summed"))
                    nc.vector.tensor_copy(RC[:, 0:4], PS[:, 7, 0:4]).then_inc(S("cols_made"), t.made("cols_made"))
                y_lo(YL[:, c, :], YH[:, c, :])
            dve.wait_ge(S("ws_in"), 16)
            nc.vector.tensor_tensor(WS[:, :, :], WS[:, :, :],
                                    const("upto", at=384).unsqueeze(1).broadcast_to([128, 8, 128]), ALU.mult).then_inc(S("ws_masked"), t.made("ws_masked"))
            for i in range(QT):
                for g in range(2):
                    dve.wait_ge(acc_free[bank(("gv", g), i)], freed(("gv", g), i))
                nc.vector.tensor_tensor(SV[:, :], GV[:, i, :], GV[:, i, :], ALU.mult).then_inc(S("dve_step"), t.made("dve_step"))
                dve.wait_ge(S("dve_step"), t.last("dve_step"))
                ins = nc.vector.tensor_reduce(SS[:, i, :], SV[:, :].rearrange("p (h d) -> p h d", h=8), AX.X, ALU.add)
                if i < QT - 1:
                    ins.then_inc(S("dve_step"), t.made("dve_step"))
                    dve.wait_ge(S("dve_step"), t.last("dve_step"))
                else:
                    ins.then_inc(S("gv_summed"), t.made("gv_summed"))
            dve.wait_ge(S("gv_rstd_made"), t.next("gv_rstd_made"))
            dve.wait_ge(S("gv_in"), 16)
            for i in range(QT):
                v = GV[:, i, :].rearrange("p (h d) -> p h d", h=8)
                nc.vector.tensor_tensor(v, v, SS[:, i, :].unsqueeze(2).broadcast_to([128, 8, 64]), ALU.mult).then_inc(S("dve_step"), t.made("dve_step"))
                dve.wait_ge(S("dve_step"), t.last("dve_step"))
                nc.vector.tensor_tensor(GV[:, i, :], GV[:, i, :], GVB[:, :], ALU.mult).then_inc(S("gv_normed"), t.made("gv_normed"))
            dve.wait_ge(S("bs_in"), 16)
            for c in range(4):
                dve.wait_ge(S("spatial_done"), t.next("spatial_done"))
                m = MB[:, c, :].rearrange("p (n k) -> p n k", n=QT)
                nc.vector.tensor_tensor(m, PS[:, 4 + c, :].rearrange("p (n k) -> p n k", n=QT),
                                        BS[:, c, :].unsqueeze(1).broadcast_to([128, QT, 128]), ALU.add).then_inc(S("dve_step"), t.made("dve_step"))
            for c in range(4):
                u = ("gu", c)
                unit(u)
                nc.vector.tensor_tensor(TMP[:, c % 2, :], PS[:, bank(u), :], RB[:, :], ALU.mult).then_inc(S("pre"), t.made("pre"))
                free_after("pre", u)
                dve.wait_ge(S("gate_made"), t.next("gate_made"))
                nc.vector.tensor_tensor(ytmp(), TMP[:, c % 2, :], MB[:, c, :], ALU.mult).then_inc(S("y_made"), t.made("y_made"))
                dve.wait_ge(S("y_made"), t.last("y_made"))
                y_lo(YL[:, 4 + c, :], YH[:, 4 + c, :])
            residual(lambda c: ("mixout", 0, c), ("g_ffn", 0))

            def feed_forward(layer):
                norm_rows()
                for n, (f0, fn) in enumerate(PASS):
                    for f in range(f0, f0 + fn):
                        u = ("fg", layer, f)
                        unit(u)
                        nc.vector.tensor_tensor(TMP[:, f % 2, :], PS[:, bank(u), :], RB[:, :], ALU.mult).then_inc(S("pre"), t.made("pre"))
                        free_after("pre", u)
                        u = ("fu", layer, f)
                        unit(u)
                        nc.vector.tensor_tensor(ytmp(), PS[:, bank(u), :], RB[:, :], ALU.mult).then_inc(S("dve_step"), t.made("dve_step"))
                        dve.wait_ge(S("dve_step"), t.last("dve_step"))
                        free_after("dve_step", u)
                        dve.wait_ge(S("gate_made"), t.next("gate_made"))
                        nc.vector.tensor_tensor(ytmp(), ytmp(), TMP[:, f % 2, :], ALU.mult).then_inc(S("y_made"), t.made("y_made"))
                        dve.wait_ge(S("y_made"), t.last("y_made"))
                        y_lo(YL[:, f - f0, :], YH[:, f - f0, :])
                    if n < len(PASS) - 1:
                        for c in range(DC):
                            u = ("fd", layer, n, c)
                            unit(u)
                            nc.vector.tensor_tensor(X[:, c, :], X[:, c, :], PS[:, bank(u), :], ALU.add).then_inc(S("dve_step"), t.made("dve_step"))
                            dve.wait_ge(S("dve_step"), t.last("dve_step"))
                            free_after("dve_step", u)
                residual(lambda c: ("fd", layer, len(PASS) - 1, c), ("g_ple", DC * layer))

            def embed(layer):
                for c in range(2):
                    dve.wait_ge(S("ple_hi_made"), t.next("ple_hi_made"))
                    nc.vector.tensor_tensor(PL[:, c, :], PR[:, c, :], PH[:, c, :].bitcast(F32), ALU.subtract).then_inc(S("ple_lo_made"), t.made("ple_lo_made"))
                norm_rows()
                for c in range(DC):
                    u = ("pg", layer, c)
                    unit(u)
                    nc.vector.tensor_tensor(TMP[:, c % 2, :], PS[:, bank(u), :], RB[:, :], ALU.mult).then_inc(S("pre"), t.made("pre"))
                    free_after("pre", u)
                    u = ("pp", layer, c)
                    unit(u)
                    dve.wait_ge(S("gate_made"), t.next("gate_made"))
                    nc.vector.tensor_tensor(TMP[:, c % 2, :], TMP[:, c % 2, :], PS[:, bank(u), :], ALU.mult).then_inc(S("dve_step"), t.made("dve_step"))
                    dve.wait_ge(S("dve_step"), t.last("dve_step"))
                    free_after("dve_step", u)
                    nc.vector.tensor_tensor(X[:, c, :], X[:, c, :], TMP[:, c % 2, :], ALU.add).then_inc(S("x_final"), t.made("x_final"))
                    if layer == 0 and c:
                        norm_chunk(c - 1, ("g_mix", DC), YH, YL)

            feed_forward(0)
            embed(0)
            norm_chunk(DC - 1, ("g_mix", DC), YH, YL)
            norm_rows()
            dve.wait_ge(S("pos_in"), 16)
            nc.vector.tensor_copy(TMP[:, 2, :], POS[:, :]).then_inc(S("dve_step"), t.made("dve_step"))
            dve.wait_ge(S("dve_step"), t.last("dve_step"))
            nc.vector.tensor_scalar(TMP[:, 3, :], TMP[:, 2, :], col("inv_freq"), None, ALU.mult).then_inc(S("dve_step"), t.made("dve_step"))
            dve.wait_ge(S("dve_step"), t.last("dve_step"))
            nc.vector.tensor_scalar(TMP[:, 2, :], TMP[:, 3, :], float(1 / (2 * np.pi)), ROUND, ALU.mult, ALU.add).then_inc(S("dve_step"), t.made("dve_step"))
            dve.wait_ge(S("dve_step"), t.last("dve_step"))
            nc.vector.tensor_scalar(TMP[:, 2, :], TMP[:, 2, :], ROUND, None, ALU.subtract).then_inc(S("dve_step"), t.made("dve_step"))
            dve.wait_ge(S("dve_step"), t.last("dve_step"))
            for part in TWO_PI:
                nc.vector.scalar_tensor_tensor(TMP[:, 3, :], TMP[:, 2, :], -part, TMP[:, 3, :], ALU.mult, ALU.add).then_inc(S("dve_step"), t.made("dve_step"))
                dve.wait_ge(S("dve_step"), t.last("dve_step"))
            nc.vector.tensor_scalar(TMP[:, 3, :], TMP[:, 3, :], PI_BELOW, -PI_BELOW, ALU.min, ALU.max).then_inc(S("angle_made"), t.made("angle_made"))

            def latent(c):
                u = ("ql", c) if c < 3 else ("kvl", c - 3)
                unit(u)
                nc.vector.tensor_tensor(LAT[:, c, :], PS[:, bank(u), :], RB[:, :], ALU.mult).then_inc(S("lat_made"), t.made("lat_made"))
                free_after("lat_made", u)

            def latent_norm(chunks, gain):
                dve.wait_ge(S("lat_rstd_made"), t.next("lat_rstd_made"))
                for n, c in enumerate(chunks):
                    nc.vector.scalar_tensor_tensor(LAT[:, c, :], LAT[:, c, :], col(gain, n), STD[:, :],
                                                   ALU.mult, ALU.mult).then_inc(S("lat_normed"), t.made("lat_normed"))
                dve.wait_ge(S("lat_normed"), t.last("lat_normed"))

            latent(0)
            latent(1)
            sum_squares(0)
            latent(2)
            sum_squares(1)
            sum_squares(2)
            latent(3)
            latent(4)
            latent_norm(range(3), "g_qa")
            sum_squares(3, first=3)
            sum_squares(4, first=3)
            u = ("small", 0)
            unit(u)
            nc.vector.tensor_tensor(SMALL[:, :], PS[:, bank(u), :], RB[:, :], ALU.mult).then_inc(S("head_raw"), t.made("head_raw"))
            free_after("head_raw", u)
            nc.vector.tensor_scalar(GR[:, 0, :], SMALL[32:36, :], col("b_i", rows=slice(32, 36)), None, ALU.add).then_inc(S("dve_step"), t.made("dve_step"))
            nc.vector.tensor_scalar(GR[:, 1, :], SMALL[64:68, :], col("b_f", rows=slice(64, 68)), None, ALU.add).then_inc(S("gate_rows_made"), t.made("gate_rows_made"))
            latent_norm(range(3, 5), "g_kva")
            for k, dst in (("mq", MQ), ("mk", MK)):
                for c in range(2):
                    unit((k, c))
                    free(nc.vector.tensor_tensor(dst[:, c, :], PS[:, bank((k, c)), :], RB[:, :], ALU.mult), (k, c))
            dve.wait_ge(S("cols_summed"), t.next("cols_summed"))
            nc.vector.tensor_copy(RC[:, 0:4], PS[:, 7, 0:4]).then_inc(S("cols_made"), t.made("cols_made"))
            for c in range(5):
                dve.wait_ge(S("lat_hi_made"), t.next("lat_hi_made"))
                nc.vector.tensor_tensor(LL[:, c, :], LAT[:, c, :], LH[:, c, :].bitcast(F32), ALU.subtract).then_inc(S("lat_lo_made"), t.made("lat_lo_made"))

            def head_raw(m):
                u, c, _, _ = HEADS[m]
                unit((u, c))
                if m >= 2:
                    dve.wait_ge(S("head_taken"), t.last("head_taken"))
                nc.vector.tensor_copy(TMP[:, m % 2, :], PS[:, bank((u, c)), :]).then_inc(S("head_raw"), t.made("head_raw"))
                free_after("head_raw", (u, c))

            def head_finish(m):
                u, c, rows, gain = HEADS[m]
                r = 32 if m == 0 else 128
                raw = SMALL[0:32, :] if m == 0 else TMP[:, m % 2, :]
                inv = SQ[0:r, m % 2, :]
                dve.wait_ge(S("head_rstd_made"), t.next("head_rstd_made"))
                if rows == 64:
                    dst = QF if u == "qn" else KF
                    for par in range(2):
                        h = slice(64 * par, 64 * par + 64)
                        ins = nc.vector.scalar_tensor_tensor(dst[0:64, 2 * c + par, :], raw[h, :], col(gain, rows=h),
                                                             SQ[h, m % 2, :], ALU.mult, ALU.mult)
                        name = "head_taken" if par else "dve_step"
                        ins.then_inc(S(name), t.made(name))
                    return
                if m:
                    if c == 0:
                        dve.wait_ge(S("kr_kept"), t.next("kr_kept"))
                nc.vector.scalar_tensor_tensor(TMP[0:r, 2, :], raw, col(gain, rows=slice(0, r)), inv,
                                               ALU.mult, ALU.mult).then_inc(S("rope_in"), t.made("rope_in"))
                dve.wait_ge(S("rot_done"), t.next("rot_done"))
                if m == 0:
                    dve.wait_ge(S("rotary_made"), t.next("rotary_made"))
                nc.vector.tensor_tensor(TMP[0:r, 3, :], PS[0:r, 7, :], SIN[0:r, :], ALU.mult).then_inc(S("dve_step"), t.made("dve_step"))
                dve.wait_ge(S("dve_step"), t.last("dve_step"))
                nc.vector.tensor_tensor(TMP[0:r, 2, :], TMP[0:r, 2, :], COS[0:r, :], ALU.mult).then_inc(S("dve_step"), t.made("dve_step"))
                dve.wait_ge(S("dve_step"), t.last("dve_step"))
                if m == 0:
                    nc.vector.tensor_tensor(TMP[0:32, 2, :], TMP[0:32, 2, :], TMP[0:32, 3, :], ALU.add).then_inc(S("kr_made"), t.made("kr_made"))
                    dve.wait_ge(S("kr_made"), t.last("kr_made"))
                    t.n["head_taken"] = 1
                    dve.sem_inc(S("head_taken"), 1)
                    return
                for k in range(4):
                    h = slice(32 * k, 32 * k + 32)
                    ins = nc.vector.tensor_tensor(QF[64:96, 4 * c + k, :], TMP[h, 2, :], TMP[h, 3, :], ALU.add)
                    name = "head_taken" if k == 3 else "dve_step"
                    ins.then_inc(S(name), t.made(name))
                dve.wait_ge(S("head_taken"), t.last("head_taken"))

            for m in range(len(HEADS)):
                if m:
                    head_raw(m)
                    head_finish(m - 1)
            head_finish(len(HEADS) - 1)
            dve.wait_ge(S("head_taken"), t.last("head_taken"))
            def rows_a():
                dve.wait_ge(S("softplus_made"), t.next("softplus_made"))
                nc.vector.scalar_tensor_tensor(F_ROW, F_ROW, 0.0, G_ROW, ALU.min, ALU.subtract).then_inc(S("lf_made"), t.made("lf_made"))

            def rows_b():
                dve.wait_ge(S("lf_turned"), t.next("lf_turned"))
                nc.vector.tensor_copy(LFC[:, 0, :, :], PS[:, 4, 0:16]).then_inc(S("lf_cols"), t.made("lf_cols"))

            def rows_c():
                dve.wait_ge(S("a_summed"), t.next("a_summed"))
                nc.vector.tensor_copy(A_ROW, PS[0:4, 5, :]).then_inc(S("dve_step"), t.made("dve_step"))
                dve.wait_ge(S("dve_step"), t.last("dve_step"))
                nc.vector.tensor_tensor(I_ROW, I_ROW, A_ROW, ALU.subtract).then_inc(S("b_made"), t.made("b_made"))
                dve.wait_ge(S("b_made"), t.last("b_made"))
                nc.vector.tensor_scalar(MAX_ROWS[0], I_ROW, 0.0, None, ALU.max).then_inc(S("dve_step"), t.made("dve_step"))
                dve.wait_ge(S("dve_step"), t.last("dve_step"))
                n, d = 0, 1
                while d < T:
                    src, dst = MAX_ROWS[n % 2], MAX_ROWS[1 - n % 2]
                    nc.vector.tensor_copy(dst[:, 0:d], src[:, 0:d]).then_inc(S("dve_step"), t.made("dve_step"))
                    nc.vector.tensor_tensor(dst[:, d:T], src[:, d:T], src[:, 0:T - d], ALU.max).then_inc(S("dve_step"), t.made("dve_step"))
                    dve.wait_ge(S("dve_step"), t.last("dve_step"))
                    n, d = n + 1, 2 * d
                nc.vector.tensor_scalar(G_ROW, MAX_ROWS[n % 2], -1.0, None, ALU.mult).then_inc(S("dve_step"), t.made("dve_step"))
                nc.vector.tensor_tensor(F_ROW, A_ROW, MAX_ROWS[n % 2], ALU.add).then_inc(S("rows_made"), t.made("rows_made"))

            def rows_d():
                dve.wait_ge(S("b_turned"), t.next("b_turned"))
                nc.vector.tensor_copy(LFC[:, 1, :, :], PS[:, 6, 0:16]).then_inc(S("b_cols"), t.made("b_cols"))
                dve.wait_ge(S("b_cols"), t.last("b_cols"))

            rows_a()
            for c, rows in enumerate((rows_b, rows_c, None, rows_d)):
                u = ("mo", c)
                unit(u)
                if c >= 2:
                    dve.wait_ge(S("gate_made"), t.next("gate_made"))
                nc.vector.tensor_tensor(TMP[:, c % 2, :], PS[:, bank(u), :], RB[:, :], ALU.mult).then_inc(S("pre"), t.made("pre"))
                free_after("pre", u)
                if rows is not None:
                    rows()
            dve.wait_ge(S("gate_made"), t.next("gate_made", 2))

            def d_max(n):
                h, i = DTILES[n]
                w = 128 * (i + 1)
                dve.wait_ge(S("d_scored"), t.next("d_scored"))
                s = PS[:, SBANK[n % 4], :]
                nc.vector.tensor_tensor(s[:, w - 128:w], s[:, w - 128:w], const("causal"), ALU.add).then_inc(S("dve_step"), t.made("dve_step"))
                dve.wait_ge(S("dve_step"), t.last("dve_step"))
                nc.vector.tensor_reduce(NEGM[:, n % 4:n % 4 + 1], s[:, 0:w], AX.X, ALU.max, negate=True).then_inc(S("dve_step"), t.made("dve_step"))
                dve.wait_ge(S("dve_step"), t.last("dve_step"))
                nc.vector.tensor_scalar(NEGM[:, n % 4:n % 4 + 1], NEGM[:, n % 4:n % 4 + 1], DSCALE, None, ALU.mult).then_inc(S("d_max_ready"), t.made("d_max_ready"))

            def d_norm(n):
                h, i = DTILES[n]
                w = 128 * (i + 1)
                dve.wait_ge(S("d_exp_made"), t.next("d_exp_made"))
                r = SUM[:, n % 4:n % 4 + 1]
                nc.vector.reciprocal(r, r).then_inc(S("dve_step"), t.made("dve_step"))
                dve.wait_ge(S("dve_step"), t.last("dve_step"))
                nc.vector.tensor_scalar(PD[:, n % 4, 0:w], PD[:, n % 4, 0:w], r, None, ALU.mult).then_inc(S("d_probs_made"), t.made("d_probs_made"))

            def d_lo(c):
                dve.wait_ge(S("y_hi_made"), t.next("y_hi_made"))
                nc.vector.tensor_tensor(YL[:, c, :], PS[:, 2 + c % 2, :], YH[:, c, :].bitcast(F32), ALU.subtract).then_inc(S("y_lo_made"), t.made("y_lo_made"))

            for n in range(len(DTILES)):
                d_max(n)
                if n >= 2:
                    d_norm(n - 2)
                if n % 8 == 6 and n > 6:
                    d_lo(n // 8 - 1)
            d_norm(len(DTILES) - 2)
            d_norm(len(DTILES) - 1)
            d_lo(3)

            def decay(k):
                h, b = k // 4, k % 4
                w = T - 128 * b
                if b == 0:
                    dve.wait_ge(S("g_spread"), t.next("g_spread"))
                nc.vector.tensor_scalar(WT[:, k % 4, 0:w], PS[:, M_G, 128 * b:T], LFC[:, 1, b, h:h + 1], 0.0,
                                        ALU.add, ALU.min).then_inc(S("decay_pre"), t.made("decay_pre"))

            def weigh(k):
                w = T - 128 * (k % 4)
                dve.wait_ge(S("decay_made"), t.next("decay_made"))
                nc.vector.tensor_tensor(WT[:, k % 4, 0:128], WT[:, k % 4, 0:128], const("upto", at=384), ALU.mult).then_inc(S("dve_step"), t.made("dve_step"))
                dve.wait_ge(S("dve_step"), t.last("dve_step"))
                dve.wait_ge(S("m_scored"), t.next("m_scored"))
                if k >= 4:
                    dve.wait_ge(S("m_added"), t.next("m_added"))
                nc.vector.scalar_tensor_tensor(SW[:, k % 4, 0:w], PS[:, M_S[k % 3], 0:w], 0.125, WT[:, k % 4, 0:w],
                                               ALU.mult, ALU.mult).then_inc(S("weighted_made"), t.made("weighted_made"))
                dve.wait_ge(S("weighted_made"), t.last("weighted_made"))

            def divide(h):
                dve.wait_ge(S("den_abs"), t.next("den_abs"))
                nc.vector.tensor_tensor(TMP[:, 0, :], TMP[:, 0, :], PS[:, M_FLOOR, :], ALU.max).then_inc(S("dve_step"), t.made("dve_step"))
                dve.wait_ge(S("dve_step"), t.last("dve_step"))
                nc.vector.reciprocal(TMP[:, 0, :], TMP[:, 0, :]).then_inc(S("dve_step"), t.made("dve_step"))
                dve.wait_ge(S("dve_step"), t.last("dve_step"))
                nc.vector.tensor_tensor(HT[:, h, :], PS[:, M_NUM[h % 2], :], TMP[:, 0, :], ALU.mult).then_inc(S("h_made"), t.made("h_made"))

            for k in range(16):
                decay(k)
                if k >= 2:
                    weigh(k - 2)
                if k % 4 == 3 and k > 4:
                    divide(k // 4 - 1)
            weigh(14)
            weigh(15)
            divide(3)
            dve.wait_ge(S("h_made"), t.last("h_made"))
            for h in range(4):
                dve.wait_ge(S("h_rstd_made"), t.next("h_rstd_made"))
                inv = SQ[:, h % 2, :]
                nc.vector.scalar_tensor_tensor(HT[:, h, :], HT[:, h, :], col("g_mh", h), inv, ALU.mult, ALU.mult).then_inc(S("dve_step"), t.made("dve_step"))
                dve.wait_ge(S("dve_step"), t.last("dve_step"))
                nc.vector.tensor_tensor(ytmp(), HT[:, h, :], MO[:, h, :], ALU.mult).then_inc(S("y_made"), t.made("y_made"))
                dve.wait_ge(S("y_made"), t.last("y_made"))
                y_lo(YL[:, 4 + h, :], YH[:, 4 + h, :])
            residual(lambda c: ("mixout", 1, c), ("g_ffn", DC))
            feed_forward(1)
            embed(1)

        @block.tensor
        def _(pe):
            t = Tally()
            uses = {}

            def take(b):
                if uses.get(b, 0):
                    pe.wait_ge(acc_free[b], uses[b])
                uses[b] = uses.get(b, 0) + 1

            def idle(b):
                pe.wait_ge(acc_free[b], uses[b])

            PASSES = ((WH, 0), (WL, 0), (WH, 1))

            def feature(u, parts, n=T, ready=None):
                d = units[u]
                (blk, _, kc), b = d["blocks"][0], bank(u)
                take(b)
                pe.wait_ge(S("lo_done"), blk + 1)
                for k in range(kc):
                    if ready is not None:
                        pe.wait_ge(S(ready), t.next(ready))
                    for p, (w, a) in enumerate(PASSES):
                        ins = nc.tensor.matmul(PS[:, b, 0:n], w[:, blk % HL, 128 * k:128 * k + 128], parts[a][:, k, 0:n],
                                               start=(k == 0 and p == 0), stop=(k == kc - 1 and p == len(PASSES) - 1))
                ins.then_inc(S("block_used"), t.made("block_used"))

            def token(u, parts, order):
                d = units[u]
                kc = sum(n for _, _, n in d["blocks"])
                for i in range(d["tiles"]):
                    take(bank(u, i))
                for blk, k0, n in d["blocks"]:
                    pe.wait_ge(S("lo_done"), blk + 1)
                    for i in range(d["tiles"]):
                        for k in range(k0, k0 + n):
                            for p, (w, a) in enumerate(PASSES):
                                ins = nc.tensor.matmul(PS[:, bank(u, i), 0:256], order(parts[a][:, k, :], i),
                                                       w[:, blk % HL, 256 * (k - k0):256 * (k - k0) + 256],
                                                       start=(k == 0 and p == 0), stop=(k == kc - 1 and p == len(PASSES) - 1))
                    ins.then_inc(S("block_used"), t.made("block_used"))

            def norm_sum(n=T, chunks=DC):
                pe.wait_ge(S("sq_taken"), t.next("sq_taken", chunks))
                nc.tensor.matmul(PS[:, 4, 0:n], const("ones"), SSQ[:, 0:n], start=True, stop=True).then_inc(S("ssum_done"), t.made("ssum_done"))

            pe.wait_ge(S("const_in"), 16)
            feature(("km", 0), (MH, ML), NMEM, "xg_lo_made")
            norm_sum(NMEM)
            feature(("km", 1), (MH, ML), NMEM)
            token(("vm", 0), (MH, ML), lambda ap, i: ap[:, 128 * i:128 * i + 128])
            pe.wait_ge(S("rstd_made"), t.next("rstd_made"))
            for i in range(2):
                ins = nc.tensor.matmul(PS[:, 7, 12 + i:13 + i], RBM[:, 128 * i:128 * i + 128], const("ident", n=1), start=True, stop=True)
            ins.then_inc(S("cols_summed"), t.made("cols_summed"))
            feature(("q", 0), (XH, XL), ready="xg_lo_made")
            norm_sum()
            for c in range(1, 6):
                feature(("q", c), (XH, XL))
            pe.wait_ge(S("rstd_made"), t.next("rstd_made"))
            pe.wait_ge(S("cols_made"), t.next("cols_made"))
            for g in range(3):
                for i in range(QT):
                    ins = nc.tensor.matmul(PS[:, 7, 4 * g + i:4 * g + i + 1], tile_tokens(RB[:, :], g, i), const("ident", n=1),
                                           start=True, stop=True)
            ins.then_inc(S("cols_summed"), t.made("cols_summed"))
            for c in range(6):
                feature(("k", c), (XH, XL))
            for g in range(3):
                token(("v", g), (XH, XL), lambda ap, i, g=g: tile_tokens(ap, g, i))
            for c in range(2):
                feature(("qm", c), (XH, XL))

            def score(n):
                g, i = TILES[n]
                w, k0 = keys(g, i)
                if n == 0:
                    pe.wait_ge(S("qk_ready"), t.next("qk_ready", 2))
                elif n == 1:
                    idle(0)
                    idle(1)
                else:
                    pe.wait_ge(S("scores_ready"), t.next("scores_ready"))
                for par in range(2):
                    for hh in range(2):
                        r = slice(64 * par, 64 * par + 64)
                        if g == 3:
                            q, k = QM[r, hh, 128 * i:128 * i + 128], KM[r, hh, :]
                        else:
                            q, k = Q[r, 2 * g + hh, 128 * i:128 * i + 128], K[r, 2 * g + hh, k0:k0 + w]
                        ins = nc.tensor.matmul(PS[:, SPAIR[n % 2] + par, w * hh:w * hh + w], q, k, start=True, stop=True)
                ins.then_inc(S("scored"), t.made("scored"))

            def turn(n):
                g, i = TILES[n]
                w, _ = keys(g, i)
                nb = w // 128
                if g == 3:
                    pe.wait_ge(S("probs_normal"), t.next("probs_normal"))
                pe.wait_ge(S("probs_made"), t.next("probs_made"))
                blocks_ = [(j, kb) for j in range(4) for kb in range(nb)]
                for half in range(nb):
                    k = t.n.get("turned", 0)
                    if k >= 2:
                        pe.wait_ge(S("turned_kept"), k - 1)
                    for q in range(4):
                        j, kb = blocks_[4 * half + q]
                        ins = nc.tensor.transpose(PS[:, 6 + k % 2, 128 * q:128 * q + 128],
                                                  sbuf(n)[:, j, 128 * kb:128 * kb + 128], const("ident"))
                    ins.then_inc(S("turned"), t.made("turned"))
                return blocks_

            def values(n):
                g, i = TILES[n]
                nb = keys(g, i)[0] // 128
                pe.wait_ge(S("turned_kept"), TURNED[n])
                if n < 2:
                    idle(2 + n)
                else:
                    pe.wait_ge(S("mix_kept"), t.next("mix_kept"))
                for j in range(4):
                    par, hh = j // 2, j % 2
                    h = 2 * hh + par
                    for kb in range(nb):
                        if g == 3:
                            v = VM[:, kb, 64 * h:64 * h + 64]
                        elif g == 0 and i:
                            v = V[:, 0, i - 1 + kb, 64 * h:64 * h + 64]
                        else:
                            v = V[:, g, i, 64 * h:64 * h + 64]
                        ins = nc.tensor.matmul(PS[64 * par:64 * par + 64, 2 + n % 2, 128 * hh:128 * hh + 128], v, PT[:, n % 2, nb * j + kb, :],
                                               start=(kb == 0), stop=(kb == nb - 1))
                ins.then_inc(S("mixed"), t.made("mixed"))

            score(0)
            score(1)
            for n in range(len(TILES)):
                if n + 2 < len(TILES):
                    score(n + 2)
                turn(n)
                if n:
                    values(n - 1)
            values(len(TILES) - 1)
            pe.wait_ge(S("scores_ready"), t.next("scores_ready", 2))
            pe.wait_ge(S("mix_kept"), t.next("mix_kept", 2))
            for n in range(6):
                kind, g = n // 3, n % 3
                if n >= 2:
                    pe.wait_ge(S("stat_kept"), t.next("stat_kept"))
                for i in range(QT):
                    ins = nc.tensor.transpose(PS[0:4, 4 + n % 2, 128 * i:128 * i + 128], STAT[:, g, i, :, kind], const("ident"))
                ins.then_inc(S("stat_turned"), t.made("stat_turned"))

            def spread(c):
                if c == 0:
                    pe.wait_ge(S("row_weight"), t.next("row_weight", 3))
                if c >= 2:
                    pe.wait_ge(S("weight_used"), t.next("weight_used"))
                nc.tensor.matmul(PS[:, 4 + c % 2, :], const("pair", rows=4, at=128 * (c % 2)), ROWS[:, c // 2, :],
                                 start=True, stop=True).then_inc(S("weight_spread"), t.made("weight_spread"))

            for c in range(DC):
                feature(("gate", c), (XH, XL))
                if 2 <= c:
                    spread(c - 2)
            for c in range(DC):
                feature(("out", c), (YH, YL), ready="y_lo_made" if c == 0 else None)
            norm_sum()
            xg = (XH, XL)
            feature(("cc", 0), xg, ready="xg_lo_made")
            norm_sum()
            for c in range(4):
                for k in ("cc", "cx", "cb"):
                    if (k, c) != ("cc", 0):
                        feature((k, c), xg)
                if c == 0:
                    pe.wait_ge(S("rstd_made"), t.next("rstd_made", 2))
                    for i in range(QT):
                        ins = nc.tensor.matmul(PS[:, 7, i:i + 1], RB[:, 128 * i:128 * i + 128], const("ident", n=1),
                                               start=True, stop=True)
                    ins.then_inc(S("cols_summed"), t.made("cols_summed"))
            for g in range(2):
                token(("gv", g), xg, lambda ap, i: ap[:, 128 * i:128 * i + 128])
            for c in range(4):
                feature(("gu", c), xg)
            pe.wait_ge(S("ws_masked"), t.next("ws_masked"))
            pe.wait_ge(S("gv_normed"), t.next("gv_normed", QT))
            for c in range(4):
                for par in range(2):
                    h = 2 * c + par
                    for i in range(QT):
                        ins = nc.tensor.matmul(PS[64 * par:64 * par + 64, 4 + c, 128 * i:128 * i + 128],
                                               GV[:, i, 64 * h:64 * h + 64], WS[:, h, :], start=True, stop=True)
                ins.then_inc(S("spatial_done"), t.made("spatial_done"))

            for c in range(DC):
                feature(("mixout", 0, c), (YH, YL), ready="y_lo_made" if c == 0 else None)

            def feed_forward(layer):
                for n, (f0, fn) in enumerate(PASS):
                    for f in range(f0, f0 + fn):
                        feature(("fg", layer, f), xg, ready="xg_lo_made" if f == 0 else None)
                        if f == 0:
                            norm_sum()
                        feature(("fu", layer, f), xg)
                    for c in range(DC):
                        feature(("fd", layer, n, c), (YH, YL), ready="y_lo_made" if c == 0 else None)

            def embed(layer):
                feature(("pg", layer, 0), xg, ready="xg_lo_made")
                norm_sum()
                pe.wait_ge(S("ple_lo_made"), t.next("ple_lo_made", 2))
                feature(("pp", layer, 0), (PH, PL))
                for c in range(1, DC):
                    feature(("pg", layer, c), xg)
                    feature(("pp", layer, c), (PH, PL))

            feed_forward(0)
            embed(0)
            xg = (YH, YL)
            feature(("ql", 0), xg, ready="xg_lo_made")
            norm_sum()
            for c in (1, 2):
                feature(("ql", c), xg)
            for c in range(2):
                feature(("kvl", c), xg)
            norm_sum(chunks=3)
            feature(("small", 0), xg)
            feature(("mq", 0), xg)
            norm_sum(chunks=2)
            feature(("mq", 1), xg)
            pe.wait_ge(S("rstd_made"), t.next("rstd_made", 3))
            for i in range(QT):
                ins = nc.tensor.matmul(PS[:, 7, i:i + 1], RB[:, 128 * i:128 * i + 128], const("ident", n=1),
                                       start=True, stop=True)
            ins.then_inc(S("cols_summed"), t.made("cols_summed"))
            for c in range(2):
                feature(("mk", c), xg)
            for g in range(2):
                token(("mv", g), xg, lambda ap, i: ap[:, 128 * i:128 * i + 128])

            def head_sum(m):
                u, c, rows, _ = HEADS[m]
                r = 32 if m == 0 else 128
                pe.wait_ge(S("head_sq_made"), t.next("head_sq_made"))
                nc.tensor.matmul(PS[0:r, 5 + m % 2, :], const("blk64" if rows == 64 else "blk32", rows=r, n=r),
                                 SQ[0:r, m % 2, :], start=True, stop=True).then_inc(S("head_summed"), t.made("head_summed"))

            def turn_pairs(m):
                r = 32 if m == 0 else 128
                pe.wait_ge(S("rope_in"), t.next("rope_in"))
                nc.tensor.matmul(PS[0:r, 7, :], const("rot", rows=r, n=r), TMP[0:r, 2, :], start=True, stop=True).then_inc(S("rot_done"), t.made("rot_done"))

            lat_q, lat_kv = (LH[:, 0:3, :], LL[:, 0:3, :]), (LH[:, 3:5, :], LL[:, 3:5, :])
            for m in range(len(HEADS) + 1):
                if 0 < m < len(HEADS):
                    u, c, _, _ = HEADS[m]
                    if m == 1:
                        pe.wait_ge(S("lat_lo_made"), t.next("lat_lo_made", 5))
                    feature((u, c), lat_kv if u == "kn" else lat_q)
                if m:
                    head_sum(m - 1)
                    if HEADS[m - 1][2] == 32:
                        turn_pairs(m - 1)
            for g in range(2):
                token(("va", g), lat_kv, lambda ap, i: ap[:, 128 * i:128 * i + 128])
            feature(("mo", 0), xg)
            pe.wait_ge(S("lf_made"), t.next("lf_made"))
            for b in range(QT):
                ins = nc.tensor.transpose(PS[:, 4, 4 * b:4 * b + 4], F_ROW[:, 128 * b:128 * b + 128], const("ident", rows=4, n=4))
            ins.then_inc(S("lf_turned"), t.made("lf_turned"))
            feature(("mo", 1), xg)
            pe.wait_ge(S("lf_cols"), t.next("lf_cols"))
            for b in range(QT):
                ins = nc.tensor.matmul(PS[0:4, 5, :], LFC[:, 0, b, :], const("upto", at=384 - 128 * b, n=512),
                                       start=(b == 0), stop=(b == QT - 1))
            ins.then_inc(S("a_summed"), t.made("a_summed"))
            feature(("mo", 2), xg)
            feature(("mo", 3), xg)
            pe.wait_ge(S("b_made"), t.next("b_made"))
            for b in range(QT):
                ins = nc.tensor.transpose(PS[:, 6, 4 * b:4 * b + 4], I_ROW[:, 128 * b:128 * b + 128], const("ident", rows=4, n=4))
            ins.then_inc(S("b_turned"), t.made("b_turned"))
            pe.wait_ge(S("b_cols"), t.next("b_cols"))

            def d_score(n):
                h, i = DTILES[n]
                w = 128 * (i + 1)
                if n == 0:
                    pe.wait_ge(S("head_taken"), t.next("head_taken", len(HEADS)))
                    pe.wait_ge(S("kr_kept"), t.next("kr_kept"))
                if n in (2, 3):
                    idle(SBANK[n])
                if n >= 4:
                    pe.wait_ge(S("d_exp_made"), t.next("d_exp_made"))
                nc.tensor.matmul(PS[:, SBANK[n % 4], 0:w], QF[:, h, 128 * i:128 * i + 128], KF[:, h, 0:w],
                                 start=True, stop=True).then_inc(S("d_scored"), t.made("d_scored"))

            def d_turn(n):
                h, i = DTILES[n]
                pe.wait_ge(S("d_probs_made"), t.next("d_probs_made"))
                if n >= 2:
                    pe.wait_ge(S("d_turn_kept"), n - 1)
                for kb in range(i + 1):
                    ins = nc.tensor.transpose(PS[:, 6 + n % 2, 128 * kb:128 * kb + 128], PD[:, n % 4, 128 * kb:128 * kb + 128],
                                              const("ident"))
                ins.then_inc(S("d_turned"), t.made("d_turned"))

            def d_values(n):
                h, i = DTILES[n]
                c, par = h // 2, h % 2
                pe.wait_ge(S("d_turn_kept"), n + 1)
                if n == 0:
                    for b in range(QT):
                        pe.wait_ge(acc_free[bank(("va", 1), b)], freed(("va", 1), b))
                if n % 8 == 0:
                    if c < 2:
                        idle(2 + c)
                    else:
                        pe.wait_ge(S("y_lo_made"), t.next("y_lo_made"))
                for kb in range(i + 1):
                    ins = nc.tensor.matmul(PS[64 * par:64 * par + 64, 2 + c % 2, 128 * i:128 * i + 128],
                                           VA[:, kb, 64 * h:64 * h + 64], PTD[:, n % 2, 128 * kb:128 * kb + 128],
                                           start=(kb == 0), stop=(kb == i))
                if n % 8 == 7:
                    ins.then_inc(S("d_mixed"), t.made("d_mixed"))

            for n in range(3):
                d_score(n)
            for n in range(len(DTILES)):
                if n + 3 < len(DTILES):
                    d_score(n + 3)
                d_turn(n)
                if n:
                    d_values(n - 1)
            d_values(len(DTILES) - 1)
            pe.wait_ge(S("y_lo_made"), t.next("y_lo_made", 2))
            pe.wait_ge(S("d_exp_made"), t.next("d_exp_made", 4))

            pe.wait_ge(S("floor_made"), t.next("floor_made"))

            def m_spread(h):
                if h:
                    pe.wait_ge(S("decay_pre"), t.next("decay_pre", 4))
                nc.tensor.matmul(PS[:, M_G, :], const("head", rows=4, at=128 * h), G_ROW, start=True, stop=True).then_inc(S("g_spread"), t.made("g_spread"))

            def m_score(k):
                h, b = k // 4, k % 4
                c, r = h // 2, slice(64 * (h % 2), 64 * (h % 2) + 64)
                if k >= 3:
                    pe.wait_ge(S("weighted_made"), k - 2)
                nc.tensor.matmul(PS[:, M_S[k % 3], 0:T - 128 * b], MK[r, c, 128 * b:128 * b + 128],
                                 MQ[r, c, 128 * b:T], start=True, stop=True).then_inc(S("m_scored"), t.made("m_scored"))

            def m_add(k):
                h, b = k // 4, k % 4
                w = T - 128 * b
                pe.wait_ge(S("weighted_made"), k + 1)
                nc.tensor.matmul(PS[:, M_NUM[h % 2], 128 * b:T], MV[:, b, 128 * h:128 * h + 128], SW[:, k % 4, 0:w],
                                 start=(b == 0), stop=(b == 3))
                if b == 0 and h:
                    pe.wait_ge(S("den_abs"), t.next("den_abs"))
                nc.tensor.matmul(PS[:, M_DEN, 128 * b:T], const("ones"), SW[:, k % 4, 0:w],
                                 start=(b == 0), stop=(b == 3)).then_inc(S("m_added"), t.made("m_added"))
                if b == 3:
                    if h:
                        pe.wait_ge(S("h_made"), t.next("h_made"))
                    nc.tensor.matmul(PS[:, M_FLOOR, :], const("head", rows=4, at=128 * h), F_ROW,
                                     start=True, stop=True).then_inc(S("h_summed"), t.made("h_summed"))

            m_spread(0)
            m_score(0)
            m_score(1)
            for k in range(16):
                if k + 2 < 16:
                    m_score(k + 2)
                if k % 4 == 1 and k < 12:
                    m_spread(k // 4 + 1)
                m_add(k)
            pe.wait_ge(S("h_made"), t.next("h_made"))
            for h in range(4):
                pe.wait_ge(S("h_sq_made"), t.next("h_sq_made"))
                nc.tensor.matmul(PS[:, 5 + h % 2, :], const("ones"), SQ[:, h % 2, :], start=True, stop=True).then_inc(S("h_sq_summed"), t.made("h_sq_summed"))
            for c in range(DC):
                if c == 0:
                    pe.wait_ge(S("y_lo_made"), t.next("y_lo_made", 4))
                feature(("mixout", 1, c), (YH, YL))
            xg = (XH, XL)
            feed_forward(1)
            embed(1)


def chunked(a):
    return np.ascontiguousarray(a.reshape(-1, 128, a.shape[-1]).transpose(1, 0, 2))


def lay_out(i):
    vec = np.zeros((128, NVEC), np.float32)

    def put(name, a):
        a = a.reshape(-1, a.shape[-1]) if a.ndim > 1 else a[None]
        a = a.reshape(a.shape[0], -1, 128).transpose(2, 0, 1).reshape(128, -1)
        vec[:, VEC[name]:VEC[name] + a.shape[1]] = a

    put("norm_g", i["norm_g"])
    put("mem_norm_g", i["mem_norm_g"])
    put("final_g", i["final_norm_g"])
    put("g_mix", i["g_mix_2"])
    put("g_ffn", i["g_ffn_2"])
    put("g_ple", i["g_ple_2"])
    put("conv", i["ev_w_conv_2"][0])
    put("g_qa", i["od_g_qa_2"])
    put("g_kva", i["od_g_kva_2"])
    gq, gk = i["od_g_q_2"][0], i["od_g_k_2"][0]
    vec[:, VEC["g_qn"]] = np.tile(gq[:64], 2)
    vec[:, VEC["g_qr"]] = np.tile(gq[64:], 4)
    vec[:, VEC["g_kn"]] = np.tile(gk[:64], 2)
    vec[:, VEC["g_kr"]] = np.tile(gk[64:], 4)
    put("g_mh", i["od_g_mh_2"])
    vec[32:36, VEC["b_i"]] = i["od_b_gate_2"][0, :4]
    vec[64:68, VEC["b_f"]] = i["od_b_gate_2"][0, 4:]
    vec[:, VEC["b_s"]:VEC["b_s"] + 8] = i["ev_b_s_2"][0].T
    vec[:, VEC["eps"]] = EPS
    vec[:, VEC["halfpi"]] = np.float32(np.pi / 2)
    vec[:, VEC["inv_freq"]] = (10000.0 ** (-np.arange(0, 32, 2) / 32.0)).astype(np.float32)[np.arange(128) % 16]
    weights = {"mem_kv": i["w_mem_kv"][0], "in": i["w_in"][0], "out": i["w_out"][0],
               "ev_in": i["ev_w_in_2"][0], "ev_out": i["ev_w_out_2"][0], "od_in": i["od_w_in_2"][0],
               "od_out": i["od_w_out_2"][0], "q_up": i["od_w_q_up_2"][0], "kv_up": i["od_w_kv_up_2"][0]}
    for n in range(2):
        weights |= {f"gate{n}": i["w_gate_2"][n], f"up{n}": i["w_up_2"][n], f"down{n}": i["w_down_2"][n],
                    f"ple_gate{n}": i["w_ple_gate_2"][n], f"ple_proj{n}": i["w_ple_proj_2"][n]}
    blocks = layout().blocks
    wall = np.zeros((len(blocks), 128, BLK), np.float32)
    for j, (name, parts, width) in enumerate(blocks):
        for n, (k, spec) in enumerate(parts):
            wall[j, :, n * width:(n + 1) * width] = block_columns(weights[name], k, spec, width)
    table, bias = constants()
    ws = np.ascontiguousarray(i["ev_w_s_2"][0].transpose(2, 0, 1)).reshape(128, 1024)
    bs = i["ev_b_s_2"][0].reshape(4, 2, 1, 128)
    bs = np.broadcast_to(bs, (4, 2, 64, 128)).transpose(1, 2, 0, 3).reshape(128, 512)
    return {
        "x": chunked(np.ascontiguousarray(i["x"][0].T)),
        "mem": chunked(np.ascontiguousarray(i["mem"][0].T)),
        "wall": wall,
        "ple": np.stack([chunked(np.ascontiguousarray(i["p_2"][n, 0].T)) for n in range(2)]),
        "vec": vec,
        "table": table,
        "bias": bias,
        "ws": ws,
        "bs": np.ascontiguousarray(bs),
        "gv": np.ascontiguousarray(np.broadcast_to(i["ev_g_v_2"][0].reshape(1, 512), (128, 512))),
        "pos": np.ascontiguousarray(np.broadcast_to(i["positions_2"].reshape(1, T), (128, T))),
    }


def kernel(**inputs):
    import concourse.bacc as _bacc
    from concourse.bass_utils import run_bass_kernel_spmd as _run

    nc = _bacc.Bacc("TRN2", target_bir_lowering=False, num_devices=1, dynamic_dma_scratch_size=1024)
    arrays = lay_out({k: np.asarray(v) for k, v in inputs.items()})
    args = {}
    for name, a in arrays.items():
        args[name] = nc.dram_tensor(f"in_{name}", a.shape, mybir.dt.from_np(a.dtype), kind="ExternalInput").ap()
    args["y"] = nc.dram_tensor("out_y", (128, DC, T), F32, kind="ExternalOutput").ap()
    build(nc, **args)
    r = _run(nc, [{f"in_{k}": v for k, v in arrays.items()}], core_ids=[0])
    y = r.results[0]["out_y"]
    return np.ascontiguousarray(y.transpose(1, 0, 2).reshape(D, T).T).reshape(1, T, D)
```

```python
import numpy as np
import concourse.bass as bass
from concourse import mybir
from contextlib import ExitStack

F32 = mybir.dt.float32
F32R = mybir.dt.float32r
I32 = mybir.dt.int32
ACT = mybir.ActivationFunctionType
ALU = mybir.AluOpType
AX = mybir.AxisListType

D, T, NMEM, DPLE, FF = 1024, 512, 256, 256, 2816
DC = D // 128
MIX, HD = 768, 64
QT = T // 128
FCH = FF // 128
PASS = [(0, 8), (8, 8), (16, 6)]
RAW, HL = 5, 4
ACC = 4
BLK = 1024
NEG = -1e30
EPS = 1e-6
DSCALE = 96.0 ** -0.5
ROUND = 12582912.0
TWO_PI = (6.28125, float(np.float32(2 * np.pi - 6.28125)), 2 * np.pi - 6.28125 - float(np.float32(2 * np.pi - 6.28125)))
PI_BELOW = 3.1415925
ORDER = (1, 4, 4)


HEADS = ([("small", 0, 32, "g_kr")] + [("qn", c, 64, "g_qn") for c in range(4)]
         + [("qr", c, 32, "g_qr") for c in range(2)] + [("kn", c, 64, "g_kn") for c in range(4)])
BESIDE = {1: ("mk", 0), 4: ("mk", 1), 6: ("mo", 0), 7: ("mo", 1), 9: ("mo", 2)}


class Plan:

    def __init__(self):
        self.blocks, self.units, self.acc = [], {}, 0

    def feature(self, name, weight, kc, cols, width=128):
        self.blocks.append((weight, [(k, cols) for k in range(kc)], width))
        self.units[name] = dict(blocks=[(len(self.blocks) - 1, 0, kc)], acc=self.acc, width=width)
        self.acc += 1

    def token(self, name, weight, kc, cols, tiles):
        first = []
        for k0 in range(0, kc, 4):
            n = min(4, kc - k0)
            self.blocks.append((weight, [(k, cols) for k in range(k0, k0 + n)], 256))
            first.append((len(self.blocks) - 1, k0, n))
        self.units[name] = dict(blocks=first, acc=self.acc, width=256, tiles=tiles)
        self.acc += tiles


def layout():
    p = Plan()
    for c in range(2):
        p.feature(("km", c), "mem_kv", DC, ("range", 128 * c))
    p.token(("vm", 0), "mem_kv", DC, ("range", 256), 2)
    for c in range(6):
        p.feature(("q", c), "in", DC, ("range", 128 * c))
    for c in range(2):
        p.feature(("qm", c), "in", DC, ("range", 3 * MIX + 128 * c))
    for c in range(6):
        p.feature(("k", c), "in", DC, ("range", MIX + 128 * c))
    for g in range(3):
        p.token(("v", g), "in", DC, ("range", 2 * MIX + 256 * g), QT)
    for c in range(DC):
        p.feature(("gate", c), "in", DC, ("range", 3 * MIX + 256 + 128 * c))
    for c in range(DC):
        p.feature(("out", c), "out", DC, ("range", 128 * c))
    for layer in range(2):
        if layer == 0:
            for c in range(4):
                p.feature(("cc", c), "ev_in", DC, ("range", 512 + 128 * c))
                p.feature(("cx", c), "ev_in", DC, ("range", 1024 + 128 * c))
                p.feature(("cb", c), "ev_in", DC, ("range", 128 * c))
            for g in range(2):
                p.token(("gv", g), "ev_in", DC, ("range", 2048 + 256 * g), QT)
            for c in range(4):
                p.feature(("gu", c), "ev_in", DC, ("range", 1536 + 128 * c))
            for c in range(DC):
                p.feature(("mixout", 0, c), "ev_out", DC, ("range", 128 * c))
        else:
            for c in range(3):
                p.feature(("ql", c), "od_in", DC, ("range", 128 * c))
            for c in range(2):
                p.feature(("kvl", c), "od_in", DC, ("range", 384 + 128 * c))
            p.feature(("small", 0), "od_in", DC, ("small", 0))
            for c in range(2):
                p.feature(("mq", c), "od_in", DC, ("range", 672 + 128 * c))
            for g in range(2):
                p.token(("mv", g), "od_in", DC, ("range", 1184 + 256 * g), QT)
            source = {"qn": ("q_up", 3, "nope", 96), "qr": ("q_up", 3, "rope", 96), "kn": ("kv_up", 2, "nope", 128)}
            start = {"mk": 928, "mo": 1696}
            for m, (name, c, _, _) in enumerate(HEADS):
                if m:
                    weight, kc, kind, size = source[name]
                    p.feature((name, c), weight, kc, (kind, size, c))
                if m in BESIDE:
                    name, c = BESIDE[m]
                    p.feature((name, c), "od_in", DC, ("range", start[name] + 128 * c))
            p.feature(("mo", 3), "od_in", DC, ("range", start["mo"] + 3 * 128))
            for g in range(2):
                p.token(("va", g), "kv_up", 2, ("values", g), QT)
            for c in range(DC):
                p.feature(("mixout", 1, c), "od_out", DC, ("range", 128 * c))
        for n, (f0, fn) in enumerate(PASS):
            for f in range(f0, f0 + fn):
                p.feature(("fg", layer, f), f"gate{layer}", DC, ("range", 128 * f))
                p.feature(("fu", layer, f), f"up{layer}", DC, ("range", 128 * f))
            for c in range(DC):
                p.feature(("fd", layer, n, c), f"down{layer}", fn, ("rows", f0, 128 * c))
        for c in range(DC):
            p.feature(("pg", layer, c), f"ple_gate{layer}", DC, ("range", 128 * c))
            p.feature(("pp", layer, c), f"ple_proj{layer}", DPLE // 128, ("range", 128 * c))
    return p


def block_columns(w, k, spec, width):
    kind = spec[0]
    if kind == "range":
        return w[128 * k:128 * k + 128, spec[1]:spec[1] + width]
    if kind == "rows":
        r = 128 * (spec[1] + k)
        return w[r:r + 128, spec[2]:spec[2] + width]
    rows = w[128 * k:128 * k + 128]
    if kind == "small":
        out = np.zeros((128, 128), w.dtype)
        out[:, 0:32] = rows[:, 640:672]
        out[:, 32:36] = rows[:, 2208:2212]
        out[:, 64:68] = rows[:, 2212:2216]
        return out
    if kind == "nope":
        heads = rows.reshape(128, -1, spec[1])
        return heads[:, 2 * spec[2]:2 * spec[2] + 2, 0:64].reshape(128, 128)
    if kind == "rope":
        heads = rows.reshape(128, -1, spec[1])
        return heads[:, 4 * spec[2]:4 * spec[2] + 4, 64:96].reshape(128, 128)
    if kind == "values":
        heads = rows.reshape(128, -1, 128)
        return heads[:, 4 * spec[1]:4 * spec[1] + 4, 64:128].reshape(128, 256)
    raise ValueError(kind)


VEC = {}


def vector_columns():
    at = 0
    for name, n in (("norm_g", 8), ("mem_norm_g", 8), ("final_g", 8), ("g_mix", 16), ("g_ffn", 16),
                    ("g_ple", 16), ("conv", 12), ("g_qa", 3), ("g_kva", 2), ("g_qn", 1), ("g_qr", 1),
                    ("g_kn", 1), ("g_kr", 1), ("g_mh", 4), ("b_i", 1), ("b_f", 1), ("b_s", 8),
                    ("eps", 1), ("inv_freq", 1), ("halfpi", 1)):
        VEC[name] = at
        at += n
    return at


NVEC = vector_columns()

CONST = {}


def const_columns():
    at = 0
    for name, n in (("ident", 128), ("ones", 128), ("blk64", 128), ("blk32", 128), ("rot", 128),
                    ("upto", 896), ("pair", 256), ("head", 512), ("causal", 128)):
        CONST[name] = at
        at += n
    return at


NCONST = const_columns()


def constants():
    c = np.zeros((128, NCONST), np.float32)
    p = np.arange(128)

    def put(name, a):
        c[:a.shape[0], CONST[name]:CONST[name] + a.shape[1]] = a

    put("ident", np.eye(128))
    put("ones", np.ones((128, 128)))
    put("blk64", p[:, None] // 64 == p[None] // 64)
    put("blk32", p[:, None] // 32 == p[None] // 32)
    rot = np.zeros((128, 128))
    for m in range(128):
        rot[m + 16 if m % 32 < 16 else m - 16, m] = -1 if m % 32 < 16 else 1
    put("rot", rot)
    put("upto", np.arange(896)[None] - 384 >= p[:, None])
    pair = np.zeros((4, 2, 128))
    for j in range(4):
        pair[j, j % 2, 64 * (j // 2):64 * (j // 2) + 64] = 1
    put("pair", pair.reshape(4, 256))
    head = np.zeros((4, 4, 128))
    for j in range(4):
        head[j, j] = 1
    put("head", head.reshape(4, 512))
    slopes = (2.0 ** (-8.0 * np.arange(1, 13) / 12)).astype(np.float32)
    bias = np.zeros((128, 4, 512), np.float32)
    b0 = bias[:, 0:2].reshape(128, 2, 2, 256)
    dist = (p[:, None] + 128) - np.arange(256)[None]
    for par in range(2):
        for hh in range(2):
            s = slopes[2 * hh + par]
            b0[:, par, hh] = np.where((dist >= 0) & (dist <= 128), -s * dist.astype(np.float32), NEG)
    d = p[:, None] - p[None]
    for par in range(2):
        for hh in range(2):
            at = (2 * par + hh) * 128
            s = slopes[4 + 2 * hh + par] * np.float32(4)
            bias[:, 2, at:at + 128] = np.where(d >= 0, -s * d.astype(np.float32), NEG)
            s = slopes[8 + 2 * hh + par] * np.float32(16)
            bias[:, 3, at:at + 128] = np.where((d >= 0) & (d % 4 == 0), -s * (d // 4).astype(np.float32), NEG)
    put("causal", np.where(d >= 0, 0.0, NEG))
    return c, bias.reshape(128, 2048)


def build(nc, x, mem, wall, ple, vec, table, bias, ws, bs, gv, pos, y):
    plan = layout()
    blocks, units = plan.blocks, plan.units
    used_width = [len(parts) * width for _, parts, width in blocks]
    nblk = len(blocks)

    ctx = ExitStack()
    with ctx:
        base = (nc.sbuf_base + 63) // 64 * 64
        top = [base]

        def place(name, shape, dt=F32, at=None):
            size = 4 * int(np.prod(shape[1:]))
            off = top[0] if at is None else at
            if at is None:
                top[0] += (size + 31) // 32 * 32
            return nc.alloc_sbuf_tensor_at(name, shape, dt, offset=off)

        KB = 1024
        X = place("x_res", [128, DC, T])
        first = top[0]
        XH = place("xg_hi", [128, DC, T], F32R)
        XL = place("xg_lo", [128, DC, T], F32R)
        second = top[0]
        YH = place("y_hi", [128, DC, T], F32R)
        YL = place("y_lo", [128, DC, T], F32R)
        scratch = top[0]
        top[0] += 56 * KB
        RAWT = place("w_raw", [128, RAW, BLK])
        WH = place("w_hi", [128, HL, BLK], F32R)
        WL = place("w_lo", [128, HL, BLK], F32R)
        VECT = place("vec_t", [128, NVEC])
        CT = place("const_t", [128, NCONST])
        RB = place("rstd_rows", [128, T])
        TMP = place("tmp", [128, 4, T])
        SQ = place("squares", [128, 2, T])
        SSQ = place("sum_sq", [128, T])
        STD = place("std", [128, T])
        QGAIN = place("query_gains", [128, 2])
        GAIN2 = place("gain_product", [128, DC])
        RC = place("rstd_cols", [128, 14])
        GR = place("gate_rows", [4, 2, T])
        STAT = place("stats", [128, 3, 4, 4, 2])
        LFC = place("gate_cols", [128, 2, 4, 4])
        NEGM = place("neg_max", [128, 16])
        SUM = place("row_sum", [128, 16])
        assert top[0] <= nc.sbuf_usable_end, (top[0], nc.sbuf_usable_end)

        Q = place("q_a", [128, 6, T], at=second)
        QM = place("qm_a", [128, 2, T], at=second + 12 * KB)
        K = place("k_a", [128, 6, T], at=second + 16 * KB)
        KM = place("km_a", [128, 2, NMEM], at=second + 28 * KB)
        MIXT = place("mix_a", [128, DC, T], at=scratch)
        V = place("v_a", [128, 3, QT, 256], at=scratch + 16 * KB)
        VM = place("vm_a", [128, 2, 256], at=scratch + 28 * KB)
        SB = place("scores_a", [128, 2, 4, 256], at=scratch + 30 * KB)
        PT = place("probs_t_a", [128, 2, 8, 128], at=scratch + 38 * KB)
        ROWS = place("rows_a", [4, 6, T], at=scratch + 30 * KB)
        BIAS = place("bias_a", [128, 4, T], at=scratch + 48 * KB)
        MEMX = place("mem_a", [128, DC, NMEM], at=scratch + 16 * KB)
        MH = place("mem_hi", [128, DC, NMEM], F32R, at=scratch)
        ML = place("mem_lo", [128, DC, NMEM], F32R, at=scratch + 8 * KB)
        RBM = place("rstd_mem", [128, NMEM], at=scratch + 46 * KB)

        GV = place("gv_b", [128, QT, 512], at=scratch)
        WS = place("ws_b", [128, 8, 128], at=scratch + 8 * KB)
        BS = place("bs_b", [128, 4, 128], at=scratch + 12 * KB)
        GVB = place("gvb_b", [128, 512], at=scratch + 14 * KB)
        MB = place("spatial_b", [128, 4, T], at=scratch + 16 * KB)
        SV = place("gv_sq_b", [128, 512], at=scratch + 24 * KB)
        SS = place("gv_ss_b", [128, QT, 8], at=scratch + 26 * KB)

        PR = place("ple_raw", [128, 2, T], at=scratch)
        PH = place("ple_hi", [128, 2, T], F32R, at=scratch + 4 * KB)
        PL = place("ple_lo", [128, 2, T], F32R, at=scratch + 8 * KB)

        QF = place("q_full", [96, 8, T], at=first)
        KF = place("k_full", [96, 8, T], at=first + 16 * KB)
        LAT = place("latent", [128, 5, T], at=first)
        SMALL = place("small_d", [128, T], at=first + 10 * KB)
        LH = place("lat_hi", [128, 5, T], F32R, at=scratch)
        LL = place("lat_lo", [128, 5, T], F32R, at=scratch + 10 * KB)
        MQ = place("mq_d", [128, 2, T], at=scratch + 20 * KB)
        MK = place("mk_d", [128, 2, T], at=scratch + 24 * KB)
        MV = place("mv_d", [128, QT, 512], at=scratch + 28 * KB)
        MO = place("mo_d", [128, 4, T], at=scratch + 36 * KB)
        VA = place("va_d", [128, QT, 512], at=scratch + 44 * KB)
        COS = place("cos_d", [128, T], at=scratch + 52 * KB)
        SIN = place("sin_d", [128, T], at=scratch + 54 * KB)
        POS = place("pos_d", [128, T], I32, at=scratch + 50 * KB)
        PD = place("probs_d", [128, 4, T], at=scratch)
        PTD = place("probs_t_d", [128, 2, T], at=scratch + 8 * KB)
        WT = place("decay_d", [128, 4, T], at=first + 16 * KB)
        SW = place("weighted_d", [128, 4, T], at=first)
        HT = place("mh_d", [128, 4, T], at=first + 24 * KB)
        PS = ctx.enter_context(nc.psum_tensor("psum", [128, 8, 512], F32))

        def const(name, rows=128, at=0, n=128):
            return CT[0:rows, CONST[name] + at:CONST[name] + at + n]

        def col(name, c=0, rows=slice(0, 128)):
            return VECT[rows, VEC[name] + c:VEC[name] + c + 1]

        sems = {}

        def S(name):
            if name not in sems:
                sems[name] = ctx.enter_context(nc.semaphore(name))
            return sems[name]

        class Tally:

            def __init__(self):
                self.n = {}

            def made(self, name):
                self.n[name] = self.n.get(name, 0) + 1
                return 1

            def next(self, name, more=1):
                self.n[name] = self.n.get(name, 0) + more
                return self.n[name]

            def last(self, name):
                return self.n[name]

        raw_full = [ctx.enter_context(nc.semaphore(f"raw_full{i}")) for i in range(RAW)]
        acc_free = [ctx.enter_context(nc.semaphore(f"acc_free{i}")) for i in range(ACC)]
        S("hi_done"), S("lo_done"), S("block_used")

        def last_block(u):
            return units[u]["blocks"][-1][0]

        def bank(u, tile=0):
            return (units[u]["acc"] + tile) % ACC

        I_ROW, F_ROW = GR[:, 0, :], GR[:, 1, :]
        G_ROW, A_ROW = SSQ[0:4, :], STD[0:4, :]
        MAX_ROWS = (TMP[0:4, 0, :], TMP[0:4, 1, :])
        b0 = bank(("mixout", 1, 0))
        M_G, M_S, M_NUM, M_DEN, M_FLOOR = 4, (5, 6, (b0 + 3) % ACC), (b0, (b0 + 2) % ACC), (b0 + 1) % ACC, 7

        def residue(ap, g):
            return ap if g == 0 else ap.rearrange("p (u r) -> p r u", r=ORDER[g])

        def tile_tokens(ap, g, i):
            if g in (0, 3):
                return ap[:, 128 * i:128 * i + 128]
            return ap.rearrange("p (u r) -> p r u", r=4)[:, i, :]

        def freed(u, tile=0):
            return (units[u]["acc"] + tile) // ACC + 1

        TILES = [(g, i) for g in (3, 0, 1, 2) for i in range(QT)]

        SPAIR = (4, 0)

        def sbuf(n):
            return SB[:, n % 2, :, :] if n % 4 < 2 else TMP[:, 2 * (n % 2):2 * (n % 2) + 2, :].rearrange("p a (b k) -> p (a b) k", b=2)

        def keys(g, i):
            if g == 3:
                return NMEM, 0
            if g == 0:
                return (256, 128 * (i - 1)) if i else (128, 0)
            return 128, 128 * i

        TURNED = np.cumsum([keys(g, i)[0] // 128 for g, i in TILES]).tolist()

        DTILES = [(h, i) for h in range(8) for i in range(QT)]
        SBANK = (4, 5, 0, 1)

        block = ctx.enter_context(nc.Block())

        @block.sync
        def _(sp):
            def load(dst, src, name):
                sp.dma_start(dst, src).then_inc(S(name), 16)

            def load_pairs(dst, src, name, pairs):
                for i in pairs:
                    load(dst[:, 2 * i:2 * i + 2, :], src[:, 2 * i:2 * i + 2, :], f"{name}{i}")

            load_pairs(MEMX, mem, "mem_in", (0,))
            load(VECT[:], vec, "vec_in")
            for j in range(nblk):
                if j >= RAW:
                    sp.wait_ge(S("lo_done"), j - RAW + 1)
                n = used_width[j]
                sp.dma_start(RAWT[:, j % RAW, 0:n], wall[j, :, 0:n]).then_inc(raw_full[j % RAW], 16)
                if j == 0:
                    load_pairs(MEMX, mem, "mem_in", range(1, DC // 2))
                if j == 1:
                    load_pairs(X, x, "x_in", (0,))
                if j == 2:
                    load(CT[:, 0:256], table[:, 0:256], "const_in")
                    load_pairs(X, x, "x_in", (1,))
                if j == 3:
                    load_pairs(X, x, "x_in", (2, 3))
                if j == 8:
                    load(CT[:, 256:NCONST], table[:, 256:NCONST], "const_rest_in")
                    load(BIAS[:], bias.rearrange("p (a b) -> p a b", a=4), "bias_in")
            for c in range(DC):
                sp.wait_ge(S("x_final"), 6 * DC + 1 + c)
                load(y[:, c, :], X[:, c, :], "y_out")
            sp.wait_ge(S("y_out"), 16 * DC)

        @block.gpsimd
        def _(pool):
            for j in range(nblk):
                n, r, s = used_width[j], j % RAW, j % HL
                pool.wait_ge(S("hi_done"), j + 1)
                pool.wait_ge(raw_full[r], 16 * (j // RAW + 1))
                nc.gpsimd.tensor_tensor(WL[:, s, 0:n], RAWT[:, r, 0:n], WH[:, s, 0:n].bitcast(F32),
                                        ALU.subtract).then_inc(S("lo_done"), 1)

        @block.scalar
        def _(act):
            t = Tally()
            at, loaded = [0], [None]

            def split_to(j):
                while at[0] <= min(j, nblk - 1):
                    b = at[0]
                    n, r, s = used_width[b], b % RAW, b % HL
                    act.wait_ge(raw_full[r], 16 * (b // RAW + 1))
                    if b >= HL:
                        act.wait_ge(S("block_used"), b - HL + 1)
                    nc.scalar.activation(WH[:, s, 0:n], RAWT[:, r, 0:n], ACT.Copy).then_inc(S("hi_done"), 1)
                    at[0] += 1

            def unit(u):
                split_to(last_block(u) + HL - 1)
                act.wait_ge(S("block_used"), last_block(u) + 1)

            def tile_result(u, i):
                tiles = units[u]["tiles"]
                split_to(last_block(u) + HL - 1)
                if i < tiles - 1:
                    act.wait_ge(S("tile_done"), t.next("tile_done"))
                else:
                    act.wait_ge(S("block_used"), last_block(u) + 1)

            def tables(name):
                if name != loaded[0]:
                    nc.scalar.preload_act_table_set(name)
                loaded[0] = name

            LOG_EXP, SILU, SIGMOID = "natural_log_exp_and_others", "silu_and_others", "sigmoid_and_others"
            GELU = "gelu_apprx_tanh_and_others"

            def inverse_root(out, src, width, signal, between=None, rows=slice(0, 128)):
                mid = out if between is None else between
                nc.scalar.activation(mid, src, ACT.Ln, scale=1.0 / width, bias=col("eps", rows=rows)).then_inc(S("act_step"), t.made("act_step"))
                act.wait_ge(S("act_step"), t.last("act_step"))
                nc.scalar.activation(out, mid, ACT.Exp, scale=-0.5).then_inc(S(signal), t.made(signal))

            def norm_part(c, gain, hi=XH):
                act.wait_ge(S("x_final"), t.next("x_final"))
                act.wait_ge(S("sq_taken"), t.next("sq_taken"))
                nc.scalar.activation(SQ[:, c % 2, :], X[:, c, :], ACT.Square).then_inc(S("sq_made"), t.made("sq_made"))
                nc.scalar.activation(hi[:, c, :], X[:, c, :], ACT.Copy, scale=col(gain[0], gain[1] + c)).then_inc(S("xg_hi_made"), t.made("xg_hi_made"))

            def x_norm(gain, behind):
                for c in range(DC):
                    split_to(last_block(behind(c)) + HL - 1)
                    norm_part(c, gain)

            def norm_root(then=None):
                tables(LOG_EXP)
                act.wait_ge(S("ssum_done"), t.next("ssum_done"))
                inverse_root(RB[:, :], PS[:, 4, :], D, "rstd_made", STD[:, :])
                if then is not None:
                    tables(then)

            tables(LOG_EXP)
            def first_half(c, src, hi, sq, gain, name):
                if c % 2 == 0:
                    act.wait_ge(S(f"{name}{c // 2}"), 16)
                if t.n.get("sq_made", 0) >= 2:
                    act.wait_ge(S("sq_taken"), t.next("sq_taken"))
                nc.scalar.activation(sq, src[:, c, :], ACT.Square).then_inc(S("sq_made"), t.made("sq_made"))
                nc.scalar.activation(hi[:, c, :], src[:, c, :], ACT.Copy, scale=col(gain, c)).then_inc(S("xg_hi_made"), t.made("xg_hi_made"))

            act.wait_ge(S("vec_in"), 16)
            for c in range(DC):
                first_half(c, MEMX, MH, SQ[:, c % 2, 0:NMEM], "mem_norm_g", "mem_in")
                if c == 1:
                    split_to(0)
            split_to(1)
            for c in range(DC):
                first_half(c, X, XH, SQ[:, c % 2, :], "norm_g", "x_in")
                if c in (1, 3):
                    split_to(c // 2 + 2)
                if c == 4:
                    act.wait_ge(S("ssum_done"), t.next("ssum_done"))
                    inverse_root(RBM[:, :], PS[:, 4, 0:NMEM], D, "rstd_made", STD[:, 0:NMEM])
                if c >= 5:
                    split_to(HL + c - 5)
            split_to(last_block(("vm", 0)) + HL - 1)
            act.wait_ge(S("cols_made"), t.next("cols_made"))
            for i in range(2):
                tile_result(("vm", 0), i)
                nc.scalar.activation(VM[:, i, :], PS[:, bank(("vm", 0), i), 0:256], ACT.Copy,
                                     scale=RC[:, 12 + i:13 + i]).then_inc(acc_free[bank(("vm", 0), i)], 1)
            split_to(last_block(("q", 0)) + HL - 1)
            norm_root()
            for u in [("q", c) for c in range(6)] + [("qm", c) for c in range(2)] + [("k", c) for c in range(6)]:
                split_to(last_block(u) + HL - 1)
            def exps(n):
                g, i = TILES[n]
                w, _ = keys(g, i)
                act.wait_ge(S("scores_ready"), t.next("scores_ready"))
                for j in range(4):
                    ins = nc.scalar.activation(
                        sbuf(n)[:, j, 0:w], sbuf(n)[:, j, 0:w], ACT.Exp,
                        bias=NEGM[:, 4 * (n % 4) + j:4 * (n % 4) + j + 1], scale=0.125 if g == 3 else 1.0,
                        accum_out=(SUM[:, 4 * (n % 4) + j:4 * (n % 4) + j + 1] if g == 3 else STAT[:, g, i, j, 1:2]))
                ins.then_inc(S("probs_made"), t.made("probs_made"))

            for g in range(3):
                if g == 0:
                    act.wait_ge(S("cols_made"), t.next("cols_made"))
                if g == 2:
                    split_to(last_block(("v", 2)) + HL - 2)
                    exps(0)
                for i in range(QT):
                    b = bank(("v", g), i)
                    tile_result(("v", g), i)
                    nc.scalar.activation(V[:, g, i, :], PS[:, b, 0:256], ACT.Copy,
                                         scale=RC[:, 4 * g + i:4 * g + i + 1]).then_inc(acc_free[b], 1)

            def transposed(n):
                g, i = TILES[n]
                nb = keys(g, i)[0] // 128
                for half in range(nb):
                    act.wait_ge(S("turned"), t.next("turned"))
                    nc.scalar.activation(PT[:, n % 2, 4 * half:4 * half + 4, :], PS[:, 6 + (t.n["turned"] - 1) % 2, :],
                                         ACT.Copy).then_inc(S("turned_kept"), t.made("turned_kept"))

            def mixed(n):
                g, i = TILES[n]
                act.wait_ge(S("mixed"), t.next("mixed"))
                c0 = 6 if g == 3 else 2 * g
                for hh in range(2):
                    src = PS[:, 2 + n % 2, 128 * hh:128 * hh + 128]
                    dst = tile_tokens(MIXT[:, c0 + hh, :], g, i)
                    ins = nc.scalar.activation(dst, src, ACT.Copy)
                ins.then_inc(S("mix_kept"), t.made("mix_kept"))

            for n in range(len(TILES)):
                if n:
                    exps(n)
                if n >= 1:
                    transposed(n - 1)
                if n >= 3:
                    mixed(n - 3)
            transposed(len(TILES) - 1)
            for n in range(len(TILES) - 3, len(TILES)):
                mixed(n)
            split_to(last_block(("gate", 0)) + HL - 1)
            act.wait_ge(S("row_max_ready"), t.next("row_max_ready"))
            for g in range(3):
                ins = nc.scalar.activation(ROWS[:, g, :], ROWS[:, g, :], ACT.Exp)
            ins.then_inc(S("row_exp"), t.made("row_exp"))
            tables(SILU)
            split_to(last_block(("gate", 1)) + HL - 1)

            def y_hi(dst):
                act.wait_ge(S("y_made"), t.next("y_made"))
                nc.scalar.activation(dst, TMP[:, 2 + (t.n["y_made"] - 1) % 2, :], ACT.Copy).then_inc(S("y_hi_made"), t.made("y_hi_made"))

            for c in range(DC):
                split_to(last_block(("gate", min(c + 1, DC - 1))) + HL - 1)
                act.wait_ge(S("pre"), t.next("pre"))
                nc.scalar.activation(TMP[:, c % 2, :], TMP[:, c % 2, :], ACT.Silu).then_inc(S("gate_made"), t.made("gate_made"))
                y_hi(YH[:, c, :])
            for c in range(DC):
                split_to(last_block(("out", c)) + HL - 1)
                act.wait_ge(S("x_final"), t.next("x_final"))
                for i in range(2):
                    act.wait_ge(S("sq_taken"), t.next("sq_taken"))
                    nc.scalar.activation(SQ[:, i, :], X[:, c, :], ACT.Square, scale=col("final_g", c) if i else 1.0).then_inc(S("sq_made"), t.made("sq_made"))
                if c == 0:
                    act.wait_ge(S("gains_made"), t.next("gains_made"))
                nc.scalar.activation(XH[:, c, :], X[:, c, :], ACT.Copy, scale=GAIN2[:, c:c + 1]).then_inc(S("xg_hi_made"), t.made("xg_hi_made"))
            tables(LOG_EXP)
            act.dma_start(WS[:], ws.rearrange("p (a b) -> p a b", a=8)).then_inc(S("ws_in"), 16)
            act.dma_start(BS[:], bs.rearrange("p (a b) -> p a b", a=4)).then_inc(S("bs_in"), 16)
            act.dma_start(GVB[:], gv).then_inc(S("gv_in"), 16)
            split_to(last_block(("cc", 0)) + HL - 1)
            act.wait_ge(S("ssum_done"), t.next("ssum_done"))
            inverse_root(STD[:, :], PS[:, 4, :], D, "r1_made")
            split_to(last_block(("cx", 0)) + HL - 1)
            act.wait_ge(S("mean2_made"), t.next("mean2_made"))
            inverse_root(TMP[:, 1, :], TMP[:, 1, :], D, "r2_made")
            tables(GELU)
            for c in range(4):
                for k in ("cc", "cx", "cb"):
                    split_to(last_block((k, c)) + HL - 1)
                y_hi(YH[:, c, :])
            for g in range(2):
                if g == 0:
                    act.wait_ge(S("cols_made"), t.next("cols_made"))
                for i in range(QT):
                    b = bank(("gv", g), i)
                    tile_result(("gv", g), i)
                    nc.scalar.activation(GV[:, i, 256 * g:256 * g + 256], PS[:, b, 0:256], ACT.Gelu_apprx_tanh,
                                         scale=RC[:, i:i + 1]).then_inc(acc_free[b], 1)
            split_to(last_block(("gu", 0)) + HL - 1)
            tables(LOG_EXP)
            act.wait_ge(S("gv_summed"), t.next("gv_summed"))
            inverse_root(SS[:, :, :], SS[:, :, :], 64, "gv_rstd_made")
            tables(GELU)
            for c in range(4):
                split_to(last_block(("gu", c)) + HL - 1)
                act.wait_ge(S("pre"), t.next("pre"))
                nc.scalar.activation(TMP[:, c % 2, :], TMP[:, c % 2, :], ACT.Gelu_apprx_tanh).then_inc(S("gate_made"), t.made("gate_made"))
                y_hi(YH[:, 4 + c, :])
            x_norm(("g_ffn", 0), behind=lambda c: ("mixout", 0, c))

            def feed_forward(layer):
                act.dma_start(PR[:], ple[layer]).then_inc(S("ple_in"), 16)
                split_to(last_block(("fg", layer, 0)) + HL - 1)
                norm_root(SILU)
                for n, (f0, fn) in enumerate(PASS):
                    for f in range(f0, f0 + fn):
                        split_to(last_block(("fg", layer, f)) + HL - 1)
                        act.wait_ge(S("pre"), t.next("pre"))
                        nc.scalar.activation(TMP[:, f % 2, :], TMP[:, f % 2, :], ACT.Silu).then_inc(S("gate_made"), t.made("gate_made"))
                        split_to(last_block(("fu", layer, f)) + HL - 1)
                        if f == f0 and n:
                            act.wait_ge(S("block_used"), last_block(("fd", layer, n - 1, DC - 1)) + 1)
                        y_hi(YH[:, f - f0, :])
                    if n < len(PASS) - 1:
                        for c in range(DC):
                            split_to(last_block(("fd", layer, n, c)) + HL - 1)
                x_norm(("g_ple", DC * layer), behind=lambda c: ("fd", layer, len(PASS) - 1, c))

            def embed(layer):
                act.wait_ge(S("ple_in"), 16 * (layer + 1))
                for c in range(2):
                    nc.scalar.activation(PH[:, c, :], PR[:, c, :], ACT.Copy).then_inc(S("ple_hi_made"), t.made("ple_hi_made"))
                split_to(last_block(("pg", layer, 0)) + HL - 1)
                norm_root(SIGMOID)
                for c in range(DC):
                    split_to(last_block(("pg", layer, c)) + HL - 1)
                    act.wait_ge(S("pre"), t.next("pre"))
                    nc.scalar.activation(TMP[:, c % 2, :], TMP[:, c % 2, :], ACT.Sigmoid).then_inc(S("gate_made"), t.made("gate_made"))
                    split_to(last_block(("pp", layer, c)) + HL - 1)
                    if layer == 0:
                        norm_part(c, ("g_mix", DC), YH)

            feed_forward(0)
            embed(0)
            act.dma_start(POS[:], pos).then_inc(S("pos_in"), 16)
            split_to(last_block(("ql", 0)) + HL - 1)
            norm_root(SILU)
            act.wait_ge(S("angle_made"), t.next("angle_made"))
            nc.scalar.activation(SIN[:, :], TMP[:, 3, :], ACT.Sin).then_inc(S("act_step"), t.made("act_step"))
            nc.scalar.activation(TMP[:, 3, :], TMP[:, 3, :], ACT.Abs).then_inc(S("act_step"), t.made("act_step"))
            act.wait_ge(S("act_step"), t.last("act_step"))
            nc.scalar.activation(COS[:, :], TMP[:, 3, :], ACT.Sin, scale=-1.0, bias=col("halfpi")).then_inc(S("rotary_made"), t.made("rotary_made"))
            tables(LOG_EXP)

            def latent_squares(chunks):
                for c in chunks:
                    split_to(last_block(("ql", c) if c < 3 else ("kvl", c - 3)) + HL - 1)
                    act.wait_ge(S("lat_made"), t.next("lat_made"))
                    act.wait_ge(S("sq_taken"), t.next("sq_taken"))
                    nc.scalar.activation(SQ[:, c % 2, :], LAT[:, c, :], ACT.Square).then_inc(S("sq_made"), t.made("sq_made"))

            def latent_root(width):
                act.wait_ge(S("ssum_done"), t.next("ssum_done"))
                inverse_root(STD[:, :], PS[:, 4, :], width, "lat_rstd_made")

            def head_square(m):
                u, c, rows, _ = HEADS[m]
                if m:
                    split_to(last_block((u, c)) + HL - 1)
                act.wait_ge(S("head_raw"), t.next("head_raw"))
                if m >= 2:
                    act.wait_ge(S("head_taken"), t.next("head_taken"))
                r = 32 if m == 0 else 128
                src = SMALL[0:32, :] if m == 0 else TMP[:, m % 2, :]
                nc.scalar.activation(SQ[0:r, m % 2, :], src, ACT.Square).then_inc(S("head_sq_made"), t.made("head_sq_made"))

            def head_root(m):
                _, _, rows, _ = HEADS[m]
                r = 32 if m == 0 else 128
                act.wait_ge(S("head_summed"), t.next("head_summed"))
                inverse_root(SQ[0:r, m % 2, :], PS[0:r, 5 + m % 2, :], rows, "head_rstd_made", rows=slice(0, r))

            latent_squares(range(3))
            split_to(last_block(("kvl", 1)) + HL - 2)
            latent_root(384)
            latent_squares(range(3, 5))
            split_to(last_block(("small", 0)) + HL - 1)
            latent_root(256)
            head_square(0)
            for c in range(5):
                act.wait_ge(S("lat_normed"), t.next("lat_normed"))
                nc.scalar.activation(LH[:, c, :], LAT[:, c, :], ACT.Copy).then_inc(S("lat_hi_made"), t.made("lat_hi_made"))
            split_to(last_block(("mq", 0)) + HL - 1)
            head_root(0)
            act.wait_ge(S("gate_rows_made"), t.next("gate_rows_made"))
            nc.scalar.activation(G_ROW, F_ROW, ACT.Abs).then_inc(S("act_step"), t.made("act_step"))
            act.wait_ge(S("act_step"), t.last("act_step"))
            nc.scalar.activation(G_ROW, G_ROW, ACT.Exp, scale=-1.0).then_inc(S("act_step"), t.made("act_step"))
            act.wait_ge(S("act_step"), t.last("act_step"))
            nc.scalar.activation(G_ROW, G_ROW, ACT.Ln, bias=1.0).then_inc(S("softplus_made"), t.made("softplus_made"))
            split_to(last_block(("mq", 1)) + HL - 1)
            for g in range(2):
                if g == 0:
                    act.wait_ge(S("cols_made"), t.next("cols_made"))
                for i in range(QT):
                    b = bank(("mv", g), i)
                    tile_result(("mv", g), i)
                    nc.scalar.activation(MV[:, i, 256 * g:256 * g + 256], PS[:, b, 0:256], ACT.Copy,
                                         scale=RC[:, i:i + 1]).then_inc(acc_free[b], 1)
                if g == 0:
                    act.wait_ge(S("kr_made"), t.next("kr_made"))
                    for h in range(8):
                        ins = nc.scalar.activation(KF[64:96, h, :], TMP[0:32, 2, :], ACT.Copy)
                    ins.then_inc(S("kr_kept"), t.made("kr_kept"))
            for m in range(1, len(HEADS)):
                head_square(m)
                if m == 1:
                    act.wait_ge(S("rows_made"), t.next("rows_made"))
                    nc.scalar.activation(F_ROW, F_ROW, ACT.Exp, scale=-1.0).then_inc(S("floor_made"), t.made("floor_made"))
                else:
                    head_root(m - 1)
            head_root(len(HEADS) - 1)
            for g in range(2):
                for i in range(QT):
                    b = bank(("va", g), i)
                    tile_result(("va", g), i)
                    nc.scalar.activation(VA[:, i, 256 * g:256 * g + 256], PS[:, b, 0:256], ACT.Copy).then_inc(acc_free[b], 1)

            def d_exp(n):
                h, i = DTILES[n]
                w = 128 * (i + 1)
                act.wait_ge(S("d_max_ready"), t.next("d_max_ready"))
                nc.scalar.activation(PD[:, n % 4, 0:w], PS[:, SBANK[n % 4], 0:w], ACT.Exp,
                                     bias=NEGM[:, n % 4:n % 4 + 1], accum_out=SUM[:, n % 4:n % 4 + 1]).then_inc(S("d_exp_made"), t.made("d_exp_made"))

            def d_keep(n):
                h, i = DTILES[n]
                w = 128 * (i + 1)
                act.wait_ge(S("d_turned"), t.next("d_turned"))
                nc.scalar.activation(PTD[:, n % 2, 0:w], PS[:, 6 + n % 2, 0:w], ACT.Copy).then_inc(S("d_turn_kept"), t.made("d_turn_kept"))
                if n % 8 == 1 and n > 1:
                    d_hi(n // 8 - 1)

            def d_hi(c):
                act.wait_ge(S("d_mixed"), t.next("d_mixed"))
                nc.scalar.activation(YH[:, c, :], PS[:, 2 + c % 2, :], ACT.Copy).then_inc(S("y_hi_made"), t.made("y_hi_made"))

            for n in range(len(DTILES)):
                d_exp(n)
                if n >= 3:
                    d_keep(n - 3)
            for n in range(len(DTILES) - 3, len(DTILES)):
                d_keep(n)
            d_hi(3)

            tables(SIGMOID)
            for c in range(4):
                act.wait_ge(S("mo_raw"), t.next("mo_raw"))
                nc.scalar.activation(MO[:, c, :], MO[:, c, :], ACT.Sigmoid).then_inc(S("gate_made"), t.made("gate_made"))
            tables(LOG_EXP)

            def denominator(h):
                act.wait_ge(S("m_added"), t.next("m_added", 4))
                nc.scalar.activation(TMP[:, 0, :], PS[:, M_DEN, :], ACT.Abs).then_inc(S("den_abs"), t.made("den_abs"))
                nc.scalar.activation(SQ[:, h % 2, :], PS[:, M_NUM[h % 2], :], ACT.Square).then_inc(S("num_squared"), t.made("num_squared"))

            def h_root(h):
                act.wait_ge(S("h_sq_summed"), t.next("h_sq_summed"))
                sq = SQ[:, h % 2, :]
                nc.scalar.activation(sq, PS[:, M_FLOOR, :], ACT.Ln, scale=1.0 / 128).then_inc(S("act_step"), t.made("act_step"))
                act.wait_ge(S("act_step"), t.last("act_step"))
                nc.scalar.activation(sq, sq, ACT.Exp, scale=-0.5).then_inc(S("h_rstd_made"), t.made("h_rstd_made"))

            for k in range(16):
                act.wait_ge(S("decay_pre"), t.next("decay_pre"))
                w = T - 128 * (k % 4)
                nc.scalar.activation(WT[:, k % 4, 0:w], WT[:, k % 4, 0:w], ACT.Exp).then_inc(S("decay_made"), t.made("decay_made"))
                if k % 4 == 2 and k > 4:
                    denominator(k // 4 - 1)
                if k % 4 == 3 and k > 4:
                    h_root(k // 4 - 1)
                if k % 4 == 2 and k > 8:
                    y_hi(YH[:, 4 + k // 4 - 2, :])
            denominator(3)
            y_hi(YH[:, 6, :])
            h_root(3)
            y_hi(YH[:, 7, :])
            x_norm(("g_ffn", DC), behind=lambda c: ("mixout", 1, c))
            feed_forward(1)
            embed(1)

        @block.vector
        def _(dve):
            t = Tally()

            def unit(u):
                dve.wait_ge(S("block_used"), last_block(u) + 1)

            def free(ins, u, tile=0):
                ins.then_inc(acc_free[bank(u, tile)], 1)

            def free_after(name, u):
                dve.wait_ge(S(name), t.last(name))
                dve.sem_inc(acc_free[bank(u)], 1)

            def sum_squares(c, n=T, first=0, acc=SSQ):
                dve.wait_ge(S("sq_made"), t.next("sq_made"))
                if c == first:
                    ins = nc.vector.tensor_copy(acc[:, 0:n], SQ[:, c % 2, 0:n])
                else:
                    dve.wait_ge(S("sq_taken"), t.n["sq_taken"])
                    ins = nc.vector.tensor_tensor(acc[:, 0:n], acc[:, 0:n], SQ[:, c % 2, 0:n], ALU.add)
                ins.then_inc(S("sq_taken"), t.made("sq_taken"))

            def lo_part(c, lo, src, g, hi):
                dve.wait_ge(S("xg_hi_made"), t.next("xg_hi_made"))
                nc.vector.scalar_tensor_tensor(lo, src, g, hi.bitcast(F32), ALU.mult, ALU.subtract).then_inc(S("xg_lo_made"), t.made("xg_lo_made"))

            def norm_rows():
                dve.wait_ge(S("rstd_made"), t.next("rstd_made"))

            dve.wait_ge(S("vec_in"), 16)
            for c in range(DC):
                if c % 2 == 0:
                    dve.wait_ge(S(f"mem_in{c // 2}"), 16)
                sum_squares(c, NMEM, acc=TMP[:, 0, :])
                lo_part(c, ML[:, c, :], MEMX[:, c, :], col("mem_norm_g", c), MH[:, c, :])
            def first_chunk(c):
                if c % 2 == 0:
                    dve.wait_ge(S(f"x_in{c // 2}"), 16)
                sum_squares(c)
                lo_part(c, XL[:, c, :], X[:, c, :], col("norm_g", c), XH[:, c, :])

            for c in range(5):
                first_chunk(c)
            norm_rows()
            for c in range(2):
                unit(("km", c))
                free(nc.vector.tensor_tensor(KM[:, c, :], PS[:, bank(("km", c)), 0:NMEM], RBM[:, :], ALU.mult),
                     ("km", c))
            for c in range(5, DC):
                first_chunk(c)
            dve.wait_ge(S("cols_summed"), t.next("cols_summed"))
            nc.vector.tensor_copy(RC[:, 12:14], PS[:, 7, 12:14]).then_inc(S("cols_made"), t.made("cols_made"))
            norm_rows()
            for c in range(6):
                unit(("q", c))
                g = c // 2
                free(nc.vector.tensor_tensor(residue(Q[:, c, :], 0) if g == 0 else Q[:, c, :].rearrange("p (r u) -> p r u", r=ORDER[g]),
                                             residue(PS[:, bank(("q", c)), :], g), residue(RB[:, :], g), ALU.mult), ("q", c))
            for c in range(2):
                unit(("qm", c))
                nc.vector.tensor_tensor(QM[:, c, :], PS[:, bank(("qm", c)), :], RB[:, :], ALU.mult).then_inc(S("qk_ready"), t.made("qk_ready"))
                free_after("qk_ready", ("qm", c))
            dve.wait_ge(S("cols_summed"), t.next("cols_summed"))
            nc.vector.tensor_copy(RC[:, 0:12], PS[:, 7, 0:12]).then_inc(S("cols_made"), t.made("cols_made"))
            for c in range(6):
                unit(("k", c))
                g = c // 2
                free(nc.vector.tensor_tensor(K[:, c, :] if g == 0 else K[:, c, :].rearrange("p (r u) -> p r u", r=ORDER[g]),
                                             residue(PS[:, bank(("k", c)), :], g), residue(RB[:, :], g), ALU.mult), ("k", c))

            def scores(n):
                g, i = TILES[n]
                w, _ = keys(g, i)
                dve.wait_ge(S("scored"), t.next("scored"))
                if n >= 4:
                    dve.wait_ge(S("turned"), TURNED[n - 4])
                s = sbuf(n)[:, :, 0:w]
                psum = PS[:, SPAIR[n % 2]:SPAIR[n % 2] + 2, 0:2 * w]
                if g == 3:
                    nc.vector.tensor_copy(sbuf(n).rearrange("p (a b) k -> p a (b k)", a=2), psum).then_inc(S("dve_step"), t.made("dve_step"))
                    dve.wait_ge(S("dve_step"), t.last("dve_step"))
                elif w == 256:
                    b = BIAS[:, 0:2, :]
                    nc.vector.scalar_tensor_tensor(sbuf(n).rearrange("p (a b) k -> p a (b k)", a=2), psum,
                                                   0.125, b, ALU.mult, ALU.add).then_inc(S("dve_step"), t.made("dve_step"))
                    dve.wait_ge(S("dve_step"), t.last("dve_step"))
                else:
                    for par in range(2):
                        if g == 0:
                            b = BIAS[:, par, :].rearrange("p (b k) -> p b k", b=2)[:, :, 128:256]
                        else:
                            b = BIAS[:, 1 + g, 256 * par:256 * par + 256].rearrange("p (b k) -> p b k", b=2)
                        ins = nc.vector.scalar_tensor_tensor(
                            sbuf(n)[:, 2 * par:2 * par + 2, 0:128],
                            PS[:, SPAIR[n % 2] + par, 0:256].rearrange("p (b k) -> p b k", b=2), 0.125, b, ALU.mult, ALU.add)
                        ins.then_inc(S("dve_step"), t.made("dve_step"))
                    dve.wait_ge(S("dve_step"), t.last("dve_step"))
                nc.vector.tensor_reduce(NEGM[:, 4 * (n % 4):4 * (n % 4) + 4], s, AX.X, ALU.max, negate=True).then_inc(S("dve_step"), t.made("dve_step"))
                dve.wait_ge(S("dve_step"), t.last("dve_step"))
                if g == 3:
                    ins = nc.vector.tensor_scalar(NEGM[:, 4 * (n % 4):4 * (n % 4) + 4], NEGM[:, 4 * (n % 4):4 * (n % 4) + 4],
                                                  0.125, None, ALU.mult)
                else:
                    ins = nc.vector.tensor_scalar(STAT[:, g, i, :, 0], NEGM[:, 4 * (n % 4):4 * (n % 4) + 4],
                                                  -1.0, None, ALU.mult)
                ins.then_inc(S("scores_ready"), t.made("scores_ready"))

            def normalise(n):
                g, i = TILES[n]
                dve.wait_ge(S("probs_made"), t.next("probs_made"))
                if g != 3:
                    return
                r = SUM[:, 4 * (n % 4):4 * (n % 4) + 4]
                nc.vector.reciprocal(r, r).then_inc(S("dve_step"), t.made("dve_step"))
                dve.wait_ge(S("dve_step"), t.last("dve_step"))
                s = sbuf(n)
                nc.vector.tensor_tensor(s, s, r.unsqueeze(2).broadcast_to([128, 4, 256]), ALU.mult).then_inc(S("probs_normal"), t.made("probs_normal"))

            nc.vector.tensor_scalar(QGAIN[:, :], VECT[:, VEC["g_qn"]:VEC["g_qn"] + 2], DSCALE, None, ALU.mult).then_inc(S("dve_step"), t.made("dve_step"))
            nc.vector.tensor_tensor(GAIN2[:, :], VECT[:, VEC["final_g"]:VEC["final_g"] + DC],
                                    VECT[:, VEC["g_mix"]:VEC["g_mix"] + DC], ALU.mult).then_inc(S("gains_made"), t.made("gains_made"))
            dve.wait_ge(S("gains_made"), t.last("gains_made"))
            dve.wait_ge(S("bias_in"), 16)
            dve.wait_ge(S("const_rest_in"), 16)
            for n in range(len(TILES)):
                scores(n)
                if n >= 1:
                    normalise(n - 1)
            normalise(len(TILES) - 1)

            dve.wait_ge(S("mix_kept"), t.next("mix_kept", len(TILES)))
            for n in range(6):
                dve.wait_ge(S("stat_turned"), t.next("stat_turned"))
                g = n % 3
                src, dst = PS[0:4, 4 + n % 2, :], ROWS[:, n, :]
                if g:
                    src = src.rearrange("p (r u) -> p r u", r=ORDER[g])
                    dst = dst.rearrange("p (u r) -> p r u", r=ORDER[g])
                nc.vector.tensor_copy(dst, src).then_inc(S("stat_kept"), t.made("stat_kept"))
            dve.wait_ge(S("stat_kept"), t.last("stat_kept"))
            top_row = SQ[0:4, 0, :]
            nc.vector.tensor_tensor(top_row, ROWS[:, 0, :], ROWS[:, 1, :], ALU.max).then_inc(S("dve_step"), t.made("dve_step"))
            dve.wait_ge(S("dve_step"), t.last("dve_step"))
            nc.vector.tensor_tensor(top_row, top_row, ROWS[:, 2, :], ALU.max).then_inc(S("dve_step"), t.made("dve_step"))
            dve.wait_ge(S("dve_step"), t.last("dve_step"))
            for g in range(3):
                ins = nc.vector.tensor_tensor(ROWS[:, g, :], ROWS[:, g, :], top_row, ALU.subtract)
            ins.then_inc(S("row_max_ready"), t.made("row_max_ready"))
            dve.wait_ge(S("row_exp"), t.next("row_exp"))
            for g in range(3):
                nc.vector.tensor_tensor(ROWS[:, 3 + g, :], ROWS[:, 3 + g, :], ROWS[:, g, :], ALU.mult).then_inc(S("dve_step"), t.made("dve_step"))
                dve.wait_ge(S("dve_step"), t.last("dve_step"))
            nc.vector.tensor_tensor(top_row, ROWS[:, 3, :], ROWS[:, 4, :], ALU.add).then_inc(S("dve_step"), t.made("dve_step"))
            dve.wait_ge(S("dve_step"), t.last("dve_step"))
            nc.vector.tensor_tensor(top_row, top_row, ROWS[:, 5, :], ALU.add).then_inc(S("dve_step"), t.made("dve_step"))
            dve.wait_ge(S("dve_step"), t.last("dve_step"))
            nc.vector.reciprocal(top_row, top_row).then_inc(S("dve_step"), t.made("dve_step"))
            dve.wait_ge(S("dve_step"), t.last("dve_step"))
            for g in range(3):
                ins = nc.vector.tensor_tensor(ROWS[:, g, :], ROWS[:, g, :], top_row, ALU.mult)
                ins.then_inc(S("row_weight"), t.made("row_weight"))

            def y_lo(dst, hi):
                dve.wait_ge(S("y_hi_made"), t.next("y_hi_made"))
                nc.vector.tensor_tensor(dst, TMP[:, 2 + (t.n["y_hi_made"] - 1) % 2, :], hi.bitcast(F32),
                                        ALU.subtract).then_inc(S("y_lo_made"), t.made("y_lo_made"))

            def ytmp():
                return TMP[:, 2 + t.n.get("y_made", 0) % 2, :]

            for c in range(DC):
                u = ("gate", c)
                unit(u)
                ins = nc.vector.tensor_tensor(TMP[:, c % 2, :], PS[:, bank(u), :], RB[:, :], ALU.mult)
                ins.then_inc(S("pre"), t.made("pre"))
                free_after("pre", u)
                if c < 6:
                    dve.wait_ge(S("weight_spread"), t.next("weight_spread"))
                    nc.vector.tensor_tensor(ytmp(), MIXT[:, c, :], PS[:, 4 + c % 2, :], ALU.mult).then_inc(S("weight_used"), t.made("weight_used"))
                    dve.wait_ge(S("weight_used"), t.last("weight_used"))
                    dve.wait_ge(S("gate_made"), t.next("gate_made"))
                    nc.vector.tensor_tensor(ytmp(), ytmp(), TMP[:, c % 2, :], ALU.mult).then_inc(S("y_made"), t.made("y_made"))
                else:
                    dve.wait_ge(S("gate_made"), t.next("gate_made"))
                    nc.vector.tensor_tensor(ytmp(), MIXT[:, c, :], TMP[:, c % 2, :], ALU.mult).then_inc(S("y_made"), t.made("y_made"))
                dve.wait_ge(S("y_made"), t.last("y_made"))
                y_lo(YL[:, c, :], YH[:, c, :])

            def residual(names, gain):
                for c in range(DC + 1):
                    if c < DC:
                        u = names(c)
                        unit(u)
                        nc.vector.tensor_tensor(X[:, c, :], X[:, c, :], PS[:, bank(u), :], ALU.add).then_inc(S("x_final"), t.made("x_final"))
                        free_after("x_final", u)
                    if c > 0:
                        norm_chunk(c - 1, gain)

            def norm_chunk(c, gain, hi=XH, lo=XL):
                sum_squares(c)
                lo_part(c, lo[:, c, :], X[:, c, :], col(gain[0], gain[1] + c), hi[:, c, :])

            def two_sums(c):
                for i in range(2):
                    acc = (SSQ, TMP[:, 0, :])[i]
                    dve.wait_ge(S("sq_made"), t.next("sq_made"))
                    if c == 0:
                        ins = nc.vector.tensor_copy(acc[:, :], SQ[:, i, :])
                    else:
                        dve.wait_ge(S("sq_taken"), t.n["sq_taken"] - 1)
                        ins = nc.vector.tensor_tensor(acc[:, :], acc[:, :], SQ[:, i, :], ALU.add)
                    ins.then_inc(S("sq_taken"), t.made("sq_taken"))
                lo_part(c, XL[:, c, :], X[:, c, :], GAIN2[:, c:c + 1], XH[:, c, :])

            for c in range(DC + 1):
                if c < DC:
                    u = ("out", c)
                    unit(u)
                    nc.vector.tensor_tensor(X[:, c, :], X[:, c, :], PS[:, bank(u), :], ALU.add).then_inc(S("x_final"), t.made("x_final"))
                    free_after("x_final", u)
                if c > 0:
                    two_sums(c - 1)
            dve.wait_ge(S("r1_made"), t.next("r1_made"))
            nc.vector.tensor_tensor(TMP[:, 1, :], PS[:, 5, :], STD[:, :], ALU.mult).then_inc(S("dve_step"), t.made("dve_step"))
            dve.wait_ge(S("dve_step"), t.last("dve_step"))
            nc.vector.tensor_tensor(TMP[:, 1, :], TMP[:, 1, :], STD[:, :], ALU.mult).then_inc(S("mean2_made"), t.made("mean2_made"))
            for c in range(DC):
                nc.vector.scalar_tensor_tensor(X[:, c, :], X[:, c, :], col("final_g", c), STD[:, :],
                                               ALU.mult, ALU.mult).then_inc(S("dve_step"), t.made("dve_step"))
                if c == 2:
                    dve.wait_ge(S("r2_made"), t.next("r2_made"))
                    nc.vector.tensor_tensor(RB[:, :], TMP[:, 1, :], STD[:, :], ALU.mult).then_inc(S("late_made"), t.made("late_made"))
            dve.wait_ge(S("dve_step"), t.last("dve_step"))
            dve.wait_ge(S("late_made"), t.last("late_made"))
            for c in range(4):
                u = ("cc", c)
                unit(u)
                nc.vector.tensor_tensor(TMP[:, 0, :], PS[:, bank(u), :], RB[:, :], ALU.mult).then_inc(S("dve_step"), t.made("dve_step"))
                dve.wait_ge(S("dve_step"), t.last("dve_step"))
                free_after("dve_step", u)
                u = ("cx", c)
                unit(u)
                nc.vector.tensor_tensor(TMP[:, 1, :], PS[:, bank(u), :], RB[:, :], ALU.mult).then_inc(S("dve_step"), t.made("dve_step"))
                dve.wait_ge(S("dve_step"), t.last("dve_step"))
                free_after("dve_step", u)
                nc.vector.tensor_tensor(TMP[:, 0, :], TMP[:, 0, :], TMP[:, 1, :], ALU.mult).then_inc(S("dve_step"), t.made("dve_step"))
                dve.wait_ge(S("dve_step"), t.last("dve_step"))
                nc.vector.tensor_scalar(TMP[:, 1, :], TMP[:, 0, :], col("conv", 8 + c), None, ALU.mult).then_inc(S("dve_step"), t.made("dve_step"))
                dve.wait_ge(S("dve_step"), t.last("dve_step"))
                for tap in (1, 0):
                    d = 2 - tap
                    nc.vector.scalar_tensor_tensor(TMP[:, 1, d:T], TMP[:, 0, 0:T - d], col("conv", 4 * tap + c),
                                                   TMP[:, 1, d:T], ALU.mult, ALU.add).then_inc(S("dve_step"), t.made("dve_step"))
                    dve.wait_ge(S("dve_step"), t.last("dve_step"))
                u = ("cb", c)
                unit(u)
                nc.vector.tensor_tensor(TMP[:, 0, :], PS[:, bank(u), :], RB[:, :], ALU.mult).then_inc(S("dve_step"), t.made("dve_step"))
                dve.wait_ge(S("dve_step"), t.last("dve_step"))
                free_after("dve_step", u)
                nc.vector.tensor_tensor(ytmp(), TMP[:, 0, :], TMP[:, 1, :], ALU.mult).then_inc(S("y_made"), t.made("y_made"))
                if c == 0:
                    dve.wait_ge(S("cols_summed"), t.next("cols_summed"))
                    nc.vector.tensor_copy(RC[:, 0:4], PS[:, 7, 0:4]).then_inc(S("cols_made"), t.made("cols_made"))
                y_lo(YL[:, c, :], YH[:, c, :])
            dve.wait_ge(S("ws_in"), 16)
            nc.vector.tensor_tensor(WS[:, :, :], WS[:, :, :],
                                    const("upto", at=384).unsqueeze(1).broadcast_to([128, 8, 128]), ALU.mult).then_inc(S("ws_masked"), t.made("ws_masked"))
            for i in range(QT):
                for g in range(2):
                    dve.wait_ge(acc_free[bank(("gv", g), i)], freed(("gv", g), i))
                nc.vector.tensor_tensor(SV[:, :], GV[:, i, :], GV[:, i, :], ALU.mult).then_inc(S("dve_step"), t.made("dve_step"))
                dve.wait_ge(S("dve_step"), t.last("dve_step"))
                ins = nc.vector.tensor_reduce(SS[:, i, :], SV[:, :].rearrange("p (h d) -> p h d", h=8), AX.X, ALU.add)
                if i < QT - 1:
                    ins.then_inc(S("dve_step"), t.made("dve_step"))
                    dve.wait_ge(S("dve_step"), t.last("dve_step"))
                else:
                    ins.then_inc(S("gv_summed"), t.made("gv_summed"))
            dve.wait_ge(S("gv_rstd_made"), t.next("gv_rstd_made"))
            dve.wait_ge(S("gv_in"), 16)
            for i in range(QT):
                v = GV[:, i, :].rearrange("p (h d) -> p h d", h=8)
                nc.vector.tensor_tensor(v, v, SS[:, i, :].unsqueeze(2).broadcast_to([128, 8, 64]), ALU.mult).then_inc(S("dve_step"), t.made("dve_step"))
                dve.wait_ge(S("dve_step"), t.last("dve_step"))
                nc.vector.tensor_tensor(GV[:, i, :], GV[:, i, :], GVB[:, :], ALU.mult).then_inc(S("gv_normed"), t.made("gv_normed"))
            dve.wait_ge(S("bs_in"), 16)
            for c in range(4):
                dve.wait_ge(S("spatial_done"), t.next("spatial_done"))
                m = MB[:, c, :].rearrange("p (n k) -> p n k", n=QT)
                nc.vector.tensor_tensor(m, PS[:, 4 + c, :].rearrange("p (n k) -> p n k", n=QT),
                                        BS[:, c, :].unsqueeze(1).broadcast_to([128, QT, 128]), ALU.add).then_inc(S("dve_step"), t.made("dve_step"))
            for c in range(4):
                u = ("gu", c)
                unit(u)
                nc.vector.tensor_tensor(TMP[:, c % 2, :], PS[:, bank(u), :], RB[:, :], ALU.mult).then_inc(S("pre"), t.made("pre"))
                free_after("pre", u)
                dve.wait_ge(S("gate_made"), t.next("gate_made"))
                nc.vector.tensor_tensor(ytmp(), TMP[:, c % 2, :], MB[:, c, :], ALU.mult).then_inc(S("y_made"), t.made("y_made"))
                dve.wait_ge(S("y_made"), t.last("y_made"))
                y_lo(YL[:, 4 + c, :], YH[:, 4 + c, :])
            residual(lambda c: ("mixout", 0, c), ("g_ffn", 0))

            def feed_forward(layer):
                norm_rows()
                for n, (f0, fn) in enumerate(PASS):
                    for f in range(f0, f0 + fn):
                        u = ("fg", layer, f)
                        unit(u)
                        nc.vector.tensor_tensor(TMP[:, f % 2, :], PS[:, bank(u), :], RB[:, :], ALU.mult).then_inc(S("pre"), t.made("pre"))
                        free_after("pre", u)
                        u = ("fu", layer, f)
                        unit(u)
                        nc.vector.tensor_tensor(ytmp(), PS[:, bank(u), :], RB[:, :], ALU.mult).then_inc(S("dve_step"), t.made("dve_step"))
                        dve.wait_ge(S("dve_step"), t.last("dve_step"))
                        free_after("dve_step", u)
                        dve.wait_ge(S("gate_made"), t.next("gate_made"))
                        nc.vector.tensor_tensor(ytmp(), ytmp(), TMP[:, f % 2, :], ALU.mult).then_inc(S("y_made"), t.made("y_made"))
                        dve.wait_ge(S("y_made"), t.last("y_made"))
                        y_lo(YL[:, f - f0, :], YH[:, f - f0, :])
                    if n < len(PASS) - 1:
                        for c in range(DC):
                            u = ("fd", layer, n, c)
                            unit(u)
                            nc.vector.tensor_tensor(X[:, c, :], X[:, c, :], PS[:, bank(u), :], ALU.add).then_inc(S("dve_step"), t.made("dve_step"))
                            dve.wait_ge(S("dve_step"), t.last("dve_step"))
                            free_after("dve_step", u)
                residual(lambda c: ("fd", layer, len(PASS) - 1, c), ("g_ple", DC * layer))

            def embed(layer):
                for c in range(2):
                    dve.wait_ge(S("ple_hi_made"), t.next("ple_hi_made"))
                    nc.vector.tensor_tensor(PL[:, c, :], PR[:, c, :], PH[:, c, :].bitcast(F32), ALU.subtract).then_inc(S("ple_lo_made"), t.made("ple_lo_made"))
                norm_rows()
                for c in range(DC):
                    u = ("pg", layer, c)
                    unit(u)
                    nc.vector.tensor_tensor(TMP[:, c % 2, :], PS[:, bank(u), :], RB[:, :], ALU.mult).then_inc(S("pre"), t.made("pre"))
                    free_after("pre", u)
                    u = ("pp", layer, c)
                    unit(u)
                    dve.wait_ge(S("gate_made"), t.next("gate_made"))
                    nc.vector.tensor_tensor(TMP[:, c % 2, :], TMP[:, c % 2, :], PS[:, bank(u), :], ALU.mult).then_inc(S("dve_step"), t.made("dve_step"))
                    dve.wait_ge(S("dve_step"), t.last("dve_step"))
                    free_after("dve_step", u)
                    nc.vector.tensor_tensor(X[:, c, :], X[:, c, :], TMP[:, c % 2, :], ALU.add).then_inc(S("x_final"), t.made("x_final"))
                    if layer == 0 and c:
                        norm_chunk(c - 1, ("g_mix", DC), YH, YL)

            feed_forward(0)
            embed(0)
            norm_chunk(DC - 1, ("g_mix", DC), YH, YL)
            norm_rows()
            dve.wait_ge(S("pos_in"), 16)
            nc.vector.tensor_copy(TMP[:, 2, :], POS[:, :]).then_inc(S("dve_step"), t.made("dve_step"))
            dve.wait_ge(S("dve_step"), t.last("dve_step"))
            nc.vector.tensor_scalar(TMP[:, 3, :], TMP[:, 2, :], col("inv_freq"), None, ALU.mult).then_inc(S("dve_step"), t.made("dve_step"))
            dve.wait_ge(S("dve_step"), t.last("dve_step"))
            nc.vector.tensor_scalar(TMP[:, 2, :], TMP[:, 3, :], float(1 / (2 * np.pi)), ROUND, ALU.mult, ALU.add).then_inc(S("dve_step"), t.made("dve_step"))
            dve.wait_ge(S("dve_step"), t.last("dve_step"))
            nc.vector.tensor_scalar(TMP[:, 2, :], TMP[:, 2, :], ROUND, None, ALU.subtract).then_inc(S("dve_step"), t.made("dve_step"))
            dve.wait_ge(S("dve_step"), t.last("dve_step"))
            for part in TWO_PI:
                nc.vector.scalar_tensor_tensor(TMP[:, 3, :], TMP[:, 2, :], -part, TMP[:, 3, :], ALU.mult, ALU.add).then_inc(S("dve_step"), t.made("dve_step"))
                dve.wait_ge(S("dve_step"), t.last("dve_step"))
            nc.vector.tensor_scalar(TMP[:, 3, :], TMP[:, 3, :], PI_BELOW, -PI_BELOW, ALU.min, ALU.max).then_inc(S("angle_made"), t.made("angle_made"))

            def latent(c):
                u = ("ql", c) if c < 3 else ("kvl", c - 3)
                unit(u)
                nc.vector.tensor_tensor(LAT[:, c, :], PS[:, bank(u), :], RB[:, :], ALU.mult).then_inc(S("lat_made"), t.made("lat_made"))
                free_after("lat_made", u)

            def latent_norm(chunks, gain):
                dve.wait_ge(S("lat_rstd_made"), t.next("lat_rstd_made"))
                for n, c in enumerate(chunks):
                    nc.vector.scalar_tensor_tensor(LAT[:, c, :], LAT[:, c, :], col(gain, n), STD[:, :],
                                                   ALU.mult, ALU.mult).then_inc(S("lat_normed"), t.made("lat_normed"))
                dve.wait_ge(S("lat_normed"), t.last("lat_normed"))

            latent(0)
            latent(1)
            sum_squares(0)
            latent(2)
            sum_squares(1)
            sum_squares(2)
            latent(3)
            latent(4)
            latent_norm(range(3), "g_qa")
            sum_squares(3, first=3)
            sum_squares(4, first=3)
            u = ("small", 0)
            unit(u)
            nc.vector.tensor_tensor(SMALL[:, :], PS[:, bank(u), :], RB[:, :], ALU.mult).then_inc(S("head_raw"), t.made("head_raw"))
            free_after("head_raw", u)
            nc.vector.tensor_scalar(GR[:, 0, :], SMALL[32:36, :], col("b_i", rows=slice(32, 36)), None, ALU.add).then_inc(S("dve_step"), t.made("dve_step"))
            nc.vector.tensor_scalar(GR[:, 1, :], SMALL[64:68, :], col("b_f", rows=slice(64, 68)), None, ALU.add).then_inc(S("gate_rows_made"), t.made("gate_rows_made"))
            def head_raw(m):
                u, c, _, _ = HEADS[m]
                unit((u, c))
                if m >= 2:
                    dve.wait_ge(S("head_taken"), t.last("head_taken"))
                nc.vector.tensor_copy(TMP[:, m % 2, :], PS[:, bank((u, c)), :]).then_inc(S("head_raw"), t.made("head_raw"))
                free_after("head_raw", (u, c))

            def head_finish(m, meanwhile=None):
                u, c, rows, gain = HEADS[m]
                r = 32 if m == 0 else 128
                raw = SMALL[0:32, :] if m == 0 else TMP[:, m % 2, :]
                inv = SQ[0:r, m % 2, :]
                g = QGAIN[:, 0:1] if gain == "g_qn" else QGAIN[:, 1:2] if gain == "g_qr" else col(gain)
                dve.wait_ge(S("head_rstd_made"), t.next("head_rstd_made"))
                if rows == 64:
                    dst = QF if u == "qn" else KF
                    for par in range(2):
                        h = slice(64 * par, 64 * par + 64)
                        ins = nc.vector.scalar_tensor_tensor(dst[0:64, 2 * c + par, :], raw[h, :], g[h, :],
                                                             SQ[h, m % 2, :], ALU.mult, ALU.mult)
                        name = "head_taken" if par else "dve_step"
                        ins.then_inc(S(name), t.made(name))
                    return
                if m:
                    if c == 0:
                        dve.wait_ge(S("kr_kept"), t.next("kr_kept"))
                nc.vector.scalar_tensor_tensor(TMP[0:r, 2, :], raw, g[0:r, :], inv,
                                               ALU.mult, ALU.mult).then_inc(S("rope_in"), t.made("rope_in"))
                if meanwhile is not None:
                    meanwhile()
                dve.wait_ge(S("rot_done"), t.next("rot_done"))
                if m == 0:
                    dve.wait_ge(S("rotary_made"), t.next("rotary_made"))
                nc.vector.tensor_tensor(TMP[0:r, 3, :], PS[0:r, 7, :], SIN[0:r, :], ALU.mult).then_inc(S("dve_step"), t.made("dve_step"))
                dve.wait_ge(S("dve_step"), t.last("dve_step"))
                nc.vector.tensor_tensor(TMP[0:r, 2, :], TMP[0:r, 2, :], COS[0:r, :], ALU.mult).then_inc(S("dve_step"), t.made("dve_step"))
                dve.wait_ge(S("dve_step"), t.last("dve_step"))
                if m == 0:
                    nc.vector.tensor_tensor(TMP[0:32, 2, :], TMP[0:32, 2, :], TMP[0:32, 3, :], ALU.add).then_inc(S("kr_made"), t.made("kr_made"))
                    dve.wait_ge(S("kr_made"), t.last("kr_made"))
                    t.n["head_taken"] = 1
                    dve.sem_inc(S("head_taken"), 1)
                    return
                for k in range(4):
                    h = slice(32 * k, 32 * k + 32)
                    ins = nc.vector.tensor_tensor(QF[64:96, 4 * c + k, :], TMP[h, 2, :], TMP[h, 3, :], ALU.add)
                    name = "head_taken" if k == 3 else "dve_step"
                    ins.then_inc(S(name), t.made(name))
                dve.wait_ge(S("head_taken"), t.last("head_taken"))

            def rows_a():
                dve.wait_ge(S("softplus_made"), t.next("softplus_made"))
                nc.vector.scalar_tensor_tensor(F_ROW, F_ROW, 0.0, G_ROW, ALU.min, ALU.subtract).then_inc(S("lf_made"), t.made("lf_made"))

            def rows_b():
                dve.wait_ge(S("lf_turned"), t.next("lf_turned"))
                nc.vector.tensor_copy(LFC[:, 0, :, :], PS[:, 4, 0:16]).then_inc(S("lf_cols"), t.made("lf_cols"))

            def rows_c():
                dve.wait_ge(S("a_summed"), t.next("a_summed"))
                nc.vector.tensor_copy(A_ROW, PS[0:4, 5, :]).then_inc(S("dve_step"), t.made("dve_step"))
                dve.wait_ge(S("dve_step"), t.last("dve_step"))
                nc.vector.tensor_tensor(I_ROW, I_ROW, A_ROW, ALU.subtract).then_inc(S("b_made"), t.made("b_made"))
                dve.wait_ge(S("b_made"), t.last("b_made"))
                nc.vector.tensor_scalar(MAX_ROWS[0], I_ROW, 0.0, None, ALU.max).then_inc(S("dve_step"), t.made("dve_step"))
                dve.wait_ge(S("dve_step"), t.last("dve_step"))
                n, d = 0, 1
                while d < T:
                    src, dst = MAX_ROWS[n % 2], MAX_ROWS[1 - n % 2]
                    nc.vector.tensor_copy(dst[:, 0:d], src[:, 0:d]).then_inc(S("dve_step"), t.made("dve_step"))
                    nc.vector.tensor_tensor(dst[:, d:T], src[:, d:T], src[:, 0:T - d], ALU.max).then_inc(S("dve_step"), t.made("dve_step"))
                    dve.wait_ge(S("dve_step"), t.last("dve_step"))
                    n, d = n + 1, 2 * d
                nc.vector.tensor_scalar(G_ROW, MAX_ROWS[n % 2], -1.0, None, ALU.mult).then_inc(S("dve_step"), t.made("dve_step"))
                nc.vector.tensor_tensor(F_ROW, A_ROW, MAX_ROWS[n % 2], ALU.add).then_inc(S("rows_made"), t.made("rows_made"))
                dve.wait_ge(S("rows_made"), t.last("rows_made"))

            def rows_d():
                dve.wait_ge(S("b_turned"), t.next("b_turned"))
                nc.vector.tensor_copy(LFC[:, 1, :, :], PS[:, 6, 0:16]).then_inc(S("b_cols"), t.made("b_cols"))
                dve.wait_ge(S("b_cols"), t.last("b_cols"))

            latent_norm(range(3, 5), "g_kva")

            def factor_columns():
                dve.wait_ge(S("cols_summed"), t.next("cols_summed"))
                nc.vector.tensor_copy(RC[:, 0:4], PS[:, 7, 0:4]).then_inc(S("cols_made"), t.made("cols_made"))

            head_finish(0, factor_columns)
            for c in range(2):
                unit(("mq", c))
                free(nc.vector.tensor_tensor(MQ[:, c, :], PS[:, bank(("mq", c)), :], RB[:, :], ALU.mult), ("mq", c))
            for c in range(5):
                dve.wait_ge(S("lat_hi_made"), t.next("lat_hi_made"))
                nc.vector.tensor_tensor(LL[:, c, :], LAT[:, c, :], LH[:, c, :].bitcast(F32), ALU.subtract).then_inc(S("lat_lo_made"), t.made("lat_lo_made"))
            rows_a()
            rows_b()
            rows_c()

            def output_gate(c):
                u = ("mo", c)
                unit(u)
                nc.vector.tensor_tensor(MO[:, c, :], PS[:, bank(u), :], RB[:, :], ALU.mult).then_inc(S("mo_raw"), t.made("mo_raw"))
                free_after("mo_raw", u)

            for m in range(1, len(HEADS)):
                head_raw(m)
                if m == 1:
                    rows_d()
                else:
                    head_finish(m - 1)
                if m in BESIDE:
                    name, c = BESIDE[m]
                    if name == "mo":
                        output_gate(c)
                    else:
                        unit((name, c))
                        free(nc.vector.tensor_tensor(MK[:, c, :], PS[:, bank((name, c)), :], RB[:, :], ALU.mult), (name, c))
            head_finish(len(HEADS) - 1)
            dve.wait_ge(S("head_taken"), t.last("head_taken"))
            output_gate(3)
            def d_max(n):
                h, i = DTILES[n]
                w = 128 * (i + 1)
                dve.wait_ge(S("d_scored"), t.next("d_scored"))
                s = PS[:, SBANK[n % 4], :]
                nc.vector.tensor_reduce(NEGM[:, n % 4:n % 4 + 1], s[:, 0:w], AX.X, ALU.max, negate=True).then_inc(S("d_max_ready"), t.made("d_max_ready"))

            def d_norm(n):
                h, i = DTILES[n]
                w = 128 * (i + 1)
                dve.wait_ge(S("d_exp_made"), t.next("d_exp_made"))
                r = SUM[:, n % 4:n % 4 + 1]
                nc.vector.reciprocal(r, r).then_inc(S("dve_step"), t.made("dve_step"))
                dve.wait_ge(S("dve_step"), t.last("dve_step"))
                nc.vector.tensor_scalar(PD[:, n % 4, 0:w], PD[:, n % 4, 0:w], r, None, ALU.mult).then_inc(S("d_probs_made"), t.made("d_probs_made"))

            def d_lo(c):
                dve.wait_ge(S("y_hi_made"), t.next("y_hi_made"))
                nc.vector.tensor_tensor(YL[:, c, :], PS[:, 2 + c % 2, :], YH[:, c, :].bitcast(F32), ALU.subtract).then_inc(S("y_lo_made"), t.made("y_lo_made"))

            for n in range(len(DTILES)):
                d_max(n)
                if n >= 2:
                    d_norm(n - 2)
                if n % 8 == 6 and n > 6:
                    d_lo(n // 8 - 1)
            d_norm(len(DTILES) - 2)
            d_norm(len(DTILES) - 1)
            d_lo(3)

            def decay(k):
                h, b = k // 4, k % 4
                w = T - 128 * b
                if b == 0:
                    dve.wait_ge(S("g_spread"), t.next("g_spread"))
                nc.vector.tensor_scalar(WT[:, k % 4, 0:w], PS[:, M_G, 128 * b:T], LFC[:, 1, b, h:h + 1], 0.0,
                                        ALU.add, ALU.min).then_inc(S("decay_pre"), t.made("decay_pre"))

            def weigh(k):
                w = T - 128 * (k % 4)
                dve.wait_ge(S("decay_made"), t.next("decay_made"))
                nc.vector.tensor_tensor(WT[:, k % 4, 0:128], WT[:, k % 4, 0:128], const("upto", at=384), ALU.mult).then_inc(S("dve_step"), t.made("dve_step"))
                dve.wait_ge(S("dve_step"), t.last("dve_step"))
                dve.wait_ge(S("m_scored"), t.next("m_scored"))
                if k >= 4:
                    dve.wait_ge(S("m_added"), t.next("m_added"))
                nc.vector.scalar_tensor_tensor(SW[:, k % 4, 0:w], PS[:, M_S[k % 3], 0:w], 0.125, WT[:, k % 4, 0:w],
                                               ALU.mult, ALU.mult).then_inc(S("weighted_made"), t.made("weighted_made"))
                dve.wait_ge(S("weighted_made"), t.last("weighted_made"))

            def combine(h):
                dve.wait_ge(S("den_abs"), t.next("den_abs"))
                dve.wait_ge(S("floor_spread"), t.next("floor_spread"))
                d = TMP[:, 0, :]
                nc.vector.tensor_tensor(d, d, PS[:, M_FLOOR, :], ALU.max).then_inc(S("dve_step"), t.made("dve_step"))
                dve.wait_ge(S("dve_step"), t.last("dve_step"))
                nc.vector.scalar_tensor_tensor(d, d, EPS, d, ALU.mult, ALU.mult).then_inc(S("dve_step"), t.made("dve_step"))
                dve.wait_ge(S("dve_step"), t.last("dve_step"))
                dve.wait_ge(S("num_squared"), t.next("num_squared"))
                nc.vector.tensor_tensor(SQ[:, h % 2, :], SQ[:, h % 2, :], d, ALU.add).then_inc(S("h_sq_made"), t.made("h_sq_made"))

            def h_finish(h):
                dve.wait_ge(S("h_rstd_made"), t.next("h_rstd_made"))
                nc.vector.scalar_tensor_tensor(HT[:, h, :], PS[:, M_NUM[h % 2], :], col("g_mh", h), SQ[:, h % 2, :],
                                               ALU.mult, ALU.mult).then_inc(S("h_made"), t.made("h_made"))
                dve.wait_ge(S("h_made"), t.last("h_made"))
                if h == 0:
                    dve.wait_ge(S("gate_made"), t.next("gate_made", 4))
                nc.vector.tensor_tensor(ytmp(), HT[:, h, :], MO[:, h, :], ALU.mult).then_inc(S("y_made"), t.made("y_made"))
                dve.wait_ge(S("y_made"), t.last("y_made"))

            for k in range(16):
                decay(k)
                if k >= 2:
                    weigh(k - 2)
                if k % 4 == 1 and k > 8:
                    h_finish(k // 4 - 2)
                if k % 4 == 3 and k > 8:
                    y_lo(YL[:, 4 + k // 4 - 2, :], YH[:, 4 + k // 4 - 2, :])
                if k % 4 == 2 and k > 4:
                    combine(k // 4 - 1)
            weigh(14)
            weigh(15)
            h_finish(2)
            combine(3)
            y_lo(YL[:, 6, :], YH[:, 6, :])
            h_finish(3)
            y_lo(YL[:, 7, :], YH[:, 7, :])
            residual(lambda c: ("mixout", 1, c), ("g_ffn", DC))
            feed_forward(1)
            embed(1)

        @block.tensor
        def _(pe):
            t = Tally()
            uses = {}

            def take(b):
                if uses.get(b, 0):
                    pe.wait_ge(acc_free[b], uses[b])
                uses[b] = uses.get(b, 0) + 1

            def idle(b):
                pe.wait_ge(acc_free[b], uses[b])

            PASSES = ((WH, 0), (WL, 0), (WH, 1))

            def products(u, parts, chunks, n, ready, ready_from, beside):
                (blk, _, kc), b = units[u]["blocks"][0], bank(u)
                if 0 in chunks:
                    take(b)
                    pe.wait_ge(S("lo_done"), blk + 1)
                for k in chunks:
                    if beside is not None and k in beside:
                        beside[k]()
                    if ready is not None and k >= ready_from:
                        pe.wait_ge(S(ready), t.next(ready))
                    for p, (w, a) in enumerate(PASSES):
                        ins = nc.tensor.matmul(PS[:, b, 0:n], w[:, blk % HL, 128 * k:128 * k + 128], parts[a][:, k, 0:n],
                                               start=(k == 0 and p == 0), stop=(k == kc - 1 and p == len(PASSES) - 1))
                if kc - 1 in chunks:
                    ins.then_inc(S("block_used"), t.made("block_used"))

            def feature(u, parts, n=T, ready=None, ready_from=0, beside=None):
                products(u, parts, range(units[u]["blocks"][0][2]), n, ready, ready_from, beside)

            def feature_pair(u, v, parts, ready, ready_from=0, late=2):
                early, rest = range(DC - late), range(DC - late, DC)
                products(u, parts, early, T, ready, ready_from, None)
                products(v, parts, early, T, None, 0, None)
                products(u, parts, rest, T, ready, ready_from, None)
                products(v, parts, rest, T, None, 0, None)

            def token(u, parts, order, between=None):
                d = units[u]
                kc = sum(n for _, _, n in d["blocks"])
                for blk, k0, n in d["blocks"]:
                    if k0 and between is not None:
                        between()
                    pe.wait_ge(S("lo_done"), blk + 1)
                    for i in range(d["tiles"]):
                        if k0 == 0:
                            take(bank(u, i))
                        for k in range(k0, k0 + n):
                            for p, (w, a) in enumerate(PASSES):
                                ins = nc.tensor.matmul(PS[:, bank(u, i), 0:256], order(parts[a][:, k, :], i),
                                                       w[:, blk % HL, 256 * (k - k0):256 * (k - k0) + 256],
                                                       start=(k == 0 and p == 0), stop=(k == kc - 1 and p == len(PASSES) - 1))
                        if k0 + n == kc and i < d["tiles"] - 1:
                            ins.then_inc(S("tile_done"), t.made("tile_done"))
                    ins.then_inc(S("block_used"), t.made("block_used"))

            def norm_sum(n=T, chunks=DC, squares=SSQ):
                pe.wait_ge(S("sq_taken"), t.next("sq_taken", chunks))
                nc.tensor.matmul(PS[:, 4, 0:n], const("ones"), squares[:, 0:n], start=True, stop=True).then_inc(S("ssum_done"), t.made("ssum_done"))

            feature(("km", 0), (MH, ML), NMEM, "xg_lo_made")
            feature(("km", 1), (MH, ML), NMEM)
            pe.wait_ge(S("const_in"), 16)
            norm_sum(NMEM, squares=TMP[:, 0, :])
            token(("vm", 0), (MH, ML), lambda ap, i: ap[:, 128 * i:128 * i + 128])
            pe.wait_ge(S("rstd_made"), t.next("rstd_made"))
            for i in range(2):
                ins = nc.tensor.matmul(PS[:, 7, 12 + i:13 + i], RBM[:, 128 * i:128 * i + 128], const("ident", n=1), start=True, stop=True)
            ins.then_inc(S("cols_summed"), t.made("cols_summed"))
            feature(("q", 0), (XH, XL), ready="xg_lo_made")
            norm_sum()
            for c in range(1, 6):
                feature(("q", c), (XH, XL))
            for c in range(2):
                feature(("qm", c), (XH, XL))
            pe.wait_ge(S("rstd_made"), t.next("rstd_made"))
            pe.wait_ge(S("cols_made"), t.next("cols_made"))
            for g in range(3):
                for i in range(QT):
                    ins = nc.tensor.matmul(PS[:, 7, 4 * g + i:4 * g + i + 1], tile_tokens(RB[:, :], g, i), const("ident", n=1),
                                           start=True, stop=True)
            ins.then_inc(S("cols_summed"), t.made("cols_summed"))
            for c in range(6):
                feature(("k", c), (XH, XL))
            for g in range(2):
                token(("v", g), (XH, XL), lambda ap, i, g=g: tile_tokens(ap, g, i))

            def score(n):
                g, i = TILES[n]
                w, k0 = keys(g, i)
                if n == 0:
                    pe.wait_ge(S("qk_ready"), t.next("qk_ready", 2))
                elif n == 1:
                    idle(0)
                    idle(1)
                else:
                    pe.wait_ge(S("scores_ready"), t.next("scores_ready"))
                for par in range(2):
                    for hh in range(2):
                        r = slice(64 * par, 64 * par + 64)
                        if g == 3:
                            q, k = QM[r, hh, 128 * i:128 * i + 128], KM[r, hh, :]
                        else:
                            q, k = Q[r, 2 * g + hh, 128 * i:128 * i + 128], K[r, 2 * g + hh, k0:k0 + w]
                        ins = nc.tensor.matmul(PS[:, SPAIR[n % 2] + par, w * hh:w * hh + w], q, k, start=True, stop=True)
                ins.then_inc(S("scored"), t.made("scored"))

            def turn(n):
                g, i = TILES[n]
                w, _ = keys(g, i)
                nb = w // 128
                if g == 3:
                    pe.wait_ge(S("probs_normal"), t.next("probs_normal"))
                pe.wait_ge(S("probs_made"), t.next("probs_made"))
                turns = [(j, kb) for j in range(4) for kb in range(nb)]
                for half in range(nb):
                    k = t.n.get("turned", 0)
                    if k >= 2:
                        pe.wait_ge(S("turned_kept"), k - 1)
                    for q in range(4):
                        j, kb = turns[4 * half + q]
                        ins = nc.tensor.transpose(PS[:, 6 + k % 2, 128 * q:128 * q + 128],
                                                  sbuf(n)[:, j, 128 * kb:128 * kb + 128], const("ident"))
                    ins.then_inc(S("turned"), t.made("turned"))

            def values(n):
                g, i = TILES[n]
                nb = keys(g, i)[0] // 128
                pe.wait_ge(S("turned_kept"), TURNED[n])
                if n < 2:
                    idle(2 + n)
                else:
                    pe.wait_ge(S("mix_kept"), t.next("mix_kept"))
                for j in range(4):
                    par, hh = j // 2, j % 2
                    h = 2 * hh + par
                    for kb in range(nb):
                        if g == 3:
                            v = VM[:, kb, 64 * h:64 * h + 64]
                        elif g == 0 and i:
                            v = V[:, 0, i - 1 + kb, 64 * h:64 * h + 64]
                        else:
                            v = V[:, g, i, 64 * h:64 * h + 64]
                        ins = nc.tensor.matmul(PS[64 * par:64 * par + 64, 2 + n % 2, 128 * hh:128 * hh + 128], v, PT[:, n % 2, nb * j + kb, :],
                                               start=(kb == 0), stop=(kb == nb - 1))
                ins.then_inc(S("mixed"), t.made("mixed"))

            pe.wait_ge(S("const_rest_in"), 16)
            score(0)
            token(("v", 2), (XH, XL), lambda ap, i: tile_tokens(ap, 2, i))
            score(1)
            for n in range(len(TILES)):
                if n + 2 < len(TILES):
                    score(n + 2)
                turn(n)
                if n:
                    values(n - 1)
            values(len(TILES) - 1)
            def turn_stats(n):
                kind, g = n // 3, n % 3
                if n >= 2:
                    pe.wait_ge(S("stat_kept"), t.next("stat_kept"))
                for i in range(QT):
                    ins = nc.tensor.transpose(PS[0:4, 4 + n % 2, 128 * i:128 * i + 128], STAT[:, g, i, :, kind], const("ident"))
                ins.then_inc(S("stat_turned"), t.made("stat_turned"))

            def spread(c):
                if c == 0:
                    pe.wait_ge(S("row_weight"), t.next("row_weight", 3))
                if c >= 2:
                    pe.wait_ge(S("weight_used"), t.next("weight_used"))
                nc.tensor.matmul(PS[:, 4 + c % 2, :], const("pair", rows=4, at=128 * (c % 2)), ROWS[:, c // 2, :],
                                 start=True, stop=True).then_inc(S("weight_spread"), t.made("weight_spread"))

            pe.wait_ge(S("scores_ready"), t.next("scores_ready", 2))
            first_bank = bank(("gate", 0))
            if first_bank >= 2:
                pe.wait_ge(S("mix_kept"), t.next("mix_kept", 2))
            feature(("gate", 0), (XH, XL), beside={4 + n: lambda n=n: turn_stats(n) for n in range(4)})
            if first_bank < 2:
                pe.wait_ge(S("mix_kept"), t.next("mix_kept", 2))
            feature(("gate", 1), (XH, XL), beside={1: lambda: turn_stats(4), 3: lambda: turn_stats(5)})
            for c in range(2, DC):
                feature(("gate", c), (XH, XL))
                if c == 3:
                    spread(0)
                if c >= 3:
                    spread(c - 2)
            feature_pair(("out", 0), ("out", 1), (YH, YL), "y_lo_made")
            for c in range(2, DC):
                feature(("out", c), (YH, YL))
            xg = (XH, XL)
            feature(("cc", 0), xg, ready="xg_lo_made")
            pe.wait_ge(S("sq_taken"), t.next("sq_taken", 2 * DC))
            nc.tensor.matmul(PS[:, 5, :], const("ones"), TMP[:, 0, :], start=True, stop=True)
            nc.tensor.matmul(PS[:, 4, :], const("ones"), SSQ[:, :], start=True, stop=True).then_inc(S("ssum_done"), t.made("ssum_done"))
            for c in range(4):
                for k in ("cc", "cx", "cb"):
                    if (k, c) != ("cc", 0):
                        feature((k, c), xg)
                if c == 0:
                    pe.wait_ge(S("late_made"), t.next("late_made"))
                    for i in range(QT):
                        ins = nc.tensor.matmul(PS[:, 7, i:i + 1], RB[:, 128 * i:128 * i + 128], const("ident", n=1),
                                               start=True, stop=True)
                    ins.then_inc(S("cols_summed"), t.made("cols_summed"))
            for g in range(2):
                token(("gv", g), xg, lambda ap, i: ap[:, 128 * i:128 * i + 128])
            feature(("gu", 0), xg)
            feature(("gu", 1), xg)
            pe.wait_ge(S("ws_masked"), t.next("ws_masked"))
            pe.wait_ge(S("gv_normed"), t.next("gv_normed", QT))
            for c in range(4):
                for par in range(2):
                    h = 2 * c + par
                    for i in range(QT):
                        ins = nc.tensor.matmul(PS[64 * par:64 * par + 64, 4 + c, 128 * i:128 * i + 128],
                                               GV[:, i, 64 * h:64 * h + 64], WS[:, h, :], start=True, stop=True)
                ins.then_inc(S("spatial_done"), t.made("spatial_done"))

            feature(("gu", 2), xg)
            feature(("gu", 3), xg)
            feature_pair(("mixout", 0, 0), ("mixout", 0, 1), (YH, YL), "y_lo_made")
            for c in range(2, DC):
                feature(("mixout", 0, c), (YH, YL))

            def feed_forward(layer):
                for n, (f0, fn) in enumerate(PASS):
                    for f in range(f0, f0 + fn):
                        feature(("fg", layer, f), xg, ready="xg_lo_made" if f == 0 else None)
                        if f == 0:
                            norm_sum()
                        feature(("fu", layer, f), xg)
                    for c in range(DC):
                        feature(("fd", layer, n, c), (YH, YL), ready="y_lo_made" if c == 0 else None)

            def embed(layer):
                feature(("pg", layer, 0), xg, ready="xg_lo_made")
                norm_sum()
                pe.wait_ge(S("ple_lo_made"), t.next("ple_lo_made", 2))
                feature(("pp", layer, 0), (PH, PL))
                for c in range(1, DC):
                    feature(("pg", layer, c), xg)
                    feature(("pp", layer, c), (PH, PL))

            feed_forward(0)
            embed(0)
            xg = (YH, YL)
            def head_sum(m):
                u, c, rows, _ = HEADS[m]
                r = 32 if m == 0 else 128
                pe.wait_ge(S("head_sq_made"), t.next("head_sq_made"))
                nc.tensor.matmul(PS[0:r, 5 + m % 2, :], const("blk64" if rows == 64 else "blk32", rows=r, n=r),
                                 SQ[0:r, m % 2, :], start=True, stop=True).then_inc(S("head_summed"), t.made("head_summed"))

            def turn_pairs(m):
                r = 32 if m == 0 else 128
                pe.wait_ge(S("rope_in"), t.next("rope_in"))
                nc.tensor.matmul(PS[0:r, 7, :], const("rot", rows=r, n=r), TMP[0:r, 2, :], start=True, stop=True).then_inc(S("rot_done"), t.made("rot_done"))

            feature(("ql", 0), xg, ready="xg_lo_made")
            norm_sum()
            for c in (1, 2):
                feature(("ql", c), xg)
            for c in range(2):
                feature(("kvl", c), xg)
            norm_sum(chunks=3)
            feature(("small", 0), xg)
            feature(("mq", 0), xg)
            norm_sum(chunks=2)
            head_sum(0)
            feature(("mq", 1), xg)
            pe.wait_ge(S("rstd_made"), t.next("rstd_made", 3))
            for i in range(QT):
                ins = nc.tensor.matmul(PS[:, 7, i:i + 1], RB[:, 128 * i:128 * i + 128], const("ident", n=1),
                                       start=True, stop=True)
            ins.then_inc(S("cols_summed"), t.made("cols_summed"))
            pe.wait_ge(S("cols_made"), t.next("cols_made", 3))
            turn_pairs(0)

            def turn_log_f():
                pe.wait_ge(S("lf_made"), t.next("lf_made"))
                for b in range(QT):
                    ins = nc.tensor.transpose(PS[:, 4, 4 * b:4 * b + 4], F_ROW[:, 128 * b:128 * b + 128], const("ident", rows=4, n=4))
                ins.then_inc(S("lf_turned"), t.made("lf_turned"))

            natural = lambda ap, i: ap[:, 128 * i:128 * i + 128]
            token(("mv", 0), xg, natural, turn_log_f)
            pe.wait_ge(S("lf_cols"), t.next("lf_cols"))
            for b in range(QT):
                ins = nc.tensor.matmul(PS[0:4, 5, :], LFC[:, 0, b, :], const("upto", at=384 - 128 * b, n=512),
                                       start=(b == 0), stop=(b == QT - 1))
            ins.then_inc(S("a_summed"), t.made("a_summed"))
            token(("mv", 1), xg, natural)
            pe.wait_ge(S("b_made"), t.next("b_made"))
            for b in range(QT):
                ins = nc.tensor.transpose(PS[:, 6, 4 * b:4 * b + 4], I_ROW[:, 128 * b:128 * b + 128], const("ident", rows=4, n=4))
            ins.then_inc(S("b_turned"), t.made("b_turned"))

            lat_q, lat_kv = (LH[:, 0:3, :], LL[:, 0:3, :]), (LH[:, 3:5, :], LL[:, 3:5, :])
            for m in range(1, len(HEADS) + 1):
                if m < len(HEADS):
                    u, c, _, _ = HEADS[m]
                    if m == 1:
                        pe.wait_ge(S("lat_lo_made"), t.next("lat_lo_made", 5))
                    feature((u, c), lat_kv if u == "kn" else lat_q)
                if 3 <= m and HEADS[m - 2][2] == 32:
                    turn_pairs(m - 2)
                if m in BESIDE:
                    feature(BESIDE[m], xg)
                if m == 2:
                    pe.wait_ge(S("b_cols"), t.next("b_cols"))
                if m == len(HEADS):
                    feature(("mo", 3), xg)
                if m >= 2:
                    head_sum(m - 1)
            for g in range(2):
                token(("va", g), lat_kv, natural)

            def d_score(n):
                h, i = DTILES[n]
                w = 128 * (i + 1)
                if n == 0:
                    pe.wait_ge(S("head_taken"), t.next("head_taken", len(HEADS)))
                    pe.wait_ge(S("kr_kept"), t.next("kr_kept"))
                if n in (2, 3):
                    idle(SBANK[n])
                if n >= 4:
                    pe.wait_ge(S("d_exp_made"), t.next("d_exp_made"))
                nc.tensor.matmul(PS[:, SBANK[n % 4], 0:w], QF[:, h, 128 * i:128 * i + 128], KF[:, h, 0:w],
                                 start=True, stop=False)
                nc.tensor.matmul(PS[:, SBANK[n % 4], w - 128:w], const("ident"), const("causal"),
                                 start=False, stop=True).then_inc(S("d_scored"), t.made("d_scored"))

            def d_turn(n):
                h, i = DTILES[n]
                pe.wait_ge(S("d_probs_made"), t.next("d_probs_made"))
                if n >= 2:
                    pe.wait_ge(S("d_turn_kept"), n - 1)
                for kb in range(i + 1):
                    ins = nc.tensor.transpose(PS[:, 6 + n % 2, 128 * kb:128 * kb + 128], PD[:, n % 4, 128 * kb:128 * kb + 128],
                                              const("ident"))
                ins.then_inc(S("d_turned"), t.made("d_turned"))

            def d_values(n):
                h, i = DTILES[n]
                c, par = h // 2, h % 2
                pe.wait_ge(S("d_turn_kept"), n + 1)
                if n == 0:
                    for b in range(QT):
                        pe.wait_ge(acc_free[bank(("va", 1), b)], freed(("va", 1), b))
                if n % 8 == 0:
                    if c < 2:
                        idle(2 + c)
                    else:
                        pe.wait_ge(S("y_lo_made"), t.next("y_lo_made"))
                for kb in range(i + 1):
                    ins = nc.tensor.matmul(PS[64 * par:64 * par + 64, 2 + c % 2, 128 * i:128 * i + 128],
                                           VA[:, kb, 64 * h:64 * h + 64], PTD[:, n % 2, 128 * kb:128 * kb + 128],
                                           start=(kb == 0), stop=(kb == i))
                if n % 8 == 7:
                    ins.then_inc(S("d_mixed"), t.made("d_mixed"))

            for n in range(3):
                d_score(n)
            for n in range(len(DTILES)):
                if n + 3 < len(DTILES):
                    d_score(n + 3)
                d_turn(n)
                if n:
                    d_values(n - 1)
            d_values(len(DTILES) - 1)
            pe.wait_ge(S("y_lo_made"), t.next("y_lo_made", 2))
            pe.wait_ge(S("d_exp_made"), t.next("d_exp_made", 4))

            pe.wait_ge(S("floor_made"), t.next("floor_made"))

            def m_spread(h):
                if h:
                    pe.wait_ge(S("decay_pre"), t.next("decay_pre", 4))
                nc.tensor.matmul(PS[:, M_G, :], const("head", rows=4, at=128 * h), G_ROW, start=True, stop=True).then_inc(S("g_spread"), t.made("g_spread"))

            def m_score(k):
                h, b = k // 4, k % 4
                c, r = h // 2, slice(64 * (h % 2), 64 * (h % 2) + 64)
                if k >= 3:
                    pe.wait_ge(S("weighted_made"), k - 2)
                nc.tensor.matmul(PS[:, M_S[k % 3], 0:T - 128 * b], MK[r, c, 128 * b:128 * b + 128],
                                 MQ[r, c, 128 * b:T], start=True, stop=True).then_inc(S("m_scored"), t.made("m_scored"))

            def m_add(k):
                h, b = k // 4, k % 4
                w = T - 128 * b
                pe.wait_ge(S("weighted_made"), k + 1)
                if b == 0 and h >= 2:
                    pe.wait_ge(S("h_made"), t.next("h_made"))
                nc.tensor.matmul(PS[:, M_NUM[h % 2], 128 * b:T], MV[:, b, 128 * h:128 * h + 128], SW[:, k % 4, 0:w],
                                 start=(b == 0), stop=(b == 3))
                if b == 0 and h:
                    pe.wait_ge(S("den_abs"), t.next("den_abs"))
                nc.tensor.matmul(PS[:, M_DEN, 128 * b:T], const("ones"), SW[:, k % 4, 0:w],
                                 start=(b == 0), stop=(b == 3)).then_inc(S("m_added"), t.made("m_added"))

            def m_floor(h):
                if h:
                    pe.wait_ge(S("h_rstd_made"), t.next("h_rstd_made"))
                nc.tensor.matmul(PS[:, M_FLOOR, :], const("head", rows=4, at=128 * h), F_ROW,
                                 start=True, stop=True).then_inc(S("floor_spread"), t.made("floor_spread"))

            def h_sum(h):
                pe.wait_ge(S("h_sq_made"), t.next("h_sq_made"))
                nc.tensor.matmul(PS[:, M_FLOOR, :], const("ones"), SQ[:, h % 2, :], start=True, stop=True).then_inc(S("h_sq_summed"), t.made("h_sq_summed"))

            m_spread(0)
            m_score(0)
            m_score(1)
            for k in range(16):
                if k + 2 < 16:
                    m_score(k + 2)
                if k % 4 == 1 and k < 12:
                    m_spread(k // 4 + 1)
                m_add(k)
                if k % 4 == 1 and k > 4:
                    h_sum(k // 4 - 1)
                if k % 4 == 3:
                    m_floor(k // 4)
            h_sum(3)
            pe.wait_ge(S("h_made"), t.next("h_made"))
            pe.wait_ge(S("den_abs"), t.next("den_abs"))
            feature_pair(("mixout", 1, 0), ("mixout", 1, 1), (YH, YL), "y_lo_made", ready_from=DC // 2)
            for c in range(2, DC):
                feature(("mixout", 1, c), (YH, YL))
            xg = (XH, XL)
            feed_forward(1)
            embed(1)


def chunked(a):
    return np.ascontiguousarray(a.reshape(-1, 128, a.shape[-1]).transpose(1, 0, 2))


def lay_out(i):
    vec = np.zeros((128, NVEC), np.float32)

    def put(name, a):
        a = a.reshape(-1, a.shape[-1]) if a.ndim > 1 else a[None]
        a = a.reshape(a.shape[0], -1, 128).transpose(2, 0, 1).reshape(128, -1)
        vec[:, VEC[name]:VEC[name] + a.shape[1]] = a

    put("norm_g", i["norm_g"])
    put("mem_norm_g", i["mem_norm_g"])
    put("final_g", i["final_norm_g"])
    put("g_mix", i["g_mix_2"])
    put("g_ffn", i["g_ffn_2"])
    put("g_ple", i["g_ple_2"])
    put("conv", i["ev_w_conv_2"][0])
    put("g_qa", i["od_g_qa_2"])
    put("g_kva", i["od_g_kva_2"])
    gq, gk = i["od_g_q_2"][0], i["od_g_k_2"][0]
    vec[:, VEC["g_qn"]] = np.tile(gq[:64], 2)
    vec[:, VEC["g_qr"]] = np.tile(gq[64:], 4)
    vec[:, VEC["g_kn"]] = np.tile(gk[:64], 2)
    vec[:, VEC["g_kr"]] = np.tile(gk[64:], 4)
    put("g_mh", i["od_g_mh_2"])
    vec[32:36, VEC["b_i"]] = i["od_b_gate_2"][0, :4]
    vec[64:68, VEC["b_f"]] = i["od_b_gate_2"][0, 4:]
    vec[:, VEC["b_s"]:VEC["b_s"] + 8] = i["ev_b_s_2"][0].T
    vec[:, VEC["eps"]] = EPS
    vec[:, VEC["halfpi"]] = np.float32(np.pi / 2)
    vec[:, VEC["inv_freq"]] = (10000.0 ** (-np.arange(0, 32, 2) / 32.0)).astype(np.float32)[np.arange(128) % 16]
    weights = {"mem_kv": i["w_mem_kv"][0], "in": i["w_in"][0], "out": i["w_out"][0],
               "ev_in": i["ev_w_in_2"][0], "ev_out": i["ev_w_out_2"][0], "od_in": i["od_w_in_2"][0],
               "od_out": i["od_w_out_2"][0], "q_up": i["od_w_q_up_2"][0], "kv_up": i["od_w_kv_up_2"][0]}
    for n in range(2):
        weights |= {f"gate{n}": i["w_gate_2"][n], f"up{n}": i["w_up_2"][n], f"down{n}": i["w_down_2"][n],
                    f"ple_gate{n}": i["w_ple_gate_2"][n], f"ple_proj{n}": i["w_ple_proj_2"][n]}
    blocks = layout().blocks
    wall = np.zeros((len(blocks), 128, BLK), np.float32)
    for j, (name, parts, width) in enumerate(blocks):
        for n, (k, spec) in enumerate(parts):
            wall[j, :, n * width:(n + 1) * width] = block_columns(weights[name], k, spec, width)
    table, bias = constants()
    ws = np.ascontiguousarray(i["ev_w_s_2"][0].transpose(2, 0, 1)).reshape(128, 1024)
    bs = i["ev_b_s_2"][0].reshape(4, 2, 1, 128)
    bs = np.broadcast_to(bs, (4, 2, 64, 128)).transpose(1, 2, 0, 3).reshape(128, 512)
    return {
        "x": chunked(np.ascontiguousarray(i["x"][0].T)),
        "mem": chunked(np.ascontiguousarray(i["mem"][0].T)),
        "wall": wall,
        "ple": np.stack([chunked(np.ascontiguousarray(i["p_2"][n, 0].T)) for n in range(2)]),
        "vec": vec,
        "table": table,
        "bias": bias,
        "ws": ws,
        "bs": np.ascontiguousarray(bs),
        "gv": np.ascontiguousarray(np.broadcast_to(i["ev_g_v_2"][0].reshape(1, 512), (128, 512))),
        "pos": np.ascontiguousarray(np.broadcast_to(i["positions_2"].reshape(1, T), (128, T))),
    }


def kernel(**inputs):
    import concourse.bacc as _bacc
    from concourse.bass_utils import run_bass_kernel_spmd as _run

    nc = _bacc.Bacc("TRN2", target_bir_lowering=False, num_devices=1, dynamic_dma_scratch_size=1024)
    arrays = lay_out({k: np.asarray(v) for k, v in inputs.items()})
    args = {}
    for name, a in arrays.items():
        args[name] = nc.dram_tensor(f"in_{name}", a.shape, mybir.dt.from_np(a.dtype), kind="ExternalInput").ap()
    args["y"] = nc.dram_tensor("out_y", (128, DC, T), F32, kind="ExternalOutput").ap()
    build(nc, **args)
    r = _run(nc, [{f"in_{k}": v for k, v in arrays.items()}], core_ids=[0])
    y = r.results[0]["out_y"]
    return np.ascontiguousarray(y.transpose(1, 0, 2).reshape(D, T).T).reshape(1, T, D)
```
